# Optimizing a Trainium2 kernel written in Bass

```python
import math
import jax, jax.numpy as jnp
from jax import lax
import numpy as np

D_MODEL = 1024
BATCH = 1
SEQ = 512
DEPTH = 2

MIX_WIDTH = D_MODEL
HEAD_DIM = 64
N_HEADS_DIFF = MIX_WIDTH // (4 * HEAD_DIM)
N_HEADS_FOX = MIX_WIDTH // (2 * HEAD_DIM)
DIFF_WIDTH = N_HEADS_DIFF * 2 * HEAD_DIM
FOX_WIDTH = N_HEADS_FOX * HEAD_DIM
IN_WIDTH = 3 * DIFF_WIDTH + 3 * FOX_WIDTH + N_HEADS_FOX
ROT_DIM = HEAD_DIM // 4
ROPE_THETA = 500000.0
Q_BLOCK = 128
D_FF = ((8 * D_MODEL // 3 + 255) // 256) * 256
EPS = 1e-6
NEG_INF = -1e30


def rms_norm(x, g):
    xf = x.astype(jnp.float32)
    y = xf * lax.rsqrt(jnp.mean(xf * xf, axis=-1, keepdims=True) + EPS)
    return (y * g.astype(jnp.float32)).astype(x.dtype)

def rotary_tables(positions, dtype):
    inv_freq = 1.0 / (ROPE_THETA ** (jnp.arange(0, ROT_DIM, 2, dtype=jnp.float32) / ROT_DIM))
    ang = positions.astype(jnp.float32)[..., None] * inv_freq
    cos = jnp.cos(ang)[:, :, None, :].astype(dtype)
    sin = jnp.sin(ang)[:, :, None, :].astype(dtype)
    return cos, sin

def partial_rotary(t, cos, sin):
    half = ROT_DIM // 2
    t1, t2, rest = t[..., :half], t[..., half:ROT_DIM], t[..., ROT_DIM:]
    return jnp.concatenate([t1 * cos - t2 * sin, t2 * cos + t1 * sin, rest], axis=-1)

def diff_attention(q, k, v, lam):
    b, s = q.shape[0], q.shape[1]
    nb = s // Q_BLOCK
    scale = HEAD_DIM ** -0.5
    q_blocks = q.reshape(b, nb, Q_BLOCK, N_HEADS_DIFF, 2, HEAD_DIM).swapaxes(0, 1)
    k_pos = jnp.arange(s)

    def block(args):
        i, qi = args
        q_pos = i * Q_BLOCK + jnp.arange(Q_BLOCK)
        causal = q_pos[:, None] >= k_pos[None, :]
        logits = jnp.einsum('bqhmd,bkhmd->bhmqk', qi, k).astype(jnp.float32) * scale
        logits = jnp.where(causal, logits, NEG_INF)
        p = jax.nn.softmax(logits, axis=-1)
        p = p[:, :, 0] - lam * p[:, :, 1]
        return jnp.einsum('bhqk,bkhe->bqhe', p.astype(v.dtype), v)

    o = lax.map(block, (jnp.arange(nb), q_blocks))
    return o.swapaxes(0, 1).reshape(b, s, N_HEADS_DIFF, 2 * HEAD_DIM)

def forgetting_attention(q, k, v, log_f):
    b, s = q.shape[0], q.shape[1]
    nb = s // Q_BLOCK
    scale = HEAD_DIM ** -0.5
    c = jnp.cumsum(log_f, axis=1)
    c_k = c.transpose(0, 2, 1)[:, :, None, :]
    q_blocks = q.reshape(b, nb, Q_BLOCK, N_HEADS_FOX, HEAD_DIM).swapaxes(0, 1)
    c_blocks = c.reshape(b, nb, Q_BLOCK, N_HEADS_FOX).swapaxes(0, 1)
    k_pos = jnp.arange(s)

    def block(args):
        i, qi, ci = args
        q_pos = i * Q_BLOCK + jnp.arange(Q_BLOCK)
        causal = q_pos[:, None] >= k_pos[None, :]
        decay = ci.transpose(0, 2, 1)[..., None] - c_k
        logits = jnp.einsum('bqhd,bkhd->bhqk', qi, k).astype(jnp.float32) * scale + decay
        logits = jnp.where(causal, logits, NEG_INF)
        p = jax.nn.softmax(logits, axis=-1)
        return jnp.einsum('bhqk,bkhd->bqhd', p.astype(v.dtype), v)

    o = lax.map(block, (jnp.arange(nb), q_blocks, c_blocks))
    return o.swapaxes(0, 1).reshape(b, s, N_HEADS_FOX, HEAD_DIM)

def first_inputs(seed: int = 0) -> dict:
    key = jax.random.key(seed)
    ks = jax.random.split(key, 16)
    f32 = jnp.float32

    def nrm(k, shape, scale):
        return jax.random.normal(k, shape, f32) * scale

    def gain(k, n):
        return 1.0 + 0.05 * jax.random.normal(k, (DEPTH, n), f32)

    return {
        "x": nrm(ks[0], (BATCH, SEQ, D_MODEL), 1.0),
        "positions": jnp.broadcast_to(jnp.arange(SEQ, dtype=jnp.int32), (BATCH, SEQ)),
        "attn_pre_g": gain(ks[1], D_MODEL),
        "w_in": nrm(ks[2], (DEPTH, D_MODEL, IN_WIDTH), D_MODEL ** -0.5),
        "forget_bias": jax.random.uniform(ks[3], (DEPTH, N_HEADS_FOX), f32, 1.0, 6.0),
        "lam_q1": nrm(ks[4], (DEPTH, HEAD_DIM), 0.1),
        "lam_k1": nrm(ks[5], (DEPTH, HEAD_DIM), 0.1),
        "lam_q2": nrm(ks[6], (DEPTH, HEAD_DIM), 0.1),
        "lam_k2": nrm(ks[7], (DEPTH, HEAD_DIM), 0.1),
        "diff_sub_g": gain(ks[8], 2 * HEAD_DIM),
        "w_out": nrm(ks[9], (DEPTH, MIX_WIDTH, D_MODEL), MIX_WIDTH ** -0.5),
        "attn_post_g": gain(ks[10], D_MODEL),
        "ffn_pre_g": gain(ks[11], D_MODEL),
        "w_gate": nrm(ks[12], (DEPTH, D_MODEL, D_FF), D_MODEL ** -0.5),
        "w_up": nrm(ks[13], (DEPTH, D_MODEL, D_FF), D_MODEL ** -0.5),
        "w_down": nrm(ks[14], (DEPTH, D_FF, D_MODEL), D_FF ** -0.5),
        "ffn_post_g": gain(ks[15], D_MODEL),
    }

def first_block(x, positions, attn_pre_g, w_in, forget_bias, lam_q1, lam_k1, lam_q2, lam_k2,
              diff_sub_g, w_out, attn_post_g, ffn_pre_g, w_gate, w_up, w_down, ffn_post_g):
    b, s, _ = x.shape
    f32 = jnp.float32
    cos, sin = rotary_tables(positions, x.dtype)
    split_at = [DIFF_WIDTH, 2 * DIFF_WIDTH, 3 * DIFF_WIDTH,
                3 * DIFF_WIDTH + FOX_WIDTH, 3 * DIFF_WIDTH + 2 * FOX_WIDTH,
                3 * DIFF_WIDTH + 3 * FOX_WIDTH]
    for l in range(DEPTH):
        h = rms_norm(x, attn_pre_g[l])
        proj = h @ w_in[l]
        qa, ka, va, qb, kb, vb, f_logit = jnp.split(proj, split_at, axis=-1)

        qa = partial_rotary(qa.reshape(b, s, 2 * N_HEADS_DIFF, HEAD_DIM), cos, sin)
        ka = partial_rotary(ka.reshape(b, s, 2 * N_HEADS_DIFF, HEAD_DIM), cos, sin)
        qa = qa.reshape(b, s, N_HEADS_DIFF, 2, HEAD_DIM)
        ka = ka.reshape(b, s, N_HEADS_DIFF, 2, HEAD_DIM)
        va = va.reshape(b, s, N_HEADS_DIFF, 2 * HEAD_DIM)
        lam_init = 0.8 - 0.6 * math.exp(-0.3 * l)
        lam = (jnp.exp(jnp.sum(lam_q1[l].astype(f32) * lam_k1[l].astype(f32)))
               - jnp.exp(jnp.sum(lam_q2[l].astype(f32) * lam_k2[l].astype(f32)))
               + lam_init)
        oa = diff_attention(qa, ka, va, lam)
        oa = rms_norm(oa, diff_sub_g[l]) * (1.0 - lam_init)

        log_f = jax.nn.log_sigmoid(f_logit.astype(f32) + forget_bias[l].astype(f32))
        ob = forgetting_attention(qb.reshape(b, s, N_HEADS_FOX, HEAD_DIM),
                                  kb.reshape(b, s, N_HEADS_FOX, HEAD_DIM),
                                  vb.reshape(b, s, N_HEADS_FOX, HEAD_DIM), log_f)

        mixed = jnp.concatenate([oa.reshape(b, s, DIFF_WIDTH), ob.reshape(b, s, FOX_WIDTH)], axis=-1)
        x = x + rms_norm(mixed @ w_out[l], attn_post_g[l])

        h = rms_norm(x, ffn_pre_g[l])
        y = (jax.nn.silu(h @ w_gate[l]) * (h @ w_up[l])) @ w_down[l]
        x = x + rms_norm(y, ffn_post_g[l])
    return x


DEPTH_2 = 1

M_HEADS = 4
M_HEAD_DIM = 128
M_WIDTH = M_HEADS * M_HEAD_DIM
M_CHUNK = 128
CONV_WIDTH = 4
N_HEADS = 8
N_KV_GROUPS = 2
N_REP = N_HEADS // N_KV_GROUPS
N_HEAD_DIM = 64
N_WIDTH = N_HEADS * N_HEAD_DIM
N_KV_WIDTH = N_KV_GROUPS * N_HEAD_DIM
CMP_BLOCK = 32
CMP_STRIDE = 16
CMP_HIDDEN = 2 * N_HEAD_DIM
SEL_BLOCK = 64
SEL_TOPK = 16
WINDOW = 512
NSA_Q_BLOCK = 64
REL_BUCKETS = 32
REL_MAX_DIST = 1024
N_BRANCH = 2
BRANCH_WIDTH = 512
D_FF_2 = -(-8 * D_MODEL // (3 * 256)) * 256
RMS_EPS = 1e-6
BIG = 1e9

IN_SIZES = (M_WIDTH, M_WIDTH, M_WIDTH, M_WIDTH, M_HEADS, M_HEADS,
            N_WIDTH, 6 * N_KV_WIDTH, 3 * N_HEADS, N_BRANCH * D_MODEL)
D_IN_TOTAL = sum(IN_SIZES)


def rms_norm_2(x, g):
    x32 = x.astype(jnp.float32)
    y = x32 * lax.rsqrt(jnp.mean(x32 * x32, axis=-1, keepdims=True) + RMS_EPS)
    return (y * g.astype(jnp.float32)).astype(x.dtype)

def split_columns(p, sizes):
    out = []
    start = 0
    for s in sizes:
        out.append(p[..., start:start + s])
        start += s
    return out

def causal_depthwise_conv(x, w):
    T = x.shape[1]
    xp = jnp.pad(x, ((0, 0), (CONV_WIDTH - 1, 0), (0, 0)))
    return sum(w[j] * xp[:, j:j + T] for j in range(CONV_WIDTH))

def rel_bucket(dist):
    n = jnp.maximum(dist, 0)
    max_exact = REL_BUCKETS // 2
    nf = jnp.maximum(n, 1).astype(jnp.float32)
    large = max_exact + (jnp.log(nf / max_exact) / math.log(REL_MAX_DIST / max_exact)
                         * (REL_BUCKETS - max_exact)).astype(jnp.int32)
    large = jnp.minimum(large, REL_BUCKETS - 1)
    return jnp.where(n < max_exact, n, large)

def masked_softmax(logits, mask):
    logits = logits.astype(jnp.float32)
    z = jnp.where(mask, logits, -1e30)
    z = z - jnp.max(z, axis=-1, keepdims=True)
    e = jnp.where(mask, jnp.exp(z), 0.0)
    return e / jnp.maximum(jnp.sum(e, axis=-1, keepdims=True), 1e-30)

def mlstm_chunkwise(q, k, v, i_pre, f_pre):
    B, H, T, dk = q.shape
    dv = v.shape[-1]
    L = M_CHUNK
    nc = T // L
    qc = q.reshape(B, H, nc, L, dk)
    kc = k.reshape(B, H, nc, L, dk)
    vc = v.reshape(B, H, nc, L, dv)
    ic = i_pre.reshape(B, H, nc, L)
    bc = jnp.cumsum(jax.nn.log_sigmoid(f_pre).reshape(B, H, nc, L), axis=-1)
    b_last = bc[..., -1]
    a = b_last[..., None] - bc + ic

    def step(carry, inp):
        C, n, m = carry
        k_j, v_j, a_j, bl = inp
        m_new = jnp.maximum(bl + m, jnp.max(a_j, axis=-1))
        decay = jnp.exp(bl + m - m_new)
        w = jnp.exp(a_j - m_new[..., None])
        C_new = decay[..., None, None] * C + jnp.einsum('bhl,bhlk,bhlv->bhkv', w, k_j, v_j)
        n_new = decay[..., None] * n + jnp.einsum('bhl,bhlk->bhk', w, k_j)
        return (C_new, n_new, m_new), (C, n, m)

    init = (jnp.zeros((B, H, dk, dv), jnp.float32), jnp.zeros((B, H, dk), jnp.float32),
            jnp.zeros((B, H), jnp.float32))
    xs = (jnp.moveaxis(kc, 2, 0), jnp.moveaxis(vc, 2, 0), jnp.moveaxis(a, 2, 0), jnp.moveaxis(b_last, 2, 0))
    _, (C_prev, n_prev, m_prev) = lax.scan(step, init, xs)
    C_prev = jnp.moveaxis(C_prev, 0, 2)
    n_prev = jnp.moveaxis(n_prev, 0, 2)
    m_prev = jnp.moveaxis(m_prev, 0, 2)

    causal = jnp.tril(jnp.ones((L, L), dtype=bool))
    log_d = jnp.where(causal, bc[..., :, None] - bc[..., None, :] + ic[..., None, :], -jnp.inf)
    log_inter = bc + m_prev[..., None]
    m_i = jnp.maximum(jnp.max(log_d, axis=-1), log_inter)
    P = jnp.exp(log_d - m_i[..., None]) * jnp.einsum('bhcid,bhcjd->bhcij', qc, kc)
    s_inter = jnp.exp(log_inter - m_i)
    num = (jnp.einsum('bhcij,bhcjv->bhciv', P, vc)
           + s_inter[..., None] * jnp.einsum('bhcid,bhcdv->bhciv', qc, C_prev))
    den = jnp.sum(P, axis=-1) + s_inter * jnp.einsum('bhcid,bhcd->bhci', qc, n_prev)
    h = num / jnp.maximum(jnp.abs(den), jnp.exp(-m_i))[..., None]
    return h.reshape(B, H, T, dv)

def mlstm_mixer(q_pre, k_pre, v, o_pre, i_pre, f_pre, b_fgate, conv_w, g_head):
    B, T, _ = q_pre.shape
    qk = jax.nn.silu(causal_depthwise_conv(jnp.concatenate([q_pre, k_pre], axis=-1), conv_w))
    to_heads = lambda t: t.reshape(B, T, M_HEADS, M_HEAD_DIM).transpose(0, 2, 1, 3).astype(jnp.float32)
    q = to_heads(qk[..., :M_WIDTH])
    k = to_heads(qk[..., M_WIDTH:]) * (M_HEAD_DIM ** -0.5)
    vh = to_heads(v)
    ig = i_pre.astype(jnp.float32).transpose(0, 2, 1)
    fg = (f_pre.astype(jnp.float32) + b_fgate.astype(jnp.float32)).transpose(0, 2, 1)
    hh = mlstm_chunkwise(q, k, vh, ig, fg)
    hh = (hh * lax.rsqrt(jnp.mean(hh * hh, axis=-1, keepdims=True) + RMS_EPS)
          * g_head.astype(jnp.float32).reshape(M_HEADS, 1, M_HEAD_DIM))
    hh = hh.transpose(0, 2, 1, 3).reshape(B, T, M_WIDTH)
    return (jax.nn.sigmoid(o_pre.astype(jnp.float32)) * hh).astype(q_pre.dtype)

def nsa_mixer(q_in, kv_in, gate_in, pe_cmp, w_cmp1, w_cmp2, rel_bias):
    B, T, _ = q_in.shape
    G, R, dh, Q = N_KV_GROUPS, N_REP, N_HEAD_DIM, NSA_Q_BLOCK
    q = q_in.reshape(B, T, G, R, dh).transpose(0, 2, 3, 1, 4) * (dh ** -0.5)
    kv = kv_in.reshape(B, T, 6, G, dh).transpose(2, 0, 3, 1, 4)
    k_c, v_c, k_s, v_s, k_w, v_w = kv[0], kv[1], kv[2], kv[3], kv[4], kv[5]
    gates = jax.nn.sigmoid(gate_in.astype(jnp.float32).reshape(B, T, G, R, 3).transpose(0, 2, 3, 1, 4))

    n_cmp = (T - CMP_BLOCK) // CMP_STRIDE + 1
    cmp_start = jnp.arange(n_cmp) * CMP_STRIDE
    cmp_idx = cmp_start[:, None] + jnp.arange(CMP_BLOCK)[None, :]
    cmp_end = cmp_start + CMP_BLOCK - 1

    def compress(kx, j):
        blk = kx[:, :, cmp_idx] + pe_cmp[j]
        flat = blk.reshape(B, G, n_cmp, CMP_BLOCK * dh)
        return jax.nn.silu(flat @ w_cmp1[j]) @ w_cmp2[j]

    kc_ = compress(k_c, 0)
    vc_ = compress(v_c, 1)

    n_slc = T // SEL_BLOCK
    n_top = min(SEL_TOPK, n_slc)
    k_sb = k_s.reshape(B, G, n_slc, SEL_BLOCK, dh)
    v_sb = v_s.reshape(B, G, n_slc, SEL_BLOCK, dh)
    slc_start = jnp.arange(n_slc) * SEL_BLOCK
    overlap = (jnp.clip(jnp.minimum(cmp_start[:, None] + CMP_BLOCK, slc_start[None, :] + SEL_BLOCK)
                        - jnp.maximum(cmp_start[:, None], slc_start[None, :]), 0)
               / CMP_STRIDE).astype(jnp.float32)

    k_wp = jnp.pad(k_w, ((0, 0), (0, 0), (WINDOW, 0), (0, 0)))
    v_wp = jnp.pad(v_w, ((0, 0), (0, 0), (WINDOW, 0), (0, 0)))

    table = rel_bias.astype(jnp.float32).T.reshape(G, R, REL_BUCKETS)
    g_ix = jnp.arange(G)[None, :, None, None, None]
    r_ix = jnp.arange(R)[None, None, :, None, None]
    gather_blocks = jax.vmap(jax.vmap(lambda blk, ix: blk[ix]))

    def block(i):
        qs = i * Q
        t = qs + jnp.arange(Q)
        qb = lax.dynamic_slice_in_dim(q, qs, Q, axis=3)
        lc = (jnp.einsum('bgrqd,bgcd->bgrqc', qb, kc_).astype(jnp.float32)
              + table[:, :, rel_bucket(t[:, None] - cmp_end[None, :])])
        p_c = masked_softmax(lc, cmp_end[None, :] <= t[:, None])
        o_c = jnp.einsum('bgrqc,bgcd->bgrqd', p_c, vc_.astype(jnp.float32))
        imp = jnp.einsum('bgrqc,cj->bgqj', p_c, overlap)
        cur = t // SEL_BLOCK
        jb = jnp.arange(n_slc)[None, :]
        forced = (jb == 0) | (jb == cur[:, None]) | (jb == cur[:, None] - 1)
        eligible = jb * SEL_BLOCK <= t[:, None]
        score = jnp.where(eligible, jnp.where(forced, BIG, imp), -BIG)
        top_val, top_idx = lax.top_k(score, n_top)
        N = n_top * SEL_BLOCK
        k_g = gather_blocks(k_sb, top_idx).reshape(B, G, Q, N, dh)
        v_g = gather_blocks(v_sb, top_idx).reshape(B, G, Q, N, dh)
        pos_u = top_idx[..., None] * SEL_BLOCK + jnp.arange(SEL_BLOCK)
        mask_u = (top_val > -BIG / 2)[..., None] & (pos_u <= t[:, None, None])
        pos = pos_u.reshape(B, G, Q, N)
        mask_s = mask_u.reshape(B, G, Q, N)
        bias_s = table[g_ix, r_ix, rel_bucket(t[:, None] - pos)[:, :, None]]
        ls = jnp.einsum('bgrqd,bgqnd->bgrqn', qb, k_g).astype(jnp.float32) + bias_s
        p_s = masked_softmax(ls, mask_s[:, :, None])
        o_s = jnp.einsum('bgrqn,bgqnd->bgrqd', p_s, v_g.astype(jnp.float32))
        span = Q + WINDOW
        k_wb = lax.dynamic_slice_in_dim(k_wp, qs, span, axis=2)
        v_wb = lax.dynamic_slice_in_dim(v_wp, qs, span, axis=2)
        pos_w = qs - WINDOW + jnp.arange(span)
        dist = t[:, None] - pos_w[None, :]
        mask_w = (pos_w[None, :] >= 0) & (dist >= 0) & (dist < WINDOW)
        lw = jnp.einsum('bgrqd,bgkd->bgrqk', qb, k_wb).astype(jnp.float32) + table[:, :, rel_bucket(dist)]
        p_w = masked_softmax(lw, mask_w)
        o_w = jnp.einsum('bgrqk,bgkd->bgrqd', p_w, v_wb.astype(jnp.float32))
        gb = lax.dynamic_slice_in_dim(gates, qs, Q, axis=3)
        return gb[..., 0:1] * o_c + gb[..., 1:2] * o_s + gb[..., 2:3] * o_w

    out = lax.map(block, jnp.arange(T // Q))
    out = out.transpose(1, 0, 4, 2, 3, 5).reshape(B, T, N_WIDTH)
    return out.astype(q_in.dtype)

def second_inputs(seed: int = 0) -> dict:
    key = jax.random.key(seed)
    ks = jax.random.split(key, 20)
    nrm = lambda k, shape, scale: jax.random.normal(k, shape, jnp.float32) * scale
    x = nrm(ks[0], (BATCH, SEQ, D_MODEL), 1.0)
    g_norm_mix = 1.0 + nrm(ks[1], (DEPTH_2, D_MODEL), 0.02)
    w_in = nrm(ks[2], (DEPTH_2, D_MODEL, D_IN_TOTAL), D_MODEL ** -0.5)
    b_in = nrm(ks[3], (DEPTH_2, D_IN_TOTAL), 0.02)
    b_fgate = jnp.linspace(3.0, 6.0, M_HEADS, dtype=jnp.float32)[None, :] + nrm(ks[4], (DEPTH_2, M_HEADS), 0.1)
    conv_qk = nrm(ks[5], (DEPTH_2, CONV_WIDTH, 2 * M_WIDTH), CONV_WIDTH ** -0.5)
    g_mlstm_head = 1.0 + nrm(ks[6], (DEPTH_2, M_WIDTH), 0.02)
    pe_cmp = nrm(ks[7], (DEPTH_2, 2, CMP_BLOCK, N_HEAD_DIM), 0.1)
    w_cmp1 = nrm(ks[8], (DEPTH_2, 2, CMP_BLOCK * N_HEAD_DIM, CMP_HIDDEN), (CMP_BLOCK * N_HEAD_DIM) ** -0.5)
    w_cmp2 = nrm(ks[9], (DEPTH_2, 2, CMP_HIDDEN, N_HEAD_DIM), CMP_HIDDEN ** -0.5)
    rel_bias = nrm(ks[10], (REL_BUCKETS, N_HEADS), 0.5)
    w_branch = nrm(ks[11], (DEPTH_2, N_BRANCH, BRANCH_WIDTH, D_MODEL), BRANCH_WIDTH ** -0.5)
    w_out = nrm(ks[12], (DEPTH_2, D_MODEL, D_MODEL), D_MODEL ** -0.5)
    g_norm_ffn = 1.0 + nrm(ks[13], (DEPTH_2, D_MODEL), 0.02)
    w_gate = nrm(ks[14], (DEPTH_2, D_MODEL, D_FF_2), D_MODEL ** -0.5)
    w_up = nrm(ks[15], (DEPTH_2, D_MODEL, D_FF_2), D_MODEL ** -0.5)
    w_down = nrm(ks[16], (DEPTH_2, D_FF_2, D_MODEL), D_FF_2 ** -0.5)
    g_final = 1.0 + nrm(ks[17], (D_MODEL,), 0.02)
    return {'x': x, 'g_norm_mix': g_norm_mix, 'w_in': w_in, 'b_in': b_in, 'b_fgate': b_fgate,
            'conv_qk': conv_qk, 'g_mlstm_head': g_mlstm_head, 'pe_cmp': pe_cmp, 'w_cmp1': w_cmp1,
            'w_cmp2': w_cmp2, 'rel_bias': rel_bias, 'w_branch': w_branch, 'w_out': w_out,
            'g_norm_ffn': g_norm_ffn, 'w_gate': w_gate, 'w_up': w_up, 'w_down': w_down, 'g_final': g_final}

def second_block(x, g_norm_mix, w_in, b_in, b_fgate, conv_qk, g_mlstm_head, pe_cmp, w_cmp1, w_cmp2,
              rel_bias, w_branch, w_out, g_norm_ffn, w_gate, w_up, w_down, g_final):
    B, T, _ = x.shape
    h = x
    for l in range(DEPTH_2):
        u = rms_norm_2(h, g_norm_mix[l])
        proj = jnp.einsum('btd,de->bte', u, w_in[l]) + b_in[l]
        mq, mk, mv, mo, mi, mf, nq, nkv, ngate, merge = split_columns(proj, IN_SIZES)
        y_m = mlstm_mixer(mq, mk, mv, mo, mi, mf, b_fgate[l], conv_qk[l], g_mlstm_head[l])
        y_n = nsa_mixer(nq, nkv, ngate, pe_cmp[l], w_cmp1[l], w_cmp2[l], rel_bias)
        ys = jnp.stack([y_m, y_n], axis=2)
        branch = jnp.einsum('btnw,nwd->btnd', ys, w_branch[l])
        gates = jax.nn.sigmoid(merge.reshape(B, T, N_BRANCH, D_MODEL))
        mixed = jnp.sum(gates * branch, axis=2)
        h = h + mixed @ w_out[l]
        f = rms_norm_2(h, g_norm_ffn[l])
        h = h + (jax.nn.silu(f @ w_gate[l]) * (f @ w_up[l])) @ w_down[l]
    return rms_norm_2(h, g_final)


def setup_inputs(seed=0):
    out = dict(first_inputs(seed))
    for name, value in second_inputs(seed + 1).items():
        if name != "x":
            out[name + "_2"] = value
    return out


def reference(
    x, positions, attn_pre_g, w_in, forget_bias, lam_q1, lam_k1, lam_q2, lam_k2, diff_sub_g,
    w_out, attn_post_g, ffn_pre_g, w_gate, w_up, w_down, ffn_post_g, g_norm_mix_2, w_in_2,
    b_in_2, b_fgate_2, conv_qk_2, g_mlstm_head_2, pe_cmp_2, w_cmp1_2, w_cmp2_2, rel_bias_2,
    w_branch_2, w_out_2, g_norm_ffn_2, w_gate_2, w_up_2, w_down_2, g_final_2,
):
    x = first_block(
        x, positions, attn_pre_g, w_in, forget_bias, lam_q1, lam_k1, lam_q2, lam_k2, diff_sub_g,
        w_out, attn_post_g, ffn_pre_g, w_gate, w_up, w_down, ffn_post_g,
    )
    return second_block(
        x, g_norm_mix_2, w_in_2, b_in_2, b_fgate_2, conv_qk_2, g_mlstm_head_2, pe_cmp_2,
        w_cmp1_2, w_cmp2_2, rel_bias_2, w_branch_2, w_out_2, g_norm_ffn_2, w_gate_2, w_up_2,
        w_down_2, g_final_2,
    )


_drawn_inputs = setup_inputs


def setup_inputs(seed=0):
    import zlib

    import numpy as np

    out = dict(_drawn_inputs(seed))
    spreads = {}
    factors = {'g_norm_mix_2': 8.0,
     'b_in_2': 6.618,
     'g_mlstm_head_2': 32.5,
     'pe_cmp_2': 7.815,
     'rel_bias_2': 3.209,
     'g_norm_ffn_2': 7.515,
     'g_final_2': 8.137}
    for name, (base, spread) in spreads.items():
        noise = np.random.default_rng([zlib.crc32(name.encode()), seed]).standard_normal(out[name].shape)
        drawn = base * np.exp(spread * noise) if base else spread * noise
        out[name] = __import__('jax').numpy.asarray(drawn.astype(out[name].dtype))
    for name, factor in factors.items():
        out[name] = (out[name] * factor).astype(out[name].dtype)
    return out
```

```python
from contextlib import ExitStack
import math

import numpy as np
import concourse.bass as bass
from concourse import mybir

F32 = mybir.dt.float32
BF16 = mybir.dt.bfloat16
I32 = mybir.dt.int32
ALU = mybir.AluOpType
ACT = mybir.ActivationFunctionType
AX = mybir.AxisListType.X

P = 128
D = 1024
T = 512
NT = T // P
ND = D // P
DFF = 2816
NF = DFF // P
LAYERS = 2
HD = 64
NEG = -1e30
EPS = 1e-6
BIG = 3e38
SCALE = HD ** -0.5

C_QA, C_KA, C_VA, C_QB, C_KB, C_VB, C_F = [512 * i for i in range(7)]
N_DIFF, N_FOX = 4, 8
C_MQ, C_MK, C_MV, C_MO, C_IF, C_NQ, C_NKV, C_NG, C_MERGE = 0, 512, 1024, 1536, 2048, 2056, 2568, 3336, 3360
MH = 4
NH, NG_, NR = 8, 2, 4
CMP_BLOCK, CMP_STRIDE = 32, 16
NCMP = (T - CMP_BLOCK) // CMP_STRIDE + 1
BUCKETS = 32
CONV = 4
REV = 640
NRING = 5

VEC = {}
_at = 0
for _name, _n in (("attn_pre", 16), ("ffn_pre", 16), ("mix_pre", 8), ("ffn2_pre", 8), ("diff_sub", 2),
                  ("b_qk", 8), ("b_mo", 4), ("b_nq", 4), ("b_kv", 6), ("b_merge", 16), ("g_head", 4),
                  ("conv", 32)):
    VEC[_name] = _at
    _at += _n
NVEC = _at

K_ID, K_ROT, K_TRI, K_MASK, K_HOT, K_FREQ = 0, 128, 256, 768, 896, 1408
NCONST = 1409


def shape_constants():
    c = np.zeros((P, NCONST), np.float32)
    c[:, K_ID:K_ID + P] = np.eye(P)
    for m in range(P):
        if m % HD < 8:
            c[m + 8, K_ROT + m] = -1.0
        elif m % HD < 16:
            c[m - 8, K_ROT + m] = 1.0
    k = np.arange(P)[:, None]
    c[:, K_TRI:K_TRI + T] = np.arange(T)[None, :] >= k
    c[:, K_MASK:K_MASK + P] = np.where(np.arange(P)[None, :] > k, NEG, 0.0)
    dist = (T - 1 - np.arange(T)).astype(np.int64)
    nf = np.maximum(dist, 1).astype(np.float32)
    large = 16 + (np.log(nf / np.float32(16)) / np.float32(math.log(64)) * np.float32(16)).astype(np.int32)
    bucket = np.where(dist < 16, dist, np.minimum(large, BUCKETS - 1))
    c[:BUCKETS, K_HOT:K_HOT + T] = bucket[None, :] == np.arange(BUCKETS)[:, None]
    freq = (1.0 / np.power(np.float32(500000.0), np.arange(0, 16, 2, dtype=np.float32) / 16)).astype(np.float32)
    for m in range(P):
        if m % HD < 16:
            c[m, K_FREQ] = freq[m % 8]
    return c


class Queue:

    def __init__(self, engine, semaphore):
        self.engine, self.semaphore, self.count, self.passed = engine, semaphore, 0, {}

    def wait(self, *tokens):
        for token in tokens:
            if token is None:
                continue
            if isinstance(token, list):
                self.wait(*token)
                continue
            semaphore, value = token
            if self.passed.get(semaphore.name, 0) < value:
                self.passed[semaphore.name] = value
                self.engine.wait_ge(semaphore, value)

    def run(self, make, *after):
        self.wait(*after)
        self.count += 1
        make(self.engine).then_inc(self.semaphore, 1)
        return (self.semaphore, self.count)

    def more(self, make, *after):
        self.wait(*after)
        make(self.engine)

    def dma(self, out, in_, arrival, *after):
        self.wait(*after)
        arrival[1] += 16
        self.engine.dma_start(out, in_).then_inc(arrival[0], 16)
        return (arrival[0], arrival[1])

    def last(self):
        return (self.semaphore, self.count) if self.count else None


class Slots:

    def __init__(self, buffers):
        self.buffers, self.turn, self.free = buffers, 0, [[] for _ in buffers]

    def take(self):
        i = self.turn
        self.turn = (i + 1) % len(self.buffers)
        assert self.free[i] is not None, "buffer taken again before its readers were named"
        readers, self.free[i] = self.free[i], None
        return i, self.buffers[i], readers

    def release(self, i, *readers):
        self.free[i] = list(readers)


def program(nc, a, out):
    ctx = ExitStack()
    with ctx:
        def sb(name, shape, dt=F32):
            return ctx.enter_context(nc.sbuf_tensor(name, shape, dt))

        def sem(name):
            return ctx.enter_context(nc.semaphore(name))

        X = sb("x_residual", [P, NT, D])
        HT = sb("h_features", [P, ND, T])
        TOK = sb("token_scratch", [P, NT, D])
        ARENA = sb("arena", [P, 18432])
        BIAS = sb("bias_rows", [P, 8, T])
        RING = [sb(f"weights{i}", [P, 2048]) for i in range(NRING)]
        GROW = sb("gain_row", [P, D])
        COS = sb("cos_table", [P, T])
        SIN = sb("sin_table", [P, T])
        CST = sb("shape_consts", [P, NCONST])
        VC = sb("vector_columns", [P, NVEC])
        PEC = sb("position_columns", [P, 2 * CMP_BLOCK])
        IDB = sb("identity_bf16", [P, P], BF16)
        MKB = sb("mask_bf16", [P, P], BF16)
        ONES = sb("ones", [P, P])
        EPSC = sb("eps_column", [P, 1])
        STAT = sb("row_stats", [P, 16, 8])
        NST = sb("norm_stats", [P, 64])
        LAM = sb("lambda_rows", [P, 4, LAYERS, HD])
        NLAM = sb("neg_lambda", [P, 16])
        FBI = sb("forget_bias_row", [P, LAYERS * N_FOX])
        JUNK = sb("junk", [P, T])
        NEGC = sb("neg_decay", [8, REV])
        BVR = sb("value_bias_rows", [P, 800])
        SM = sb("small_tok", [P, 600])
        PSUM = [ctx.enter_context(nc.psum_tensor(f"bank{i}", [P, T], F32)) for i in range(8)]
        decay_dram = nc.dram_tensor("decay_scratch", [LAYERS, N_FOX, T], F32).ap()
        strip_dram = nc.dram_tensor("bias_scratch", [NH, P, T], F32).ap()

        pe = Queue(nc.tensor, sem("pe_done"))
        act = Queue(nc.scalar, sem("act_done"))
        dve = Queue(nc.vector, sem("dve_done"))
        pool = Queue(nc.gpsimd, sem("pool_done"))
        sync = Queue(nc.sync, sem("sync_done"))
        ring_arrival = [[sem(f"weights{i}_arrival"), 0] for i in range(NRING)]
        ring = Slots(list(range(NRING)))
        banks = Slots(PSUM)
        IDENT = CST[:, K_ID:K_ID + P]
        TRI = CST[:, K_TRI:K_TRI + T]
        MASK = CST[:, K_MASK:K_MASK + P]
        stat = Slots([STAT[:, i, :] for i in range(16)])

        def arena(at, *shape):
            n = int(np.prod(shape))
            assert at + n <= 18432
            v = ARENA[:, at:at + n]
            if len(shape) == 2:
                return v.rearrange("p (a b) -> p a b", a=shape[0])
            if len(shape) == 3:
                return v.rearrange("p (a b c) -> p a b c", a=shape[0], b=shape[1])
            return v

        const_in = [sem("consts_arrival"), 0]
        x_in = [[sem(f"x{t}_arrival"), 0] for t in range(NT)]
        vec_in = [sem("vectors_arrival"), 0]
        row_in = [sem("rows_arrival"), 0]
        gain_in = [sem("gain_row_arrival"), 0]

        x_ready = [sync.dma(X[:, t, :], a["x"][0, t * P:(t + 1) * P, :], x_in[t]) for t in range(NT)]
        consts = pool.dma(CST[:, :], a["shape_constants"], const_in)

        ROWS = arena(0, P)
        PER = arena(128, P)

        def rows(name, src, at=0, cols=None):
            r = VEC[name] + at
            n = src.shape[0]
            dst = ARENA[r:r + n, 0:P] if cols is None else ARENA[r:r + n, cols[0]:cols[1]]
            return pool.dma(dst, src, vec_in)

        def tiles_of(v):
            return v.rearrange("l (k p) -> (l k) p", p=P)

        def row_tiles(v):
            return v.rearrange("(k p) -> k p", p=P)

        b_in = a["b_in_2"][0]
        rows("attn_pre", tiles_of(a["attn_pre_g"]))
        rows("ffn_pre", tiles_of(a["ffn_pre_g"]))
        rows("mix_pre", tiles_of(a["g_norm_mix_2"]))
        rows("ffn2_pre", tiles_of(a["g_norm_ffn_2"]))
        rows("diff_sub", a["diff_sub_g"])
        rows("b_qk", row_tiles(b_in[C_MQ:C_MV]))
        rows("b_mo", row_tiles(b_in[C_MO:C_IF]))
        for g in range(NG_):
            rows("b_nq", b_in[C_NQ + 256 * g:C_NQ + 256 * (g + 1)].rearrange("(r d) -> r d", d=HD),
                 cols=(HD * g, HD * (g + 1)))
        rows("b_kv", row_tiles(b_in[C_NKV:C_NG]))
        rows("b_merge", row_tiles(b_in[C_MERGE:C_MERGE + 2 * D]))
        rows("g_head", tiles_of(a["g_mlstm_head_2"]))
        rows("conv", a["conv_qk_2"][0].rearrange("j (k p) -> (j k) p", p=P))
        for g in range(2):
            vectors = pool.dma(ARENA[0:2 * CMP_BLOCK, P + HD * g:P + HD * (g + 1)],
                               a["pe_cmp_2"][0].rearrange("j l d -> (j l) d"), vec_in)
        for i, name in enumerate(("lam_q1", "lam_q2", "lam_k1", "lam_k2")):
            pool.dma(LAM[:, i, :, :], a[name].partition_broadcast(P), row_in)
        pool.dma(FBI[:, :].rearrange("p (l h) -> p l h", l=LAYERS), a["forget_bias"].partition_broadcast(P), row_in)
        pool.dma(BVR[:, 0:512], b_in[C_MV:C_MO].partition_broadcast(P), row_in)
        pool.dma(BVR[:, 512:640], b_in[C_NKV + 384:C_NKV + 512].partition_broadcast(P), row_in)
        pool.dma(BVR[:, 640:768], b_in[C_NKV + 640:C_NKV + 768].partition_broadcast(P), row_in)
        pool.dma(BVR[:, 768:776], b_in[C_IF:C_NQ].partition_broadcast(P), row_in)
        pool.dma(BVR[:, 776:800], b_in[C_NG:C_MERGE].partition_broadcast(P), row_in)
        BFG = NLAM[:, 8:12]
        pool.dma(BFG, a["b_fgate_2"][0].partition_broadcast(P), row_in)
        POSI = arena(14336, T).bitcast(I32)
        pool.dma(POSI, a["positions"][0].partition_broadcast(P), row_in)
        W2C = sb("w_cmp2_sb", [P, 3, HD])
        for slot, j in ((0, 0), (1, 0), (2, 1)):
            pool.dma(W2C[:, slot, :], a["w_cmp2_2"][0, j], row_in)
        RELB = sb("rel_bias_sb", [BUCKETS, NH])
        row_vectors = pool.dma(RELB[:, :], a["rel_bias_2"], row_in)

        ones_ready = dve.run(lambda e: e.memset(ONES[:, :], 1.0))
        eps_ready = dve.run(lambda e: e.memset(EPSC[:, :], EPS))
        dve.run(lambda e: e.tensor_copy(IDB[:, :], IDENT), consts)
        bf_ready = dve.run(lambda e: e.tensor_copy(MKB[:, :], MASK))

        def weights(kt, pieces):
            i, r, readers = ring.take()
            width = max(p[1].stop for p in pieces)
            view = RING[r][:, 0:kt * width].rearrange("p (k c) -> p k c", k=kt)
            for parts, cols, src in pieces:
                token = sync.dma(view[parts, :, cols], src, ring_arrival[r], *readers)
            return i, view, token

        def slab(w, c0, c1, k0=0, kt=ND):
            return weights(kt, [(slice(0, P), slice(0, c1 - c0),
                                 w[k0 * P:(k0 + kt) * P, c0:c1].rearrange("(k p) c -> p k c", p=P))])

        def matmuls(out_ap, pairs, *after):
            pe.wait(*after)
            n = len(pairs)
            for j, (l, r) in enumerate(pairs):
                f = lambda e, l=l, r=r, j=j: e.matmul(out_ap, l, r, start=(j == 0), stop=(j == n - 1))
                token = pe.run(f) if j == n - 1 else pe.more(f)
            return token

        flip = [0]

        def evacuate(dst, src, *after, scale=None, bias=None, engine=None):
            flip[0] ^= 1
            q = engine or (dve if flip[0] else act)
            if q is dve:
                if scale is None and bias is None:
                    f = lambda e: e.tensor_copy(dst, src)
                elif bias is None:
                    f = lambda e: e.tensor_scalar(dst, src, scale, None, ALU.mult)
                elif scale is None:
                    f = lambda e: e.tensor_scalar(dst, src, bias, None, ALU.add)
                else:
                    f = lambda e: e.tensor_scalar(dst, src, scale, bias, ALU.mult, ALU.add)
            elif bias is None:
                f = lambda e: e.activation(dst, src, ACT.Copy, scale=1.0 if scale is None else scale)
            else:
                f = lambda e: e.activation(dst, src, ACT.Identity, bias=bias, scale=1.0 if scale is None else scale)
            return q.run(f, *after)

        def rstd(dst, ss, n, *after):
            ln = act.run(lambda e: e.activation(dst, ss, ACT.Ln, bias=EPSC[:, 0:1], scale=1.0 / n), eps_ready, *after)
            return act.run(lambda e: e.activation(dst, dst, ACT.Exp, scale=-0.5), ln)

        def turn_tokens(source, gains, ready, k_range=range(ND), dest=None):
            done = []
            for k in k_range:
                b, bank, free = banks.take()
                pe.wait(consts, *ready)
                for t in range(NT):
                    f = lambda e, t=t, k=k, bank=bank: e.transpose(bank[:, t * P:(t + 1) * P], source(t, k), IDENT)
                    turned = pe.run(f, *free) if t == NT - 1 else pe.more(f, *free)
                dst = HT[:, k, :] if dest is None else dest[:, k, :]
                token = evacuate(dst, bank[:, :], turned, scale=gains(k))
                banks.release(b, token)
                done.append(token)
            return done

        def pre_norm(x_tokens, gain_col):
            scaled = []
            for t in range(NT):
                squares = act.run(lambda e, t=t: e.activation(TOK[:, t, :], X[:, t, :], ACT.Square,
                                                              accum_out=NST[:, t:t + 1]),
                                  x_tokens[t], pe.last(), dve.last())
                r = rstd(NST[:, 4 + t:5 + t], NST[:, t:t + 1], D, squares)
                scaled.append(dve.run(lambda e, t=t: e.tensor_scalar(TOK[:, t, :], X[:, t, :], NST[:, 4 + t:5 + t],
                                                                     None, ALU.mult), r))
            return turn_tokens(lambda t, k: TOK[:, t, k * P:(k + 1) * P],
                               lambda k: VC[:, gain_col + k:gain_col + k + 1], scaled)

        def project_features(w, c0, width, h_ready, sink, pieces=None):
            for s in range(0, width, 256):
                cols = min(256, width - s)
                i, view, arrived = slab(w, c0 + s, c0 + s + cols) if pieces is None else weights(ND, pieces(s))
                for m in range(cols // P):
                    b, bank, free = banks.take()
                    token = matmuls(bank[:, :], [(view[:, k, m * P:(m + 1) * P], HT[:, k, :]) for k in range(ND)],
                                    arrived, *h_ready, *free)
                    banks.release(b, *sink(s // P + m, bank, token))
                ring.release(i, token)

        def project_tokens(w, c0, width, h_ready, sink):
            for s in range(0, width, 256):
                cols = min(256, width - s)
                i, view, arrived = slab(w, c0 + s, c0 + s + cols)
                for t in range(NT):
                    b, bank, free = banks.take()
                    token = matmuls(bank[:, 0:cols], [(HT[:, k, t * P:(t + 1) * P], view[:, k, 0:cols]) for k in range(ND)],
                                    arrived, *h_ready, *free)
                    banks.release(b, *sink(t, s, cols, bank, token))
                ring.release(i, token)

        def product_tokens(source, kt, w, ready, sink):
            for half in range(2):
                taken = [banks.take() for _ in range(NT)]
                for k0 in range(0, kt, 4):
                    n = min(4, kt - k0)
                    i, view, arrived = slab(w, half * 512, half * 512 + 512, k0, n)
                    for k in range(k0, k0 + n):
                        for t in range(NT):
                            b, bank, free = taken[t]
                            f = lambda e, k=k, t=t, k0=k0, view=view, bank=bank: e.matmul(
                                bank[:, :], source(k)[:, t * P:(t + 1) * P], view[:, k - k0, :],
                                start=(k == 0), stop=(k == kt - 1))
                            waits = [arrived, ready[k]] + (free if k == 0 else [])
                            if k == kt - 1:
                                token = pe.run(f, *waits)
                                banks.release(b, *sink(half, t, bank, token))
                            elif t == NT - 1 and k == k0 + n - 1:
                                token = pe.run(f, *waits)
                            else:
                                pe.more(f, *waits)
                    ring.release(i, token)

        def gain_row(src):
            return pool.dma(GROW[:, :], src.partition_broadcast(P), gain_in, dve.last())

        def post_norm_sink(g_row, x_tokens):
            copied = {}

            def sink(half, t, bank, token):
                y = TOK[:, t, half * 512:(half + 1) * 512]
                copy = dve.run(lambda e: e.tensor_copy(y, bank[:, :]), token)
                sq = act.run(lambda e: e.activation(JUNK[:, :], y, ACT.Square,
                                                    accum_out=NST[:, 16 + 4 * half + t:17 + 4 * half + t]),
                             copy, act.last())
                if half == 1:
                    total = dve.run(lambda e: e.tensor_tensor(NST[:, 24 + t:25 + t], NST[:, 16 + t:17 + t],
                                                              NST[:, 20 + t:21 + t], ALU.add), sq)
                    r = rstd(NST[:, 28 + t:29 + t], NST[:, 24 + t:25 + t], D, total)
                    n = dve.run(lambda e: e.scalar_tensor_tensor(TOK[:, t, :], TOK[:, t, :], NST[:, 28 + t:29 + t],
                                                                 GROW[:, :], ALU.mult, ALU.mult), r, g_row)
                    x_tokens[t] = dve.run(lambda e: e.tensor_tensor(X[:, t, :], X[:, t, :], TOK[:, t, :], ALU.add), n)
                return [copy]
            return sink

        def feed_forward(w_gate, w_up, w_down, h_ready, sink):
            G = arena(0, NF, T)
            silu = Slots([arena(11264 + 512 * i, T) for i in range(3)])
            ready = [None] * NF
            quiet = [pe.last(), act.last(), dve.last()]
            for s in range(0, DFF, 256):
                gi, gv, g_in = slab(w_gate, s, s + 256)
                ui, uv, u_in = slab(w_up, s, s + 256)
                for m in range(2):
                    f = s // P + m
                    tokens, bs = [], []
                    for view, arrived in ((gv, g_in), (uv, u_in)):
                        b, bank, free = banks.take()
                        tokens.append(matmuls(bank[:, :], [(view[:, k, m * P:(m + 1) * P], HT[:, k, :]) for k in range(ND)],
                                              arrived, *h_ready, *free))
                        bs.append((b, bank))
                    si, sg, sfree = silu.take()
                    gated = act.run(lambda e, sg=sg, bank=bs[0][1]: e.activation(sg, bank[:, :], ACT.Silu),
                                    tokens[0], *quiet, *sfree)
                    banks.release(bs[0][0], gated)
                    ready[f] = dve.run(lambda e, f=f, sg=sg, bank=bs[1][1]: e.tensor_tensor(G[:, f, :], bank[:, :], sg, ALU.mult),
                                       tokens[1], gated, *quiet)
                    silu.release(si, ready[f])
                    banks.release(bs[1][0], ready[f])
                ring.release(gi, tokens[0])
                ring.release(ui, tokens[1])
            product_tokens(lambda k: G[:, k, :], NF, w_down, ready, sink)

        def attend(units, e_slots, p_slots):

            def scores(u):
                u.banks = []
                for l, r in u.maps:
                    b, bank, free = banks.take()
                    pe.wait(*u.ready, *free)
                    f = lambda e, l=l, r=r, bank=bank: e.matmul(bank[:, 0:u.w], l, r, start=True, stop=not u.mask)
                    if u.mask:
                        pe.more(f)
                        token = pe.run(lambda e, bank=bank: e.matmul(bank[:, u.w - P:u.w], IDB[:, :], MKB[:, :],
                                                                     start=False, stop=True), bf_ready)
                    else:
                        token = pe.run(f)
                    u.banks.append((b, bank, token))

            def soften(u):
                si, u.stat, sfree = stat.take()
                u.si, u.e = si, []
                for j, (b, bank, token) in enumerate(u.banks):
                    ei, e_, efree = e_slots.take()
                    nm, sm = u.stat[:, j:j + 1], u.stat[:, 2 + j:3 + j]
                    dst = e_[:, 0:u.w]
                    if u.bias is None:
                        mx = dve.run(lambda e, bank=bank, nm=nm: e.tensor_reduce(nm, bank[:, 0:u.w], AX, ALU.max, negate=True),
                                     token, *sfree)
                        ex = act.run(lambda e, bank=bank, nm=nm, sm=sm, dst=dst: e.activation(
                            dst, bank[:, 0:u.w], ACT.Exp, bias=nm, accum_out=sm), mx, *efree, *sfree)
                        banks.release(b, ex)
                    else:
                        mx = dve.run(lambda e, bank=bank, nm=nm, dst=dst: e.tensor_tensor_reduce(
                            dst, bank[:, 0:u.w], u.bias, -1.0, u.floor, ALU.add, ALU.min, nm),
                            token, *sfree, *efree, *u.bias_ready)
                        ex = act.run(lambda e, nm=nm, sm=sm, dst=dst: e.activation(
                            dst, dst, ACT.Exp, bias=nm, scale=-1.0, accum_out=sm), mx)
                        banks.release(b, mx)
                    u.e.append((ei, e_, ex))

            def mix(u):
                n = len(u.maps)
                rc = u.stat[:, 4:4 + n]
                u.rc = rc
                if u.coef is not None:
                    cf = u.stat[:, 6:7]
                    s1 = dve.run(lambda e: e.tensor_scalar(cf, u.stat[:, 2:3], 1e-30, None, ALU.max), u.e[0][2])
                    s2 = dve.run(lambda e: e.reciprocal(rc, cf), s1)
                    u.norm = dve.run(lambda e: e.tensor_tensor(cf, rc, u.coef, ALU.mult), s2, *u.coef_ready)
                    u.scalar = cf
                else:
                    u.norm = dve.run(lambda e: e.reciprocal(rc, u.stat[:, 2:2 + n]), *[x[2] for x in u.e])
                    u.scalar = rc
                u.p_ready = u.e[0][2]
                if n == 2:
                    (i0, e0, _), (i1, e1, _) = u.e
                    nl = u.stat[:, 6:7]
                    l = dve.run(lambda e: e.tensor_tensor(nl, u.stat[:, 5:6], u.neg_lambda, ALU.mult), u.norm)
                    s = act.run(lambda e: e.activation(e0[:, 0:u.w], e0[:, 0:u.w], ACT.Copy, scale=u.stat[:, 4:5]), u.norm)
                    u.p_ready = dve.run(lambda e: e.scalar_tensor_tensor(e0[:, 0:u.w], e1[:, 0:u.w], nl, e0[:, 0:u.w],
                                                                         ALU.mult, ALU.add), l, s)
                    e_slots.release(i1, u.p_ready)

            def turn(u):
                b, bank, free = banks.take()
                pe.wait(u.p_ready, *free)
                e0 = u.e[0][1]
                chunks = [(c, min(P, u.w - c)) for c in range(0, u.w, P)]
                for c, n in chunks:
                    f = lambda e, c=c, n=n: e.transpose(bank[0:n, c:c + P], e0[:, c:c + n], IDENT)
                    token = pe.run(f) if c + n == u.w else pe.more(f)
                e_slots.release(u.e[0][0], token)
                u.pi, u.pt, pfree = p_slots.take()
                n = chunks[0][1]
                w = len(chunks) * P
                u.pt_ready = evacuate(u.pt[0:n, 0:w], bank[0:n, 0:w], token, *pfree)
                banks.release(b, u.pt_ready)

            def values(u):
                b, bank, free = banks.take()
                pairs = []
                for j, c in enumerate(range(0, u.w, P)):
                    n = min(P, u.w - c)
                    pairs.append((u.pt[0:n, c:c + P], u.v(j)))
                token = matmuls(bank[:, 0:u.nv], pairs, u.pt_ready, *u.v_ready, *free)
                p_slots.release(u.pi, token)
                tokens = u.finish(u, bank, token)
                banks.release(b, *tokens)
                stat.release(u.si, *tokens)

            n = len(units)
            for i in range(n + 3):
                if i < n:
                    scores(units[i])
                    soften(units[i])
                if 1 <= i <= n:
                    mix(units[i - 1])
                if 2 <= i <= n + 1:
                    turn(units[i - 2])
                if i >= 3:
                    values(units[i - 3])

        class Unit:

            def __init__(self, w, nv, maps, ready, v, v_ready, finish, neg_lambda=None, bias=None, bias_ready=(),
                         floor=BIG, coef=None, coef_ready=(), mask=True):
                self.w, self.nv, self.maps, self.ready, self.v, self.v_ready = w, nv, maps, ready, v, v_ready
                self.finish, self.neg_lambda, self.bias, self.bias_ready = finish, neg_lambda, bias, bias_ready
                self.floor, self.coef, self.coef_ready, self.mask = floor, coef, coef_ready, mask

        def log_sigmoid(dst, src, tmp, ready):
            m = dve.run(lambda e: e.tensor_scalar(dst, src, 0.0, None, ALU.min), ready)
            ab = dve.run(lambda e: e.scalar_tensor_tensor(tmp, src, -1.0, src, ALU.mult, ALU.max), ready)
            ex = act.run(lambda e: e.activation(tmp, tmp, ACT.Exp, scale=-1.0), ab)
            ln = act.run(lambda e: e.activation(tmp, tmp, ACT.Ln, bias=ONES[:, 0:1]), ex, ones_ready)
            return dve.run(lambda e: e.tensor_tensor(dst, dst, tmp, ALU.subtract), ln, m)

        b, bank, free = banks.take()
        turned = pe.run(lambda e, bank=bank: e.transpose(bank[:, 0:NVEC], ROWS[0:NVEC, :], CST[0:NVEC, 0:NVEC]), consts, vectors)
        vc_ready = evacuate(VC[:, :], bank[:, 0:NVEC], turned, engine=dve)
        banks.release(b, vc_ready)
        b, bank, free = banks.take()
        turned = pe.run(lambda e, bank=bank: e.transpose(bank[:, 0:64], PER[0:64, :], CST[0:64, 0:64]))
        pec_ready = evacuate(PEC[:, :], bank[:, 0:64], turned, engine=dve)
        banks.release(b, pec_ready)
        lam_init = [0.8 - 0.6 * math.exp(-0.3 * l) for l in range(LAYERS)]
        for l in range(LAYERS):
            c = VEC["diff_sub"] + l
            vc_ready = dve.run(lambda e, c=c, l=l: e.tensor_scalar(VC[:, c:c + 1], VC[:, c:c + 1], 1.0 - lam_init[l],
                                                                   None, ALU.mult), vc_ready)
        act.wait(vc_ready)
        h_ready = pre_norm(x_ready, VEC["attn_pre"])

        prod = dve.run(lambda e: e.tensor_tensor(LAM[:, 0:2, :, :], LAM[:, 0:2, :, :], LAM[:, 2:4, :, :], ALU.mult), row_vectors)
        dots = dve.run(lambda e: e.tensor_reduce(NLAM[:, 0:4], LAM[:, 0:2, :, :].rearrange("p a l d -> p (a l) d"),
                                                 AX, ALU.add), prod)
        exps = act.run(lambda e: e.activation(NLAM[:, 0:4], NLAM[:, 0:4], ACT.Exp), dots)
        diff = dve.run(lambda e: e.tensor_tensor(NLAM[:, 4:6], NLAM[:, 2:4], NLAM[:, 0:2], ALU.subtract), exps)
        for l in range(LAYERS):
            lam_ready = dve.run(lambda e, l=l: e.tensor_scalar(NLAM[:, 4 + l:5 + l], NLAM[:, 4 + l:5 + l], -lam_init[l],
                                                               None, ALU.add), diff)

        ang, turns_, arg = arena(14848, T), arena(15360, T), arena(15872, T)
        c2pi = [6.28125, 0.0019350051879882812, 3.019916050561733e-07]
        posf = dve.run(lambda e: e.tensor_copy(ang, POSI), row_vectors)
        angle = dve.run(lambda e: e.tensor_scalar(ang, ang, CST[:, K_FREQ:K_FREQ + 1], None, ALU.mult), posf, consts)
        for table, quarter in ((SIN, 0.0), (COS, 0.25)):
            q = dve.run(lambda e, quarter=quarter: e.tensor_scalar(turns_, ang, 1.0 / (2 * math.pi), quarter, ALU.mult, ALU.add),
                        angle, act.last(), dve.last())
            q = dve.run(lambda e: e.tensor_scalar(turns_, turns_, 12582912.0, None, ALU.add), q)
            q = dve.run(lambda e: e.tensor_scalar(turns_, turns_, -12582912.0, None, ALU.add), q)
            src = ang
            for c in c2pi:
                q = dve.run(lambda e, c=c, src=src: e.scalar_tensor_tensor(arg, turns_, -c, src, ALU.mult, ALU.add), q)
                src = arg
            q = dve.run(lambda e, quarter=quarter: e.tensor_scalar(arg, arg, quarter * 2 * math.pi, 3.1415925, ALU.add, ALU.min), q)
            q = dve.run(lambda e: e.tensor_scalar(arg, arg, -3.1415925, None, ALU.max), q)
            rope_ready = act.run(lambda e, table=table: e.activation(table[:, :], arg, ACT.Sin), q)

        rev_io = [sem("bias_scratch_io"), 0]
        strip_in = [sem("bias_strips_arrival"), 0]
        b, bank, free = banks.take()
        hot = matmuls(bank[0:NH, :], [(RELB[:, :], CST[0:BUCKETS, K_HOT:K_HOT + T])], row_vectors, *free)
        REVB = sb("reversed_bias", [NH, REV])
        rv = dve.run(lambda e, bank=bank: e.tensor_copy(REVB[:, 0:T], bank[0:NH, :]), hot)
        banks.release(b, rv)
        rv2 = dve.run(lambda e: e.memset(REVB[:, T:REV], NEG))
        rows_of = REVB[:, P - 1:P - 1 + T]
        shifted = bass.AP(rows_of.tensor, rows_of.offset, [list(rows_of.ap[0]), [-1, P], [1, T]])
        rev_written = pool.dma(strip_dram, shifted, rev_io, rv, rv2)

        decay_io = [sem("decay_scratch_io"), 0]
        decay_in = [sem("decay_rows_arrival"), 0]
        x_tokens = list(x_ready)
        for layer in range(LAYERS):
            w_in = a["w_in"][layer]
            QA, KA, QB, KB = (arena(2048 * i, 4, T) for i in range(4))
            V = arena(8192, NT, D)
            e_slots = Slots([arena(12288 + 512 * i, T) for i in range(6)])
            p_slots = Slots([arena(15360 + 512 * i, T) for i in range(3)])
            rope = Slots([arena(16896 + 512 * i, T) for i in range(3)])
            if layer:
                h_ready = pre_norm(x_tokens, VEC["attn_pre"] + ND * layer)
            quiet = [pe.last(), act.last(), dve.last()]
            act.wait(*quiet)
            dve.wait(*quiet)

            LF = SM[:, 0:32]

            def gate_sink(t, s, cols, bank, token):
                return [dve.run(lambda e: e.tensor_tensor(LF[:, 8 * t:8 * t + 8], bank[:, 0:8],
                                                          FBI[:, 8 * layer:8 * layer + 8], ALU.add), token, row_vectors)]
            project_tokens(w_in, C_F, N_FOX, h_ready, gate_sink)
            lf = log_sigmoid(SM[:, 32:64], LF, SM[:, 64:96], dve.last())
            qk_ready = {}

            def rotary_sink(dst, scale, key):
                pending = []

                def finish():
                    m, tmp, ri, copied = pending.pop(0)
                    b, bank, free = banks.take()
                    rot = matmuls(bank[:, :], [(CST[:, K_ROT:K_ROT + P], tmp)], copied, consts, *free)
                    straight = dve.run(lambda e: e.tensor_tensor(dst[:, m, :], tmp, COS[:, :], ALU.mult), copied, rope_ready)
                    crossed = dve.run(lambda e: e.tensor_tensor(tmp, bank[:, :], SIN[:, :], ALU.mult), rot, straight)
                    banks.release(b, crossed)
                    qk_ready[key, m] = dve.run(lambda e: e.tensor_tensor(dst[:, m, :], dst[:, m, :], tmp, ALU.add), crossed)
                    rope.release(ri, qk_ready[key, m])

                def sink(m, bank, token):
                    if pending:
                        finish()
                    ri, tmp, rfree = rope.take()
                    copied = evacuate(tmp, bank[:, :], token, *rfree, scale=scale, engine=act)
                    pending.append((m, tmp, ri, copied))
                    return [copied]
                return sink, finish

            sink, finish = rotary_sink(QA, SCALE, "qa")
            project_features(w_in, C_QA, 512, h_ready, sink)
            b, bank, free = banks.take()
            pe.wait(lf, *free)
            for s in range(NT):
                f = lambda e, s=s, bank=bank: e.matmul(bank[0:N_FOX, s * P:T], SM[:, 32 + 8 * s:40 + 8 * s], TRI[:, 0:T - s * P],
                                                       start=(s == 0), stop=(s == NT - 1))
                summed = pe.run(f) if s == NT - 1 else pe.more(f)
            nc_ready = dve.run(lambda e, bank=bank: e.tensor_scalar(NEGC[:, 0:T], bank[0:N_FOX, :], -1.0, None, ALU.mult), summed)
            banks.release(b, nc_ready)
            decay_written = pool.dma(decay_dram[layer], NEGC[:, 0:T], decay_io, nc_ready)
            decay_ready = pool.dma(BIAS[:, :, :], decay_dram[layer].partition_broadcast(P), decay_in, decay_written,
                                   dve.last())
            finish()
            sink, finish = rotary_sink(KA, None, "ka")
            project_features(w_in, C_KA, 512, h_ready, sink)

            v_ready = {}

            def value_sink(base):
                def sink(t, s, cols, bank, token):
                    v_ready[t, base + s] = evacuate(V[:, t, base + s:base + s + cols], bank[:, 0:cols], token)
                    return [v_ready[t, base + s]]
                return sink
            project_tokens(w_in, C_VA, 512, h_ready, value_sink(0))
            finish()

            def plain_sink(dst, scale, key):
                def sink(m, bank, token):
                    qk_ready[key, m] = evacuate(dst[:, m, :], bank[:, :], token, scale=scale)
                    return [qk_ready[key, m]]
                return sink
            project_features(w_in, C_QB, 512, h_ready, plain_sink(QB, SCALE, "qb"))
            project_features(w_in, C_KB, 512, h_ready, plain_sink(KB, None, "kb"))
            project_tokens(w_in, C_VB, 512, h_ready, value_sink(512))
            all_v = list(v_ready.values())

            SS = NST[:, 32:48]
            tok_free = [pe.last()]
            squares = []

            def diff_finish(h, t):
                def finish(u, bank, token):
                    dst = TOK[:, t, h * P:(h + 1) * P]
                    copy = dve.run(lambda e: e.tensor_copy(dst, bank[:, 0:P]), token, *tok_free)
                    squares.append(act.run(lambda e: e.activation(JUNK[:, 0:P], dst, ACT.Square,
                                                                  accum_out=SS[:, 4 * t + h:4 * t + h + 1]), copy, act.last()))
                    return [copy]
                return finish

            fox_done = []

            def fox_finish(h, t):
                def finish(u, bank, token):
                    fox_done.append(dve.run(lambda e: e.tensor_scalar(TOK[:, t, 512 + h * HD:512 + (h + 1) * HD], bank[:, 0:HD],
                                                                      u.scalar, None, ALU.mult), token, u.norm, *tok_free))
                    return [fox_done[-1]]
                return finish

            units = []
            for h in range(N_DIFF):
                for t in range(NT):
                    w = (t + 1) * P
                    units.append(Unit(
                        w=w, nv=P, maps=[(QA[m * HD:(m + 1) * HD, h, t * P:w], KA[m * HD:(m + 1) * HD, h, 0:w]) for m in range(2)],
                        ready=[qk_ready["qa", h], qk_ready["ka", h]], neg_lambda=NLAM[:, 4 + layer:5 + layer],
                        v=lambda j, h=h: V[:, j, h * P:(h + 1) * P], v_ready=all_v, finish=diff_finish(h, t)))
            dve.wait(lam_ready)
            for h in range(N_FOX):
                m, r = h // 2, slice(HD * (h % 2), HD * (h % 2) + HD)
                for t in range(NT):
                    w = (t + 1) * P
                    units.append(Unit(
                        w=w, nv=HD, maps=[(QB[r, m, t * P:w], KB[r, m, 0:w])], ready=[qk_ready["qb", m], qk_ready["kb", m]],
                        bias=BIAS[:, h, 0:w], bias_ready=[decay_ready],
                        v=lambda j, h=h: V[:, j, 512 + h * HD:512 + (h + 1) * HD], v_ready=all_v, finish=fox_finish(h, t)))
            attend(units, e_slots, p_slots)

            r = rstd(SS, SS, P, *squares)
            heads = TOK[:, :, 0:512].rearrange("p t (h e) -> p t h e", h=N_DIFF)
            by = SS.rearrange("p (t h) -> p t h", t=NT).unsqueeze(3).to_broadcast([P, NT, N_DIFF, P])
            normed = dve.run(lambda e: e.tensor_tensor(heads, heads, by, ALU.mult), r)
            c = VEC["diff_sub"] + layer
            m_ready = turn_tokens(lambda t, k: TOK[:, t, k * P:(k + 1) * P],
                                  lambda k: VC[:, c:c + 1] if k < 4 else None, [normed, fox_done[-1]])
            g_row = gain_row(a["attn_post_g"][layer])
            product_tokens(lambda k: HT[:, k, :], ND, a["w_out"][layer], m_ready, post_norm_sink(g_row, x_tokens))
            h_ready = pre_norm(x_tokens, VEC["ffn_pre"] + ND * layer)
            g_row = gain_row(a["ffn_post_g"][layer])
            feed_forward(a["w_gate"][layer], a["w_up"][layer], a["w_down"][layer], h_ready, post_norm_sink(g_row, x_tokens))

        w_in = a["w_in_2"][0]
        h_ready = pre_norm(x_tokens, VEC["mix_pre"])
        strips_ready = pool.dma(BIAS[:, :, :], strip_dram.rearrange("h p m -> p h m"), strip_in, rev_written, dve.last())
        quiet = [pe.last(), act.last(), dve.last()]
        act.wait(*quiet)
        dve.wait(*quiet)

        QK = arena(0, 8, T)
        VA = arena(4096, NT, MH, P + 1)
        SO = arena(6160, MH, T)
        KTOK = arena(8208, NT, MH, P)
        RM = arena(10256, NT, T)
        HH = arena(12304, NT, MH, P + 1)
        conv_in = Slots([arena(14368 + 516 * i, 516) for i in range(2)])
        conv_acc = Slots([arena(15400 + 512 * i, T) for i in range(2)])
        VW = Slots([arena(16424 + 129 * i, P + 1) for i in range(2)])
        CST8 = arena(16682, MH, P + 1)
        PM = Slots([arena(17198 + 128 * i, P) for i in range(3)])
        PTM = Slots([arena(17582 + 128 * i, P) for i in range(3)])
        O1 = Slots([arena(17966 + 129 * i, P + 1) for i in range(2)])

        IFG = SM[:, 0:32].rearrange("p (t c) -> p t c", t=NT)
        NGT = SM[:, 32:128].rearrange("p (t c) -> p t c", t=NT)

        def if_sink(t, s, cols, bank, token):
            return [dve.run(lambda e: e.tensor_tensor(IFG[:, t, :], bank[:, 0:8], BVR[:, 768:776], ALU.add), token)]
        project_tokens(w_in, C_IF, 8, h_ready, if_sink)
        LF = SM[:, 128:144]
        fb = dve.run(lambda e: e.tensor_tensor(LF.rearrange("p (c h) -> p c h", c=NT), IFG[:, :, 4:8],
                                               BFG.unsqueeze(1).to_broadcast([P, NT, MH]), ALU.add), dve.last())
        LS = SM[:, 144:160]
        lf_ready = log_sigmoid(LS, LF, SM[:, 160:176], fb)

        qk_ready = [None] * 8

        def conv_sink(m, bank, token):
            ci, cin, cfree = conv_in.take()
            ai, acc, afree = conv_acc.take()
            pad = dve.run(lambda e: e.memset(cin[:, 0:CONV - 1], 0.0), *cfree)
            copied = act.run(lambda e: e.activation(cin[:, CONV - 1:CONV - 1 + T], bank[:, :], ACT.Identity,
                                                    bias=VC[:, VEC["b_qk"] + m:VEC["b_qk"] + m + 1]), token, *cfree)
            col = lambda j: VC[:, VEC["conv"] + 8 * j + m:VEC["conv"] + 8 * j + m + 1]
            s = dve.run(lambda e: e.tensor_scalar(acc, cin[:, 0:T], col(0), None, ALU.mult), copied, pad, *afree)
            for j in range(1, CONV):
                s = dve.run(lambda e, j=j: e.scalar_tensor_tensor(acc, cin[:, j:j + T], col(j), acc, ALU.mult, ALU.add), s)
            conv_in.release(ci, s)
            done = act.run(lambda e: e.activation(QK[:, m, :], acc, ACT.Silu), s)
            if m >= 4:
                done = dve.run(lambda e: e.tensor_scalar(QK[:, m, :], QK[:, m, :], P ** -0.5, None, ALU.mult), done)
            conv_acc.release(ai, done)
            qk_ready[m] = done
            return [copied]
        project_features(w_in, C_MQ, 1024, h_ready, conv_sink)

        so_ready = [None] * MH

        def so_sink(m, bank, token):
            so_ready[m] = act.run(lambda e: e.activation(SO[:, m, :], bank[:, :], ACT.Sigmoid,
                                                         bias=VC[:, VEC["b_mo"] + m:VEC["b_mo"] + m + 1]), token)
            return [so_ready[m]]
        project_features(w_in, C_MO, 512, h_ready, so_sink)

        def ng_sink(t, s, cols, bank, token):
            add = dve.run(lambda e: e.tensor_tensor(NGT[:, t, :], bank[:, 0:24], BVR[:, 776:800], ALU.add), token)
            ng_ready.append(act.run(lambda e: e.activation(NGT[:, t, :], NGT[:, t, :], ACT.Sigmoid), add))
            return [add]
        ng_ready = []
        project_tokens(w_in, C_NG, 24, h_ready, ng_sink)

        va_ones = dve.run(lambda e: e.memset(VA[:, :, :, P:P + 1], 1.0))
        va_ready = [[va_ones] for _ in range(NT)]

        def va_sink(t, s, cols, bank, token):
            h0 = s // P
            dst = VA[:, t, h0:h0 + 2, 0:P]
            done = dve.run(lambda e: e.tensor_tensor(dst, bank[:, 0:256].rearrange("p (h e) -> p h e", h=2),
                                                     BVR[:, s:s + 256].rearrange("p (h e) -> p h e", h=2), ALU.add), token)
            va_ready[t].append(done)
            return [done]
        project_tokens(w_in, C_MV, 512, h_ready, va_sink)

        ktok_ready = []
        for c in range(NT):
            b, bank, free = banks.take()
            pe.wait(*free, *qk_ready[4:8])
            for h in range(MH):
                f = lambda e, c=c, h=h, bank=bank: e.transpose(bank[:, h * P:(h + 1) * P], QK[:, 4 + h, c * P:(c + 1) * P], IDENT)
                turned = pe.run(f) if h == MH - 1 else pe.more(f)
            ktok_ready.append(evacuate(KTOK[:, c, :, :].rearrange("p h e -> p (h e)"), bank[:, :], turned))
            banks.release(b, ktok_ready[-1])

        b, bank, free = banks.take()
        pe.more(lambda e, bank=bank: e.matmul(bank[:, 0:16], TRI[:, 0:P], LS, start=True, stop=True), lf_ready, *free)
        sums = pe.run(lambda e, bank=bank: e.matmul(bank[:, 16:32], ONES[:, :], LS, start=True, stop=True), ones_ready)
        BCBL = SM[:, 176:208]
        bc = dve.run(lambda e, bank=bank: e.tensor_copy(BCBL, bank[:, 0:32]), sums)
        banks.release(b, bc)
        BC, BL = BCBL[:, 0:16], BCBL[:, 16:32]
        R = SM[:, 208:224]
        r_ready = dve.run(lambda e: e.tensor_tensor(R.rearrange("p (c h) -> p c h", c=NT), IFG[:, :, 0:4],
                                                    BC.rearrange("p (c h) -> p c h", c=NT), ALU.subtract), bc)
        MR, RX = SM[:, 224:240], SM[:, 240:256]
        DG = HH.rearrange("p a b c -> p (a b c)")[:, 0:2048].rearrange("p (c h e) -> p c h e", c=NT, h=MH)
        rm_ready, diags = [], []
        for c in range(NT):
            for h in range(MH):
                d = dve.run(lambda e, c=c, h=h: e.tensor_scalar(DG[:, c, h, :], IDENT, R[:, 4 * c + h:4 * c + h + 1],
                                                                None, ALU.mult), r_ready)
            diags.append(d)
        for c in range(NT):
            b, bank, free = banks.take()
            spread = matmuls(bank[:, :], [(ONES[:, :], DG[:, c, :, :].rearrange("p h e -> p (h e)"))], diags[c], *free)
            b3 = bank[:, :].rearrange("p (h e) -> p h e", h=MH)
            r3 = RM[:, c, :].rearrange("p (h e) -> p h e", h=MH)
            whole = dve.run(lambda e, c=c, b3=b3: e.tensor_reduce(RX[:, 4 * c:4 * c + 4], b3, AX, ALU.max), spread)
            masked = dve.run(lambda e, b3=b3, r3=r3: e.tensor_tensor(r3, b3, MASK.unsqueeze(1).to_broadcast([P, MH, P]), ALU.add), spread)
            banks.release(b, masked)
            rm_ready.append(dve.run(lambda e, c=c, r3=r3: e.tensor_reduce(MR[:, 4 * c:4 * c + 4], r3, AX, ALU.max), masked))
        MP, MX = SM[:, 256:276], SM[:, 276:292]
        step = dve.run(lambda e: e.memset(MP[:, 0:4], 0.0))
        for c in range(NT):
            s = slice(4 * c, 4 * c + 4)
            mx = dve.run(lambda e, s=s: e.tensor_tensor(MX[:, s], MP[:, s], RX[:, s], ALU.max), step, rm_ready[c])
            step = dve.run(lambda e, s=s, c=c: e.tensor_tensor(MP[:, 4 * c + 4:4 * c + 8], BL[:, s], MX[:, s], ALU.add), mx)
        NM2, SI, EM, WK, DC = (SM[:, 292 + 16 * i:308 + 16 * i] for i in range(5))
        q = dve.run(lambda e: e.tensor_tensor(NM2, MR, MP[:, 0:16], ALU.max), step)
        q = dve.run(lambda e: e.tensor_scalar(NM2, NM2, -1.0, None, ALU.mult), q)
        q1 = dve.run(lambda e: e.tensor_tensor(SI, MP[:, 0:16], NM2, ALU.add), q)
        q2 = dve.run(lambda e: e.tensor_tensor(EM, NM2, BC, ALU.subtract), q)
        q3 = dve.run(lambda e: e.tensor_tensor(WK, R, MX, ALU.subtract), step)
        q4 = dve.run(lambda e: e.tensor_tensor(DC, MP[:, 0:16], MX, ALU.subtract), step)
        gates_ready = act.run(lambda e: e.activation(SM[:, 308:372], SM[:, 308:372], ACT.Exp), q1, q2, q3, q4)
        dve.wait(gates_ready)

        hh_ready = []
        c_ready = [None] * MH
        for c in range(NT):
            for h in range(MH):
                col = 4 * c + h
                q_ = QK[:, h, c * P:(c + 1) * P]
                b, bank, free = banks.take()
                s_tok = matmuls(bank[:, 0:P], [(q_, QK[:, 4 + h, c * P:(c + 1) * P])], *qk_ready, *free)
                pi, pm, pfree = PM.take()
                ex = act.run(lambda e, pm=pm, c=c, h=h, col=col: e.activation(
                    pm, RM[:, c, h * P:(h + 1) * P], ACT.Exp, bias=NM2[:, col:col + 1]), gates_ready, rm_ready[c], *pfree)
                pr = dve.run(lambda e, pm=pm, bank=bank: e.tensor_tensor(pm, bank[:, 0:P], pm, ALU.mult), ex, s_tok)
                banks.release(b, pr)
                b, bank, free = banks.take()
                tt = pe.run(lambda e, pm=pm, bank=bank: e.transpose(bank[:, 0:P], pm, IDENT), pr, *free)
                PM.release(pi, tt)
                ti, pt, tfree = PTM.take()
                pt_ready = evacuate(pt, bank[:, 0:P], tt, *tfree, engine=act)
                banks.release(b, pt_ready)
                b, bank, free = banks.take()
                o1 = matmuls(bank[:, 0:P + 1], [(pt, VA[:, c, h, :])], pt_ready, *va_ready[c], *free)
                PTM.release(ti, o1)
                if c == 0:
                    done = dve.run(lambda e, bank=bank, c=c, h=h: e.tensor_copy(HH[:, c, h, :], bank[:, 0:P + 1]), o1)
                    banks.release(b, done)
                else:
                    oi, o, ofree = O1.take()
                    cp = evacuate(o, bank[:, 0:P + 1], o1, *ofree, engine=act)
                    banks.release(b, cp)
                    b, bank, free = banks.take()
                    o2 = matmuls(bank[:, 0:P + 1], [(q_, CST8[:, h, :])], c_ready[h], *free)
                    done = dve.run(lambda e, bank=bank, o=o, c=c, h=h, col=col: e.scalar_tensor_tensor(
                        HH[:, c, h, :], bank[:, 0:P + 1], SI[:, col:col + 1], o, ALU.mult, ALU.add), o2, cp)
                    banks.release(b, done)
                    O1.release(oi, done)
                hh_ready.append(done)
                if c < NT - 1:
                    wi, vw, wfree = VW.take()
                    vwr = dve.run(lambda e, vw=vw, c=c, h=h, col=col: e.tensor_scalar(vw, VA[:, c, h, :], WK[:, col:col + 1],
                                                                                      None, ALU.mult), *va_ready[c], *wfree)
                    b, bank, free = banks.take()
                    up = matmuls(bank[:, 0:P + 1], [(KTOK[:, c, h, :], vw)], vwr, ktok_ready[c], *free)
                    VW.release(wi, up)
                    if c == 0:
                        c_ready[h] = dve.run(lambda e, bank=bank, h=h: e.tensor_copy(CST8[:, h, :], bank[:, 0:P + 1]), up)
                    else:
                        c_ready[h] = dve.run(lambda e, bank=bank, h=h, col=col: e.scalar_tensor_tensor(
                            CST8[:, h, :], CST8[:, h, :], DC[:, col:col + 1], bank[:, 0:P + 1], ALU.mult, ALU.add), up, o2)
                    banks.release(b, c_ready[h])

        DEN, SSM, FAC = SM[:, 372:388], SM[:, 388:404], SM[:, 404:420]
        per_head = lambda v: v.rearrange("p (c h) -> p c h", c=NT)
        q = dve.run(lambda e: e.scalar_tensor_tensor(per_head(DEN), HH[:, :, :, P], -1.0, HH[:, :, :, P],
                                                     ALU.mult, ALU.max), *hh_ready)
        q = dve.run(lambda e: e.tensor_tensor(DEN, DEN, EM, ALU.max), q)
        den = dve.run(lambda e: e.reciprocal(DEN, DEN), q)
        for c in range(NT):
            for h in range(MH):
                col = 4 * c + h
                sc = dve.run(lambda e, c=c, h=h, col=col: e.tensor_scalar(HH[:, c, h, 0:P], HH[:, c, h, 0:P], DEN[:, col:col + 1],
                                                                          None, ALU.mult), den)
                ssq = act.run(lambda e, c=c, h=h, col=col: e.activation(JUNK[:, 0:P], HH[:, c, h, 0:P], ACT.Square,
                                                                        accum_out=SSM[:, col:col + 1]), sc, act.last())
        r = rstd(FAC, SSM, P, ssq)
        by = FAC.rearrange("p (c h) -> p c h", c=NT).unsqueeze(3).to_broadcast([P, NT, MH, P])
        normed = dve.run(lambda e: e.tensor_tensor(HH[:, :, :, 0:P], HH[:, :, :, 0:P], by, ALU.mult), r)
        YN = TOK[:, 0:2, :].rearrange("p a (b c) -> p (a b) c", b=2)
        YM = TOK[:, 2:4, :].rearrange("p a (b c) -> p (a b) c", b=2)
        ym_ready = []
        for h in range(MH):
            b, bank, free = banks.take()
            pe.wait(normed, *free)
            for c in range(NT):
                f = lambda e, c=c, h=h, bank=bank: e.transpose(bank[:, c * P:(c + 1) * P], HH[:, c, h, 0:P], IDENT)
                turned = pe.run(f) if c == NT - 1 else pe.more(f)
            g = VC[:, VEC["g_head"] + h:VEC["g_head"] + h + 1]
            ym_ready.append(dve.run(lambda e, h=h, bank=bank, g=g: e.scalar_tensor_tensor(
                YM[:, h, :], bank[:, :], g, SO[:, h, :], ALU.mult, ALU.mult), turned, so_ready[h]))
            banks.release(b, ym_ready[-1])

        quiet = [pe.last(), act.last(), dve.last()]
        act.wait(*quiet)
        dve.wait(*quiet)
        NQ = arena(0, 4, T)
        KC, VCM = arena(2048, T), arena(2560, T)
        KS, KW = arena(3072, T), arena(3584, T)
        VSW = arena(4096, NT, 256)
        XC = [arena(5120 + 1024 * j, CMP_BLOCK, 32) for j in range(2)]
        HID = arena(7168, 4, 32)
        KCC = arena(7296, 32)
        VCC = arena(7328, NG_, HD)
        e_slots = Slots([arena(8192 + 512 * i, T) for i in range(6)])
        p_slots = Slots([arena(11264 + 512 * i, T) for i in range(3)])
        YNT = arena(4096, 4, T)
        MIX = arena(14336, 8, T)

        kv_ready = {}

        def kv_sink(dsts, col):
            def sink(m, bank, token):
                c = VEC["b_kv"] + col + m
                kv_ready[col + m] = evacuate(dsts[m], bank[:, :], token, bias=VC[:, c:c + 1])
                return [kv_ready[col + m]]
            return sink
        project_features(w_in, C_NKV, 256, h_ready, kv_sink([KC, VCM], 0))
        blocks_ready = []
        for j, src in enumerate((KC, VCM)):
            windows = bass.AP(src.tensor, src.offset, [list(src.ap[0]), [1, CMP_BLOCK], [CMP_STRIDE, NCMP]])
            pos = PEC[:, CMP_BLOCK * j:CMP_BLOCK * (j + 1)].unsqueeze(2).to_broadcast([P, CMP_BLOCK, NCMP])
            blocks_ready.append(dve.run(lambda e, j=j, windows=windows, pos=pos: e.tensor_tensor(
                XC[j][:, :, 0:NCMP], windows, pos, ALU.add), kv_ready[j]))

        nq_ready = [None] * 4

        def nq_sink(m, bank, token):
            c = VEC["b_nq"] + m
            add = evacuate(NQ[:, m, :], bank[:, :], token, bias=VC[:, c:c + 1], engine=dve)
            nq_ready[m] = dve.run(lambda e: e.tensor_scalar(NQ[:, m, :], NQ[:, m, :], SCALE, None, ALU.mult), add)
            return [add]

        def nq_pieces(s):
            tiles = []
            for m in range(2):
                for g in range(NG_):
                    c0 = C_NQ + 256 * g + HD * (s // P + m)
                    tiles.append((slice(0, P), slice(P * m + HD * g, P * m + HD * (g + 1)),
                                  w_in[:, c0:c0 + HD].rearrange("(k p) c -> p k c", p=P)))
            return tiles
        project_features(w_in, C_NQ, 512, h_ready, nq_sink, pieces=nq_pieces)
        project_features(w_in, C_NKV + 256, 128, h_ready, kv_sink([KS], 2))
        project_features(w_in, C_NKV + 512, 128, h_ready, kv_sink([KW], 4))
        vs_ready = []

        def vs_sink(base):
            def sink(t, s, cols, bank, token):
                vs_ready.append(dve.run(lambda e: e.tensor_tensor(VSW[:, t, base:base + P], bank[:, 0:P],
                                                                  BVR[:, 512 + base:512 + base + P], ALU.add), token))
                return [vs_ready[-1]]
            return sink
        project_tokens(w_in, C_NKV + 384, 128, h_ready, vs_sink(0))
        project_tokens(w_in, C_NKV + 640, 128, h_ready, vs_sink(P))

        hid_ready = {}
        for j in range(2):
            taken = [banks.take() for _ in range(NG_)]
            for part in range(2):
                w1 = a["w_cmp1_2"][0, j].rearrange("(l d) h -> d l h", d=HD)[:, 16 * part:16 * part + 16, :]
                i, view, arrived = weights(16, [(slice(0, HD), slice(0, P), w1), (slice(HD, P), slice(0, P), w1)])
                for l in range(16):
                    for g in range(NG_):
                        b, bank, free = taken[g]
                        r = slice(HD * g, HD * (g + 1))
                        ll = 16 * part + l
                        f = lambda e, j=j, view=view, l=l, ll=ll, bank=bank, r=r: e.matmul(
                            bank[:, 0:NCMP], view[r, l, :], XC[j][r, ll, 0:NCMP], start=(ll == 0), stop=(ll == CMP_BLOCK - 1))
                        if l == 15:
                            token = pe.run(f)
                            if part == 1:
                                hid_ready[j, g] = act.run(lambda e, j=j, g=g, bank=bank: e.activation(
                                    HID[:, 2 * j + g, 0:NCMP], bank[:, 0:NCMP], ACT.Silu), token)
                                banks.release(b, hid_ready[j, g])
                        else:
                            pe.more(f, arrived, blocks_ready[j], *(free if ll == 0 else []))
                ring.release(i, token)
        cmp_ready = []
        for g in range(NG_):
            r = slice(HD * g, HD * (g + 1))
            b, bank, free = banks.take()
            w2 = W2C[:, 0:2, :].rearrange("p a d -> p (a d)")
            k2 = pe.run(lambda e, g=g, bank=bank, w2=w2: e.matmul(bank[:, 0:NCMP], w2, HID[:, g, 0:NCMP], start=True, stop=True),
                        hid_ready[0, g], *free)
            cmp_ready.append(dve.run(lambda e, r=r, bank=bank: e.tensor_copy(KCC[r, 0:NCMP], bank[r, 0:NCMP]), k2))
            banks.release(b, cmp_ready[-1])
            b, bank, free = banks.take()
            v2 = pe.run(lambda e, g=g, bank=bank: e.matmul(bank[0:NCMP, 0:HD], HID[:, 2 + g, 0:NCMP], W2C[:, 2, :], start=True, stop=True),
                        hid_ready[1, g], *free)
            cmp_ready.append(dve.run(lambda e, g=g, bank=bank: e.tensor_copy(VCC[0:NCMP, g, :], bank[0:NCMP, 0:HD]), v2))
            banks.release(b, cmp_ready[-1])

        yn_ready = {}
        units = []

        def branch_finish(h, t, first):
            def finish(u, bank, token):
                dst = YN[:, t, h * HD:(h + 1) * HD]
                if first:
                    f = lambda e: e.tensor_scalar(dst, bank[:, 0:HD], u.scalar, None, ALU.mult)
                else:
                    f = lambda e: e.scalar_tensor_tensor(dst, bank[:, 0:HD], u.scalar, dst, ALU.mult, ALU.add)
                yn_ready[h, t] = dve.run(f, token, u.norm, yn_ready.get((h, t)))
                return [yn_ready[h, t]]
            return finish

        for h in range(NH):
            g, rr = h // NR, h % NR
            r = slice(HD * g, HD * (g + 1))
            for t in range(NT):
                qt = NQ[r, rr, t * P:(t + 1) * P]
                w = (t + 1) * P
                nc_ = 8 * t + 7
                at = 384 + CMP_BLOCK - 1 - P * t
                strip = BIAS[:, h, at:at + CMP_STRIDE * (nc_ - 1) + 1:CMP_STRIDE]
                gate = lambda br, t=t, h=h: NGT[:, t, 3 * h + br:3 * h + br + 1]
                common = dict(coef_ready=ng_ready, bias_ready=[strips_ready], mask=False, nv=HD)
                units.append(Unit(w=nc_, maps=[(qt, KCC[r, 0:nc_])], ready=[*nq_ready, *cmp_ready], bias=strip, floor=1e29,
                                  coef=gate(0), v=lambda j, nc_=nc_, g=g: VCC[0:nc_, g, :], v_ready=cmp_ready,
                                  finish=branch_finish(h, t, True), **common))
                for br, keys, base in ((1, KS, 0), (2, KW, P)):
                    units.append(Unit(w=w, maps=[(qt, keys[r, 0:w])], ready=[*nq_ready, kv_ready[2 * br]],
                                      bias=BIAS[:, h, 384 - P * t:T], coef=gate(br),
                                      v=lambda j, g=g, base=base: VSW[:, j, base + HD * g:base + HD * (g + 1)],
                                      v_ready=vs_ready, finish=branch_finish(h, t, False), **common))
        attend(units, e_slots, p_slots)
        yn_t = turn_tokens(lambda t, k: YN[:, t, k * P:(k + 1) * P], lambda k: None, [dve.last()], range(4), YNT)

        gate_buf = Slots([arena(512 * i, T) for i in range(4)])
        act.wait(pe.last())
        dve.wait(pe.last())
        mix_ready = []
        for s in range(0, D, 256):
            gi = [slab(w_in, C_MERGE + D * n + s, C_MERGE + D * n + s + 256) for n in range(2)]
            bi = [slab(a["w_branch_2"][0, n], s, s + 256, 0, 4) for n in range(2)]
            for m in range(2):
                d = s // P + m
                parts = []
                for n in range(2):
                    b, bank, free = banks.take()
                    tok = matmuls(bank[:, :], [(gi[n][1][:, k, m * P:(m + 1) * P], HT[:, k, :]) for k in range(ND)],
                                  gi[n][2], *free)
                    si, sg, sfree = gate_buf.take()
                    c = VEC["b_merge"] + ND * n + d
                    sig = act.run(lambda e, sg=sg, bank=bank, c=c: e.activation(sg, bank[:, :], ACT.Sigmoid, bias=VC[:, c:c + 1]),
                                  tok, *sfree)
                    banks.release(b, sig)
                    b, bank, free = banks.take()
                    y, y_tok = (YM, ym_ready) if n == 0 else (YNT, yn_t)
                    tok2 = matmuls(bank[:, :], [(bi[n][1][:, k, m * P:(m + 1) * P], y[:, k, :]) for k in range(4)],
                                   bi[n][2], *y_tok, *free)
                    pr = dve.run(lambda e, sg=sg, bank=bank: e.tensor_tensor(sg, bank[:, :], sg, ALU.mult), tok2, sig)
                    banks.release(b, pr)
                    parts.append((si, sg, pr))
                mix_ready.append(dve.run(lambda e, d=d, p=parts: e.tensor_tensor(MIX[:, d, :], p[0][1], p[1][1], ALU.add),
                                         parts[0][2], parts[1][2]))
                for si, _, _ in parts:
                    gate_buf.release(si, mix_ready[-1])
            for x in gi:
                ring.release(x[0], tok2)
            for x in bi:
                ring.release(x[0], tok2)

        def residual_sink(x_tokens):
            def sink(half, t, bank, token):
                dst = X[:, t, half * 512:(half + 1) * 512]
                x_tokens[t] = dve.run(lambda e: e.tensor_tensor(dst, bank[:, :], dst, ALU.add), token)
                return [x_tokens[t]]
            return sink
        product_tokens(lambda k: MIX[:, k, :], ND, a["w_out_2"][0], mix_ready, residual_sink(x_tokens))
        h_ready = pre_norm(x_tokens, VEC["ffn2_pre"])
        g_row = gain_row(a["g_final_2"])
        feed_forward(a["w_gate_2"][0], a["w_up_2"][0], a["w_down_2"][0], h_ready, residual_sink(x_tokens))

        out_done = [sem("out_stored"), 0]
        for t in range(NT):
            sq = act.run(lambda e, t=t: e.activation(TOK[:, t, :], X[:, t, :], ACT.Square, accum_out=NST[:, t:t + 1]), x_tokens[t])
            r = rstd(NST[:, 4 + t:5 + t], NST[:, t:t + 1], D, sq)
            f = dve.run(lambda e, t=t: e.scalar_tensor_tensor(TOK[:, t, :], X[:, t, :], NST[:, 4 + t:5 + t], GROW[:, :],
                                                              ALU.mult, ALU.mult), r, g_row)
            stored = sync.dma(out[0, t * P:(t + 1) * P, :], TOK[:, t, :], out_done, f)
        sync.wait(stored, decay_written, rev_written)


_INS = ['x', 'positions', 'attn_pre_g', 'w_in', 'forget_bias', 'lam_q1', 'lam_k1', 'lam_q2', 'lam_k2', 'diff_sub_g',
        'w_out', 'attn_post_g', 'ffn_pre_g', 'w_gate', 'w_up', 'w_down', 'ffn_post_g', 'g_norm_mix_2', 'w_in_2',
        'b_in_2', 'b_fgate_2', 'conv_qk_2', 'g_mlstm_head_2', 'pe_cmp_2', 'w_cmp1_2', 'w_cmp2_2', 'rel_bias_2',
        'w_branch_2', 'w_out_2', 'g_norm_ffn_2', 'w_gate_2', 'w_up_2', 'w_down_2', 'g_final_2']


def kernel(**inputs):
    import numpy as _np
    import concourse.bacc as _bacc
    from concourse import mybir as _mybir
    from concourse.bass_utils import run_bass_kernel_spmd as _run

    nc = _bacc.Bacc("TRN2", target_bir_lowering=False, num_devices=1)
    arrays, args = {}, {}
    given = {name: inputs[name] for name in _INS}
    given["shape_constants"] = shape_constants()
    for name, value in given.items():
        v = _np.ascontiguousarray(value)
        if name.startswith("g_final"):
            v = v.reshape(-1)
        arrays[f"in_{name}_dram"] = v
        args[name] = nc.dram_tensor(f"in_{name}_dram", v.shape, _mybir.dt.from_np(v.dtype), kind="ExternalInput").ap()
    result = nc.dram_tensor("out_0_dram", (1, T, D), F32, kind="ExternalOutput").ap()
    program(nc, args, result)
    r = _run(nc, [arrays], core_ids=[0])
    return r.results[0]["out_0_dram"]
```

```python
from contextlib import ExitStack
import math

import numpy as np
import concourse.bass as bass
from concourse import mybir

F32 = mybir.dt.float32
F32R = mybir.dt.float32r
BF16 = mybir.dt.bfloat16
I32 = mybir.dt.int32
ALU = mybir.AluOpType
ACT = mybir.ActivationFunctionType
AX = mybir.AxisListType.X

P = 128
D = 1024
T = 512
NT = T // P
ND = D // P
DFF = 2816
NF = DFF // P
LAYERS = 2
HD = 64
NEG = -1e30
EPS = 1e-6
BIG = 3e38
SCALE = HD ** -0.5

C_QA, C_KA, C_VA, C_QB, C_KB, C_VB, C_F = [512 * i for i in range(7)]
N_DIFF, N_FOX = 4, 8
C_MQ, C_MK, C_MV, C_MO, C_IF, C_NQ, C_NKV, C_NG, C_MERGE = 0, 512, 1024, 1536, 2048, 2056, 2568, 3336, 3360
MH = 4
NH, NG_, NR = 8, 2, 4
CMP_BLOCK, CMP_STRIDE = 32, 16
NCMP = (T - CMP_BLOCK) // CMP_STRIDE + 1
BUCKETS = 32
CONV = 4
REV = 640
RAW_SLOTS = 4
TAIL = 2
PAIR_SLOTS = 3
SLAB = 1024
NCHUNK = 2
NFC = NF // NCHUNK
ARENA_WORDS = 16896

VEC = {}
_at = 0
for _name, _n in (("attn_pre", 16), ("ffn_pre", 16), ("mix_pre", 8), ("ffn2_pre", 8), ("diff_sub", 2),
                  ("b_qk", 8), ("b_mo", 4), ("b_nq", 4), ("b_kv", 6), ("b_merge", 16), ("g_head", 4),
                  ("conv", 32)):
    VEC[_name] = _at
    _at += _n
NVEC = _at

K_ID, K_ROT, K_TRI, K_MASK, K_FREQ, K_HOT = 0, 128, 256, 768, 896, 897
NCONST = 897
NTABLE = K_HOT + T


def shape_constants():
    c = np.zeros((P, NTABLE), np.float32)
    c[:, K_ID:K_ID + P] = np.eye(P)
    for m in range(P):
        if m % HD < 8:
            c[m + 8, K_ROT + m] = -1.0
        elif m % HD < 16:
            c[m - 8, K_ROT + m] = 1.0
    k = np.arange(P)[:, None]
    c[:, K_TRI:K_TRI + T] = np.arange(T)[None, :] >= k
    c[:, K_MASK:K_MASK + P] = np.where(np.arange(P)[None, :] > k, NEG, 0.0)
    dist = (T - 1 - np.arange(T)).astype(np.int64)
    nf = np.maximum(dist, 1).astype(np.float32)
    large = 16 + (np.log(nf / np.float32(16)) / np.float32(math.log(64)) * np.float32(16)).astype(np.int32)
    bucket = np.where(dist < 16, dist, np.minimum(large, BUCKETS - 1))
    c[:BUCKETS, K_HOT:K_HOT + T] = bucket[None, :] == np.arange(BUCKETS)[:, None]
    freq = (1.0 / np.power(np.float32(500000.0), np.arange(0, 16, 2, dtype=np.float32) / 16)).astype(np.float32)
    for m in range(P):
        if m % HD < 16:
            c[m, K_FREQ] = freq[m % 8]
    return c


class Queue:

    def __init__(self, engine, semaphore):
        self.engine, self.semaphore, self.count, self.passed = engine, semaphore, 0, {}

    def wait(self, *tokens):
        for token in tokens:
            if token is None:
                continue
            if isinstance(token, list):
                self.wait(*token)
                continue
            semaphore, value = token
            if self.passed.get(semaphore.name, 0) < value:
                self.passed[semaphore.name] = value
                self.engine.wait_ge(semaphore, value)

    def run(self, make, *after):
        self.wait(*after)
        self.count += 1
        make(self.engine).then_inc(self.semaphore, 1)
        return (self.semaphore, self.count)

    def more(self, make, *after):
        self.wait(*after)
        make(self.engine)

    def dma(self, out, in_, arrival, *after):
        self.wait(*after)
        arrival[1] += 16
        self.engine.dma_start(out, in_).then_inc(arrival[0], 16)
        return (arrival[0], arrival[1])

    def last(self):
        return (self.semaphore, self.count) if self.count else None


class Slots:

    def __init__(self, buffers):
        self.buffers, self.turn, self.free = buffers, 0, [[] for _ in buffers]

    def take(self):
        i = self.turn
        self.turn = (i + 1) % len(self.buffers)
        assert self.free[i] is not None, "buffer taken again before its readers were named"
        readers, self.free[i] = self.free[i], None
        return i, self.buffers[i], readers

    def release(self, i, *readers):
        self.free[i] = list(readers)


def program(nc, a, out):
    ctx = ExitStack()
    with ctx:
        def sb(name, shape, dt=F32):
            return ctx.enter_context(nc.sbuf_tensor(name, shape, dt))

        def sem(name):
            return ctx.enter_context(nc.semaphore(name))

        X = sb("x_residual", [P, NT, D])
        HT = sb("h_features", [P, 2, ND, T], F32R)
        TOK = sb("token_scratch", [P, NT, D])
        arena_at = -(-nc.sbuf_base // 32) * 32
        ARENA = sb("arena", [P, ARENA_WORDS])
        HIDDEN = nc.alloc_sbuf_tensor_at("hidden", [P, 2, NFC, T], F32R, offset=arena_at)
        YM = nc.alloc_sbuf_tensor_at("mlstm_features", [P, 2, 4, T], F32R, offset=arena_at + 4 * 12800)
        YNT = nc.alloc_sbuf_tensor_at("nsa_features", [P, 2, 4, T], F32R, offset=arena_at)
        MIX = nc.alloc_sbuf_tensor_at("mixed_features", [P, 2, ND, T], F32R, offset=arena_at + 4 * 4096)
        BIAS = [sb(f"bias_rows{i}", [P, T]) for i in range(3)]
        RAW = [sb(f"weights{i}", [P, SLAB]) for i in range(RAW_SLOTS)]
        PAIRS = [sb(f"weights_hi_lo{i}", [P, 2, SLAB], F32R) for i in range(PAIR_SLOTS)]
        GROW = sb("gain_row", [P, D])
        COS = sb("cos_table", [P, T])
        SIN = sb("sin_table", [P, T])
        CST = sb("shape_consts", [P, NCONST])
        VC = sb("vector_columns", [P, NVEC])
        PEC = sb("position_columns", [P, 2 * CMP_BLOCK])
        IDB = sb("identity_bf16", [P, P], BF16)
        MKB = sb("mask_bf16", [P, P], BF16)
        ONES = sb("ones", [P, P])
        EPSC = sb("eps_column", [P, 1])
        DIAG = sb("diag_rstd", [P, NT, P])
        STAT = sb("row_stats", [P, 16, 8])
        NST = sb("norm_stats", [P, 64])
        NLAM = sb("neg_lambda", [P, 16])
        FBI = sb("forget_bias_columns", [N_FOX, LAYERS])
        JUNK = sb("junk", [P, T])
        NEGC = sb("neg_decay", [8, T])
        BVR = sb("value_bias_rows", [P, 800])
        SM = sb("small_tok", [P, 600])
        PSUM = [ctx.enter_context(nc.psum_tensor(f"bank{i}", [P, T], F32)) for i in range(8)]
        tok_done = [[] for _ in range(NT)]
        diag_read = [None] * NT
        decay_dram = nc.dram_tensor("decay_scratch", [LAYERS, N_FOX, T], F32).ap()
        strip_dram = nc.dram_tensor("bias_scratch", [NH, P, T], F32).ap()

        pe = Queue(nc.tensor, sem("pe_done"))
        act = Queue(nc.scalar, sem("act_done"))
        dve = Queue(nc.vector, sem("dve_done"))
        pool = Queue(nc.gpsimd, sem("pool_done"))
        sync = Queue(nc.sync, sem("sync_done"))
        raw_arrival = [[sem(f"weights{i}_arrival"), 0] for i in range(RAW_SLOTS)]
        raw_slots = Slots(list(range(RAW_SLOTS)))
        pair_slots = Slots(PAIRS)
        bias_slots = Slots(BIAS)
        bias_in = [[sem(f"bias_rows{i}_arrival"), 0] for i in range(3)]
        banks = Slots(PSUM)
        IDENT = CST[:, K_ID:K_ID + P]
        TRI = CST[:, K_TRI:K_TRI + T]
        MASK = CST[:, K_MASK:K_MASK + P]
        stat = Slots([STAT[:, i, :] for i in range(16)])

        def arena(at, *shape):
            n = int(np.prod(shape))
            assert at + n <= ARENA_WORDS
            v = ARENA[:, at:at + n]
            if len(shape) == 2:
                return v.rearrange("p (a b) -> p a b", a=shape[0])
            if len(shape) == 3:
                return v.rearrange("p (a b c) -> p a b c", a=shape[0], b=shape[1])
            return v

        const_in = [sem("consts_arrival"), 0]
        x_in = [[sem(f"x{t}_arrival"), 0] for t in range(NT)]
        vec_in = [sem("vectors_arrival"), 0]
        row_in = [sem("rows_arrival"), 0]
        gain_in = [sem("gain_row_arrival"), 0]

        x_ready = [sync.dma(X[:, t, :], a["x"][0, t * P:(t + 1) * P, :], x_in[t]) for t in range(NT)]
        pool.dma(CST[:, :], a["shape_constants"][:, 0:NCONST], const_in)
        HOT = arena(12288, T)[0:BUCKETS]
        consts = pool.dma(HOT, a["shape_constants"][0:BUCKETS, K_HOT:NTABLE], const_in)

        LAM = arena(10240, 4 * LAYERS * HD).rearrange("p (a l d) -> p a l d", a=4, l=LAYERS)
        ROWS = arena(0, P)
        PER = arena(128, P)

        def rows(name, src, at=0, cols=None):
            r = VEC[name] + at
            n = src.shape[0]
            dst = ARENA[r:r + n, 0:P] if cols is None else ARENA[r:r + n, cols[0]:cols[1]]
            return pool.dma(dst, src, vec_in)

        def tiles_of(v):
            return v.rearrange("l (k p) -> (l k) p", p=P)

        def row_tiles(v):
            return v.rearrange("(k p) -> k p", p=P)

        b_in = a["b_in_2"][0]
        rows("attn_pre", tiles_of(a["attn_pre_g"]))
        rows("ffn_pre", tiles_of(a["ffn_pre_g"]))
        rows("mix_pre", tiles_of(a["g_norm_mix_2"]))
        rows("ffn2_pre", tiles_of(a["g_norm_ffn_2"]))
        rows("diff_sub", a["diff_sub_g"])
        rows("b_qk", row_tiles(b_in[C_MQ:C_MV]))
        rows("b_mo", row_tiles(b_in[C_MO:C_IF]))
        for g in range(NG_):
            rows("b_nq", b_in[C_NQ + 256 * g:C_NQ + 256 * (g + 1)].rearrange("(r d) -> r d", d=HD),
                 cols=(HD * g, HD * (g + 1)))
        rows("b_kv", row_tiles(b_in[C_NKV:C_NG]))
        rows("b_merge", row_tiles(b_in[C_MERGE:C_MERGE + 2 * D]))
        rows("g_head", tiles_of(a["g_mlstm_head_2"]))
        rows("conv", a["conv_qk_2"][0].rearrange("j (k p) -> (j k) p", p=P))
        for g in range(2):
            vectors = pool.dma(ARENA[0:2 * CMP_BLOCK, P + HD * g:P + HD * (g + 1)],
                               a["pe_cmp_2"][0].rearrange("j l d -> (j l) d"), vec_in)
        for i, name in enumerate(("lam_q1", "lam_q2", "lam_k1", "lam_k2")):
            pool.dma(LAM[:, i, :, :], a[name].partition_broadcast(P), row_in)
        for l in range(LAYERS):
            pool.dma(FBI[:, l:l + 1], a["forget_bias"][l].unsqueeze(1), row_in)
        pool.dma(BVR[:, 0:512], b_in[C_MV:C_MO].partition_broadcast(P), row_in)
        pool.dma(BVR[:, 512:640], b_in[C_NKV + 384:C_NKV + 512].partition_broadcast(P), row_in)
        pool.dma(BVR[:, 640:768], b_in[C_NKV + 640:C_NKV + 768].partition_broadcast(P), row_in)
        pool.dma(BVR[:, 768:776], b_in[C_IF:C_NQ].partition_broadcast(P), row_in)
        pool.dma(BVR[:, 776:800], b_in[C_NG:C_MERGE].partition_broadcast(P), row_in)
        BFG = NLAM[:, 8:12]
        pool.dma(BFG, a["b_fgate_2"][0].partition_broadcast(P), row_in)
        POSI = arena(8192, T).bitcast(I32)
        pool.dma(POSI, a["positions"][0].partition_broadcast(P), row_in)
        W2C = sb("w_cmp2_sb", [P, 3, HD])
        for slot, j in ((0, 0), (1, 0), (2, 1)):
            pool.dma(W2C[:, slot, :], a["w_cmp2_2"][0, j], row_in)
        RELB = sb("rel_bias_sb", [BUCKETS, NH])
        row_vectors = pool.dma(RELB[:, :], a["rel_bias_2"], row_in)

        ones_ready = dve.run(lambda e: e.memset(ONES[:, :], 1.0))
        eps_ready = dve.run(lambda e: e.memset(EPSC[:, :], EPS))
        dve.run(lambda e: e.tensor_copy(IDB[:, :], IDENT), consts)
        bf_ready = dve.run(lambda e: e.tensor_copy(MKB[:, :], MASK))

        def plan_features(name, w, c0, width, kt=ND):
            return [((name, c0 + s), kt, P, True,
                     [(slice(0, P), slice(0, P), w[0:kt * P, c0 + s:c0 + s + P].rearrange("(k p) c -> p k c", p=P))])
                    for s in range(0, width, P)]

        def plan_tokens(name, w, columns, kt, k_start=0):
            width = sum(c1 - c0 for c0, c1 in columns)
            step, entries = SLAB // width, []
            for k in range(k_start, k_start + kt, step):
                n, pieces, at = min(step, k_start + kt - k), [], 0
                for c0, c1 in columns:
                    pieces.append((slice(0, P), slice(at, at + c1 - c0),
                                   w[k * P:(k + n) * P, c0:c1].rearrange("(k p) c -> p k c", p=P)))
                    at += c1 - c0
                entries.append(((name, columns[0][0], k), n, width, True, pieces))
            return entries

        def plan_pieces(name, w, columns):
            pieces, at = [], 0
            for c0, c1 in columns:
                pieces.append((slice(0, P), slice(at, at + c1 - c0), w[:, c0:c1].rearrange("(k p) c -> p k c", p=P)))
                at += c1 - c0
            return [((name, "pieces", columns[0][0]), ND, P, True, pieces)]

        def plan_ffn(name, wg, wu, wd):
            entries = []
            for c in range(NCHUNK):
                for f in range(NFC * c, NFC * (c + 1)):
                    entries += plan_features(name + " gate", wg, f * P, P) + plan_features(name + " up", wu, f * P, P)
                for half in range(2):
                    entries += plan_tokens(name + " down", wd, [(512 * half, 512 * half + 512)], NFC, NFC * c)
            return entries

        plan = []
        for layer in range(LAYERS):
            w = a["w_in"][layer]
            plan += plan_pieces("forget", w, [(C_F, C_F + N_FOX), (C_QB, C_QB + P - N_FOX)])
            plan += plan_features("qkv", w, C_QA, 1024)
            plan += plan_tokens("values", w, [(C_VA, C_VA + 512)], ND)
            plan += plan_features("qkv", w, C_QB, 1024)
            plan += plan_tokens("values", w, [(C_VB, C_VB + 512)], ND)
            for half in range(2):
                plan += plan_tokens("out", a["w_out"][layer], [(512 * half, 512 * half + 512)], ND)
            plan += plan_ffn("ffn", a["w_gate"][layer], a["w_up"][layer], a["w_down"][layer])
        w = a["w_in_2"][0]
        plan += plan_pieces("gates", w, [(C_IF, C_IF + 8), (C_NG, C_NG + P - 8)])
        plan += plan_features("qk", w, C_MQ, 1024)
        plan += plan_tokens("values", w, [(C_MV, C_MV + 512)], ND)
        plan += plan_features("output gate", w, C_MO, 512)
        plan += plan_features("nsa", w, C_NKV, 256)
        for m in range(4):
            plan += plan_pieces("nsa q", w, [(C_NQ + HD * m, C_NQ + HD * (m + 1)),
                                             (C_NQ + 256 + HD * m, C_NQ + 256 + HD * (m + 1))])
        plan += plan_features("nsa", w, C_NKV + 256, P)
        plan += plan_features("nsa", w, C_NKV + 512, P)
        plan += plan_tokens("nsa values", w, [(C_NKV + 384, C_NKV + 512), (C_NKV + 640, C_NKV + 768)], ND)
        for j in range(2):
            w1 = a["w_cmp1_2"][0, j].rearrange("(l d) h -> d l h", d=HD)
            for l in range(0, CMP_BLOCK, 8):
                plan.append((("compress", j, l), 8, P, False, [(slice(0, HD), slice(0, P), w1[:, l:l + 8, :]),
                                                               (slice(HD, P), slice(0, P), w1[:, l:l + 8, :])]))
        for d in range(ND):
            for n in range(2):
                plan += plan_features("merge", w, C_MERGE + D * n + d * P, P)
                plan += plan_features(f"branch{n}", a["w_branch_2"][0, n], d * P, P, 4)
        for half in range(2):
            plan += plan_tokens("out", a["w_out_2"][0], [(512 * half, 512 * half + 512)], ND)
        plan += plan_ffn("ffn", a["w_gate_2"][0], a["w_up_2"][0], a["w_down_2"][0])

        arrivals, splits = [], []

        def advance(using):
            while len(splits) < min(len(plan), using + PAIR_SLOTS):
                transfers()
                i, r, token, kt, width, split = arrivals[len(splits)]
                if split and pair_slots.free[pair_slots.turn] is None:
                    break
                if not split:
                    splits.append(None)
                    continue
                raw = RAW[r][:, 0:kt * width]
                j, pair, readers = pair_slots.take()
                hi, lo = pair[:, 0, 0:kt * width], pair[:, 1, 0:kt * width]
                h = act.run(lambda e: e.activation(hi, raw, ACT.Copy), token, *readers)
                l = dve.run(lambda e: e.tensor_tensor(lo, raw, hi.bitcast(F32), ALU.subtract), h)
                raw_slots.release(i, l)
                splits.append((j, hi.rearrange("p (k c) -> p k c", k=kt), lo.rearrange("p (k c) -> p k c", k=kt), l))
            transfers()

        def transfers():
            while len(arrivals) < len(plan) and raw_slots.free[raw_slots.turn] is not None:
                _, kt, width, split, pieces = plan[len(arrivals)]
                i, r, readers = raw_slots.take()
                view = RAW[r][:, 0:kt * width].rearrange("p (k c) -> p k c", k=kt)
                for parts, cols, src in pieces:
                    token = sync.dma(view[parts, :, cols], src, raw_arrival[r], *readers)
                arrivals.append((i, r, token, kt, width, split))

        used = [0]

        def slab(*key):
            i = used[0]
            assert plan[i][0] == key, (plan[i][0], key)
            used[0] += 1
            advance(i)
            return splits[i]

        def matmuls(out_ap, pairs, *after):
            pe.wait(*after)
            n = len(pairs)
            for j, (l, r) in enumerate(pairs):
                f = lambda e, l=l, r=r, j=j: e.matmul(out_ap, l, r, start=(j == 0), stop=(j == n - 1))
                token = pe.run(f) if j == n - 1 else pe.more(f)
            return token

        def matmuls3(out_ap, pairs, *after):
            return matmuls(out_ap, [x for (lh, ll), (rh, rl) in pairs for x in ((lh, rl), (ll, rh), (lh, rh))], *after)

        flip = [0]

        def evacuate(dst, src, *after, scale=None, bias=None, engine=None):
            flip[0] ^= 1
            q = engine or (dve if flip[0] else act)
            if q is dve:
                if scale is None and bias is None:
                    f = lambda e: e.tensor_copy(dst, src)
                elif bias is None:
                    f = lambda e: e.tensor_scalar(dst, src, scale, None, ALU.mult)
                elif scale is None:
                    f = lambda e: e.tensor_scalar(dst, src, bias, None, ALU.add)
                else:
                    f = lambda e: e.tensor_scalar(dst, src, scale, bias, ALU.mult, ALU.add)
            elif bias is None:
                f = lambda e: e.activation(dst, src, ACT.Copy, scale=1.0 if scale is None else scale)
            else:
                f = lambda e: e.activation(dst, src, ACT.Identity, bias=bias, scale=1.0 if scale is None else scale)
            return q.run(f, *after)

        def rstd(dst, ss, n, *after):
            ln = act.run(lambda e: e.activation(dst, ss, ACT.Ln, bias=EPSC[:, 0:1], scale=1.0 / n), eps_ready, *after)
            return act.run(lambda e: e.activation(dst, dst, ACT.Exp, scale=-0.5), ln)

        def log_exp_table():
            act.engine.preload_act_table_set("natural_log_exp_and_others")

        def split_pair(hi, lo, src, *after, engine=None):
            h = act.run(lambda e: e.activation(hi, src, ACT.Copy), *after)
            return (engine or dve).run(lambda e: e.tensor_tensor(lo, src, hi.bitcast(F32), ALU.subtract), h, *after)

        def evacuate_pair(hi, lo, bank, *after):
            h = act.run(lambda e: e.activation(hi, bank, ACT.Copy), *after)
            return dve.run(lambda e: e.tensor_tensor(lo, bank, hi.bitcast(F32), ALU.subtract), h)

        turn_slots = Slots([arena(15360 + 512 * i, T) for i in range(3)])

        def to_features(dest, t, k0, bank, token, gains=None):
            hi = dest[:, 0, k0:k0 + 4, t * P:(t + 1) * P]
            lo = dest[:, 1, k0:k0 + 4, t * P:(t + 1) * P]
            b4 = bank[:, :].rearrange("p (k n) -> p k n", k=4)
            if gains is None:
                h = act.run(lambda e: e.activation(hi, b4, ACT.Copy), token)
                return None, lambda: dve.run(lambda e: e.tensor_tensor(lo, b4, hi.bitcast(F32), ALU.subtract), h)
            i, tmp, free = turn_slots.take()
            tmp4 = tmp.rearrange("p (k n) -> p k n", k=4)
            scaled = dve.run(lambda e: e.tensor_tensor(tmp4, b4, gains, ALU.mult), token, *free)
            h = act.run(lambda e: e.activation(hi, tmp4, ACT.Copy), scaled)

            def rest():
                q = pool if k0 else dve
                done = q.run(lambda e: e.tensor_tensor(lo, tmp4, hi.bitcast(F32), ALU.subtract), h)
                turn_slots.release(i, done)
                return done
            return scaled, rest

        diags = [None] * NT

        def diag_of(t):
            diags[t] = row_norm(x_tokens[t], t)

        def turn(tiles, halves, operands, dest, gains, ready, finished=lambda t, token: None):
            done, rest = [], []

            def settle():
                b, left, f = rest.pop(0)
                token = f()
                if left is None:
                    banks.release(b, token)
                done.append(token)

            for t in range(tiles):
                for k0 in halves:
                    b, bank, free = banks.take()
                    pe.wait(*ready(t), *free)
                    for k in range(4):
                        f = lambda e: operands(e, bank[:, k * P:(k + 1) * P], t, k0 + k)
                        token = pe.run(f) if k == 3 else pe.more(f)
                    left, later = to_features(dest, t, k0, bank, token, gains(k0))
                    if left is not None:
                        banks.release(b, left)
                    rest.append((b, left, later))
                    if len(rest) > 1:
                        settle()
                finished(t, token)
                if t == 1:
                    advance(used[0])
            while rest:
                settle()
            return done

        def turn_tokens(source, tiles, kt, dest, ready, gains=lambda k0: None):
            return turn(tiles, range(0, kt, 4),
                        lambda e, out_ap, t, k: e.transpose(out_ap, source[:, t, k * P:(k + 1) * P], IDENT),
                        dest, gains, lambda t: [consts, *ready])

        def row_norm(x_token, t):
            squares = act.run(lambda e: e.activation(TOK[:, t, :], X[:, t, :], ACT.Square,
                                                     accum_out=NST[:, t:t + 1]), x_token, *tok_done[t])
            r = rstd(NST[:, 4 + t:5 + t], NST[:, t:t + 1], D, squares)
            return dve.run(lambda e: e.tensor_scalar(DIAG[:, t, :], IDENT, NST[:, 4 + t:5 + t], None, ALU.mult), r, consts,
                           diag_read[t])

        def pre_norm(diags, gain_col):
            def read(t, token):
                diag_read[t] = token
            return turn(NT, (0, 4),
                        lambda e, out_ap, t, k: e.matmul(out_ap, X[:, t, k * P:(k + 1) * P], DIAG[:, t, :], start=True, stop=True),
                        HT, lambda k0: VC[:, gain_col + k0:gain_col + k0 + 4].unsqueeze(2).to_broadcast([P, 4, P]),
                        lambda t: [diags[t]], read)

        def hi_lo(v, *index):
            return v[(slice(None), 0) + index], v[(slice(None), 1) + index]

        def feature_tile(key, source, ready, kt=ND, width=T):
            i, hi, lo, arrived = slab(*key)
            b, bank, free = banks.take()
            token = matmuls3(bank[:, :], [((hi[:, k, :], lo[:, k, :]), hi_lo(source, k, slice(None))) for k in range(kt)],
                             arrived, *ready, *free)
            pair_slots.release(i, token)
            return b, bank, token

        def project_features(name, c0, width, h_ready, sink):
            for s in range(0, width, P):
                b, bank, token = feature_tile((name, c0 + s), HT, h_ready)
                banks.release(b, *sink(s // P, bank, token))

        def project_tokens(name, c0, width, source, kt, ready, sink, k_start=0, tail=False):
            taken = [banks.take() for _ in range(NT)]
            step = SLAB // width
            starts = list(range(0, kt, step))
            together = min(len(starts), TAIL if tail else 1)
            groups = [[k0] for k0 in starts[:-together]] + [starts[-together:]]
            for group in groups:
                slabs = [slab(name, c0, k_start + k0) for k0 in group]
                for t in range(NT):
                    b, bank, free = taken[t]
                    toks = slice(t * P, (t + 1) * P)
                    for (i, hi, lo, arrived), k0 in zip(slabs, group):
                        for k in range(k0, min(k0 + step, kt)):
                            sh, sl = hi_lo(source, k, toks)
                            wh, wl = hi[:, k - k0, :], lo[:, k - k0, :]
                            pe.wait(arrived, *(ready if isinstance(ready, list) else ready(k)), *(free if k == 0 else []))
                            for j, (l, r) in enumerate(((sh, wl), (sl, wh), (sh, wh))):
                                first, last = k == 0 and j == 0, k == kt - 1 and j == 2
                                f = lambda e: e.matmul(bank[:, 0:width], l, r, start=first, stop=last)
                                ends = last or (t == NT - 1 and k == min(k0 + step, kt) - 1 and j == 2)
                                token = pe.run(f) if ends else pe.more(f)
                        if t == NT - 1:
                            pair_slots.release(i, token)
                    if group is groups[-1]:
                        readers = sink(t, b, bank, token)
                        if readers is not None:
                            banks.release(b, *readers)

        def gain_row(src):
            return pool.dma(GROW[:, :], src.partition_broadcast(P), gain_in, dve.last())

        def post_norm(g_row, x_tokens, added=None):
            rstd_ready, scaled = {}, {}

            def weigh(half, t, b, bank, token):
                cols = slice(half * 512, half * 512 + 512)
                dst, y = TOK[:, t, cols], bank[:, :]
                if added is not None:
                    y = dst
                    token = dve.run(lambda e: e.tensor_tensor(y, bank[:, :], y, ALU.add), token, added[half, t])
                    banks.release(b, token)
                ss = NST[:, 16 + 4 * half + t:17 + 4 * half + t]
                sq = act.run(lambda e: e.activation(JUNK[:, :], y, ACT.Square, accum_out=ss), token, act.last())
                if half == 0:
                    rstd_ready[t] = dve.run(lambda e: e.tensor_scalar(NST[:, 24 + t:25 + t], ss, 1.0 / D, EPS, ALU.mult, ALU.add), sq)
                else:
                    r = NST[:, 28 + t:29 + t]
                    ln = act.run(lambda e: e.activation(r, ss, ACT.Ln, bias=NST[:, 24 + t:25 + t], scale=1.0 / D),
                                 sq, rstd_ready[t])
                    rstd_ready[t] = act.run(lambda e: e.activation(r, r, ACT.Exp, scale=-0.5), ln)
                scaled[half, t] = dve.run(lambda e: e.tensor_tensor(dst, y, GROW[:, cols], ALU.mult), sq, g_row, *tok_done[t])
                if added is None:
                    banks.release(b, scaled[half, t])

            def update(t):
                x_tokens[t] = dve.run(lambda e: e.scalar_tensor_tensor(X[:, t, :], TOK[:, t, :], NST[:, 28 + t:29 + t], X[:, t, :],
                                                                       ALU.mult, ALU.add), rstd_ready[t], scaled[1, t])
                tok_done[t] = [x_tokens[t]]

            def sink(half, t, b, bank, token):
                weigh(half, t, b, bank, token)
                if half == 1:
                    if t >= 1:
                        update(t - 1)
                    if t >= 2:
                        diag_of(t - 2)
                    if t == NT - 1:
                        update(t)
                        diag_of(t - 1)
                        diag_of(t)
                return None
            return sink

        def residual(x_tokens, then=None):
            def sink(half, t, b, bank, token):
                dst = X[:, t, half * 512:half * 512 + 512]
                x_tokens[t] = dve.run(lambda e: e.tensor_tensor(dst, bank[:, :], dst, ALU.add), token)
                banks.release(b, x_tokens[t])
                if half == 1 and then is not None:
                    then(t)
                return None
            return sink

        def out_product(name, source, kt, ready, sink, k_start=0):
            for half in range(2):
                project_tokens(name, 512 * half, 512, source, kt, ready, lambda t, b, bank, token: sink(half, t, b, bank, token),
                               k_start, tail=half == 1)

        def feed_forward(h_ready, first_sink, last_sink):
            silu = Slots([arena(11264 + 512 * i, T) for i in range(2)])
            full = Slots([arena(12288 + 512 * i, T) for i in range(2)])
            quiet = [pe.last(), act.last(), dve.last(), pool.last()]
            act.wait(*quiet)
            dve.wait(*quiet)
            for c in range(NCHUNK):
                ready = []
                for f in range(NFC):
                    col = (c * NFC + f) * P
                    gb, gate, g_done = feature_tile(("ffn gate", col), HT, h_ready)
                    si, sg, sfree = silu.take()
                    gated = act.run(lambda e: e.activation(sg, gate[:, :], ACT.Silu), g_done, *sfree)
                    banks.release(gb, gated)
                    ub, up, u_done = feature_tile(("ffn up", col), HT, h_ready)
                    fi, fl, ffree = full.take()
                    prod = dve.run(lambda e: e.tensor_tensor(fl, up[:, :], sg, ALU.mult), u_done, gated, *ffree)
                    silu.release(si, prod)
                    banks.release(ub, prod)
                    hi, lo = hi_lo(HIDDEN, f, slice(None))
                    ready.append(split_pair(hi, lo, fl, prod))
                    full.release(fi, ready[-1])
                if c == NCHUNK - 1:
                    log_exp_table()
                out_product("ffn down", HIDDEN, NFC, lambda k: [ready[k]], last_sink if c == NCHUNK - 1 else first_sink,
                            NFC * c)

        def keep_first(kept):
            def sink(half, t, b, bank, token):
                kept[half, t] = evacuate(TOK[:, t, half * 512:half * 512 + 512], bank[:, :], token, *tok_done[t])
                banks.release(b, kept[half, t])
                return None
            return sink

        def attend(units, e_slots, p_slots):

            def scores(u):
                u.banks = []
                for l, r in u.maps:
                    b, bank, free = banks.take()
                    pe.wait(*u.ready, *free)
                    n = r.shape[1]
                    f = lambda e: e.matmul(bank[:, 0:n], l, r, start=True, stop=not u.mask)
                    if u.mask:
                        pe.more(f)
                        token = pe.run(lambda e, bank=bank: e.matmul(bank[:, u.w - P:u.w], IDB[:, :], MKB[:, :],
                                                                     start=False, stop=True), bf_ready)
                    else:
                        token = pe.run(f)
                    u.banks.append((b, bank, token))

            def soften(u):
                si, u.stat, sfree = stat.take()
                u.si, u.e = si, []
                for j, (b, bank, token) in enumerate(u.banks):
                    ei, e_, efree = e_slots.take()
                    nm, sm = u.stat[:, j:j + 1], u.stat[:, 2 + j:3 + j]
                    dst = e_[:, 0:u.w]
                    if u.bias is None:
                        mx = dve.run(lambda e, bank=bank, nm=nm: e.tensor_reduce(nm, bank[:, 0:u.w], AX, ALU.max, negate=True),
                                     token, *sfree)
                        ex = act.run(lambda e, bank=bank, nm=nm, sm=sm, dst=dst: e.activation(
                            dst, bank[:, 0:u.w], ACT.Exp, bias=nm, accum_out=sm), mx, *efree, *sfree)
                        banks.release(b, ex)
                    else:
                        mx = dve.run(lambda e, bank=bank, nm=nm, dst=dst: e.tensor_tensor_reduce(
                            dst, bank[:, 0:u.w], u.bias(), -1.0, u.floor, ALU.add, ALU.min, nm),
                            token, *sfree, *efree, *u.bias_ready())
                        if u.last_of_head is not None:
                            u.last_of_head(mx)
                        ex = act.run(lambda e, nm=nm, sm=sm, dst=dst: e.activation(
                            dst, dst, ACT.Exp, bias=nm, scale=-1.0, accum_out=sm), mx)
                        banks.release(b, mx)
                    u.e.append((ei, e_, ex))

            def mix(u):
                n = len(u.maps)
                rc = u.stat[:, 4:4 + n]
                u.rc = rc
                if u.coef is not None:
                    cf = u.stat[:, 6:7]
                    s1 = dve.run(lambda e: e.tensor_scalar(cf, u.stat[:, 2:3], 1e-30, None, ALU.max), u.e[0][2])
                    s2 = dve.run(lambda e: e.reciprocal(rc, cf), s1)
                    u.norm = dve.run(lambda e: e.tensor_tensor(cf, rc, u.coef, ALU.mult), s2, *u.coef_ready)
                    u.scalar = cf
                else:
                    u.norm = dve.run(lambda e: e.reciprocal(rc, u.stat[:, 2:2 + n]), *[x[2] for x in u.e])
                    u.scalar = rc
                u.p_ready = u.e[0][2]
                if n == 2:
                    (i0, e0, _), (i1, e1, _) = u.e
                    nl = u.stat[:, 6:7]
                    l = dve.run(lambda e: e.tensor_tensor(nl, u.stat[:, 5:6], u.neg_lambda, ALU.mult), u.norm)
                    s = act.run(lambda e: e.activation(e0[:, 0:u.w], e0[:, 0:u.w], ACT.Copy, scale=u.stat[:, 4:5]), u.norm)
                    u.p_ready = dve.run(lambda e: e.scalar_tensor_tensor(e0[:, 0:u.w], e1[:, 0:u.w], nl, e0[:, 0:u.w],
                                                                         ALU.mult, ALU.add), l, s)
                    e_slots.release(i1, u.p_ready)

            def turn(u):
                b, bank, free = banks.take()
                pe.wait(u.p_ready, *free)
                e0 = u.e[0][1]
                chunks = [(c, min(P, u.w - c)) for c in range(0, u.w, P)]
                for c, n in chunks:
                    f = lambda e, c=c, n=n: e.transpose(bank[0:n, c:c + P], e0[:, c:c + n], IDENT)
                    token = pe.run(f) if c + n == u.w else pe.more(f)
                e_slots.release(u.e[0][0], token)
                u.pi, u.pt, pfree = p_slots.take()
                n = chunks[0][1]
                w = len(chunks) * P
                u.pt_ready = evacuate(u.pt[0:n, 0:w], bank[0:n, 0:w], token, *pfree)
                banks.release(b, u.pt_ready)

            def values(u):
                b, bank, free = banks.take()
                pairs = []
                for j, c in enumerate(range(0, u.w, P)):
                    n = min(P, u.w - c)
                    pairs.append((u.pt[0:n, c:c + P], u.v(j)))
                token = matmuls(bank[:, 0:P], pairs, u.pt_ready, *u.v_ready, *free)
                p_slots.release(u.pi, token)
                tokens = u.finish(u, bank[:, u.at:u.at + u.nv], token)
                banks.release(b, *tokens)
                stat.release(u.si, *tokens)

            n = len(units)
            for i in range(n + 3):
                if i < n:
                    if units[i].start is not None:
                        units[i].start()
                    scores(units[i])
                    soften(units[i])
                if 1 <= i <= n:
                    mix(units[i - 1])
                if 2 <= i <= n + 1:
                    turn(units[i - 2])
                if i >= 3:
                    values(units[i - 3])

        class Unit:

            def __init__(self, w, nv, maps, ready, v, v_ready, finish, neg_lambda=None, bias=None, bias_ready=(),
                         floor=BIG, coef=None, coef_ready=(), mask=True, at=0, start=None, last_of_head=None):
                self.w, self.nv, self.maps, self.ready, self.v, self.v_ready = w, nv, maps, ready, v, v_ready
                self.finish, self.neg_lambda, self.bias, self.bias_ready = finish, neg_lambda, bias, bias_ready
                self.floor, self.coef, self.coef_ready, self.mask = floor, coef, coef_ready, mask
                self.at, self.start, self.last_of_head = at, start, last_of_head

        def log_sigmoid(dst, src, tmp, ready):
            m = dve.run(lambda e: e.tensor_scalar(dst, src, 0.0, None, ALU.min), ready)
            ab = dve.run(lambda e: e.scalar_tensor_tensor(tmp, src, -1.0, src, ALU.mult, ALU.max), ready)
            ex = act.run(lambda e: e.activation(tmp, tmp, ACT.Exp, scale=-1.0), ab)
            ln = act.run(lambda e: e.activation(tmp, tmp, ACT.Ln, bias=ONES[0:tmp.shape[0], 0:1]), ex, ones_ready)
            return dve.run(lambda e: e.tensor_tensor(dst, dst, tmp, ALU.subtract), ln, m)

        b, bank, free = banks.take()
        turned = pe.run(lambda e, bank=bank: e.transpose(bank[:, 0:NVEC], ROWS[0:NVEC, :], CST[0:NVEC, 0:NVEC]), consts, vectors)
        vc_ready = evacuate(VC[:, :], bank[:, 0:NVEC], turned, engine=dve)
        banks.release(b, vc_ready)
        b, bank, free = banks.take()
        turned = pe.run(lambda e, bank=bank: e.transpose(bank[:, 0:64], PER[0:64, :], CST[0:64, 0:64]))
        pec_ready = evacuate(PEC[:, :], bank[:, 0:64], turned, engine=dve)
        banks.release(b, pec_ready)
        lam_init = [0.8 - 0.6 * math.exp(-0.3 * l) for l in range(LAYERS)]
        for l in range(LAYERS):
            c = VEC["diff_sub"] + l
            vc_ready = dve.run(lambda e, c=c, l=l: e.tensor_scalar(VC[:, c:c + 1], VC[:, c:c + 1], 1.0 - lam_init[l],
                                                                   None, ALU.mult), vc_ready)
        act.wait(vc_ready)
        log_exp_table()
        h_ready = pre_norm([row_norm(x_ready[t], t) for t in range(NT)], VEC["attn_pre"])

        prod = dve.run(lambda e: e.tensor_tensor(LAM[:, 0:2, :, :], LAM[:, 0:2, :, :], LAM[:, 2:4, :, :], ALU.mult), row_vectors)
        dots = dve.run(lambda e: e.tensor_reduce(NLAM[:, 0:4], LAM[:, 0:2, :, :].rearrange("p a l d -> p (a l) d"),
                                                 AX, ALU.add), prod)
        exps = act.run(lambda e: e.activation(NLAM[:, 0:4], NLAM[:, 0:4], ACT.Exp), dots)
        diff = dve.run(lambda e: e.tensor_tensor(NLAM[:, 4:6], NLAM[:, 2:4], NLAM[:, 0:2], ALU.subtract), exps)
        for l in range(LAYERS):
            lam_ready = dve.run(lambda e, l=l: e.tensor_scalar(NLAM[:, 4 + l:5 + l], NLAM[:, 4 + l:5 + l], -lam_init[l],
                                                               None, ALU.add), diff)

        ang, turns_, arg = arena(8704, T), arena(9216, T), arena(9728, T)
        c2pi = [6.28125, 0.0019350051879882812, 3.019916050561733e-07]
        posf = dve.run(lambda e: e.tensor_copy(ang, POSI), row_vectors)
        angle = dve.run(lambda e: e.tensor_scalar(ang, ang, CST[:, K_FREQ:K_FREQ + 1], None, ALU.mult), posf, consts)
        for table, quarter in ((SIN, 0.0), (COS, 0.25)):
            q = dve.run(lambda e, quarter=quarter: e.tensor_scalar(turns_, ang, 1.0 / (2 * math.pi), quarter, ALU.mult, ALU.add),
                        angle, act.last(), dve.last())
            q = dve.run(lambda e: e.tensor_scalar(turns_, turns_, 12582912.0, None, ALU.add), q)
            q = dve.run(lambda e: e.tensor_scalar(turns_, turns_, -12582912.0, None, ALU.add), q)
            src = ang
            for c in c2pi:
                q = dve.run(lambda e, c=c, src=src: e.scalar_tensor_tensor(arg, turns_, -c, src, ALU.mult, ALU.add), q)
                src = arg
            q = dve.run(lambda e, quarter=quarter: e.tensor_scalar(arg, arg, quarter * 2 * math.pi, 3.1415925, ALU.add, ALU.min), q)
            q = dve.run(lambda e: e.tensor_scalar(arg, arg, -3.1415925, None, ALU.max), q)
            rope_ready = act.run(lambda e, table=table: e.activation(table[:, :], arg, ACT.Sin), q)

        rev_io = [sem("bias_scratch_io"), 0]
        strip_in = [sem("bias_strips_arrival"), 0]
        b, bank, free = banks.take()
        hot = matmuls(bank[0:NH, :], [(RELB[:, :], HOT)], row_vectors, consts, *free)
        REVB = ARENA[0:NH, 11264:11264 + REV]
        rv = dve.run(lambda e: e.tensor_copy(REVB[:, 0:T], bank[0:NH, :]), hot)
        banks.release(b, rv)
        rv2 = dve.run(lambda e: e.memset(REVB[:, T:REV], NEG))
        rows_of = REVB[:, P - 1:P - 1 + T]
        shifted = bass.AP(rows_of.tensor, rows_of.offset, [list(rows_of.ap[0]), [-1, P], [1, T]])
        rev_written = pool.dma(strip_dram, shifted, rev_io, rv, rv2)

        decay_io = [sem("decay_scratch_io"), 0]
        x_tokens = list(x_ready)
        act.wait(rope_ready)

        def bias_rows(src, written):
            state = [None, None]

            def start():
                i, buf, readers = bias_slots.take()
                state[0] = buf
                state[1] = [pool.dma(buf[:, :], src, bias_in[i], written, *readers)]
                state.append(i)
            return start, lambda: state[0], lambda: state[1], lambda token: bias_slots.release(state[2], token)

        for layer in range(LAYERS):
            QA, KA, QB, KB = (arena(2048 * i, 4, T) for i in range(4))
            V = arena(8192, NT, D)
            e_slots = Slots([arena(12288 + 512 * i, T) for i in range(6)])
            p_slots = Slots([arena(15360 + 512 * i, T) for i in range(3)])
            rope = Slots([arena(15360 + 512 * i, T) for i in range(3)])
            FG, FGT = arena(12288, 2, T)[0:N_FOX], arena(13312, NT * N_FOX)
            if layer:
                h_ready = pre_norm(diags, VEC["attn_pre"] + ND * layer)
            quiet = [pe.last(), act.last(), dve.last(), pool.last(), rev_written]
            act.wait(*quiet)
            dve.wait(*quiet)

            b, bank, token = feature_tile(("forget", "pieces", C_F), HT, h_ready)
            biased = dve.run(lambda e: e.tensor_scalar(FG[:, 0, :], bank[0:N_FOX, :], FBI[:, layer:layer + 1], None, ALU.add),
                             token, row_vectors)
            banks.release(b, biased)
            lf = log_sigmoid(NEGC[:, :], FG[:, 0, :], FG[:, 1, :], biased)
            qk_ready = {}

            def rotary_sink(dst, scale, key):
                pending = []

                def finish():
                    m, tmp, ri, copied = pending.pop(0)
                    b, bank, free = banks.take()
                    rot = matmuls(bank[:, :], [(CST[:, K_ROT:K_ROT + P], tmp)], copied, consts, *free)
                    straight = dve.run(lambda e: e.tensor_tensor(dst[:, m, :], tmp, COS[:, :], ALU.mult), copied, rope_ready)
                    crossed = dve.run(lambda e: e.tensor_tensor(tmp, bank[:, :], SIN[:, :], ALU.mult), rot, straight)
                    banks.release(b, crossed)
                    qk_ready[key, m] = dve.run(lambda e: e.tensor_tensor(dst[:, m, :], dst[:, m, :], tmp, ALU.add), crossed)
                    rope.release(ri, qk_ready[key, m])

                def sink(m, bank, token):
                    if pending:
                        finish()
                    ri, tmp, rfree = rope.take()
                    copied = evacuate(tmp, bank[:, :], token, *rfree, scale=scale, engine=act)
                    pending.append((m, tmp, ri, copied))
                    return [copied]
                return sink, finish

            sink, finish = rotary_sink(QA, SCALE, "qa")
            project_features("qkv", C_QA, 512, h_ready, sink)
            finish()
            b, bank, free = banks.take()
            pe.wait(lf, *free)
            for t in range(NT):
                f = lambda e: e.transpose(bank[:, N_FOX * t:N_FOX * (t + 1)], NEGC[:, t * P:(t + 1) * P],
                                          CST[0:N_FOX, 0:N_FOX])
                token = pe.run(f) if t == NT - 1 else pe.more(f)
            fgt = dve.run(lambda e: e.tensor_copy(FGT, bank[:, 0:NT * N_FOX]), token)
            banks.release(b, fgt)
            sink, finish = rotary_sink(KA, None, "ka")
            project_features("qkv", C_KA, 512, h_ready, sink)
            finish()
            b, bank, free = banks.take()
            pe.wait(fgt, *free)
            for s in range(NT):
                f = lambda e: e.matmul(bank[0:N_FOX, s * P:T], FGT[:, N_FOX * s:N_FOX * (s + 1)], TRI[:, 0:T - s * P],
                                       start=(s == 0), stop=(s == NT - 1))
                summed = pe.run(f) if s == NT - 1 else pe.more(f)
            nc_ready = dve.run(lambda e: e.tensor_scalar(NEGC[:, :], bank[0:N_FOX, :], -1.0, None, ALU.mult), summed)
            banks.release(b, nc_ready)
            decay_written = pool.dma(decay_dram[layer], NEGC[:, :], decay_io, nc_ready)

            v_ready = {}

            def value_sink(base):
                def sink(t, b, bank, token):
                    v_ready[t, base] = evacuate(V[:, t, base:base + 512], bank[:, :], token)
                    return [v_ready[t, base]]
                return sink
            project_tokens("values", C_VA, 512, HT, ND, h_ready, value_sink(0))

            def plain_sink(dst, scale, key):
                def sink(m, bank, token):
                    qk_ready[key, m] = evacuate(dst[:, m, :], bank[:, :], token, scale=scale)
                    return [qk_ready[key, m]]
                return sink
            project_features("qkv", C_QB, 512, h_ready, plain_sink(QB, SCALE, "qb"))
            project_features("qkv", C_KB, 512, h_ready, plain_sink(KB, None, "kb"))
            project_tokens("values", C_VB, 512, HT, ND, h_ready, value_sink(512))
            all_v = list(v_ready.values())
            dve.wait(act.last())

            SS = NST[:, 32:48]
            tok_free = [x for y in tok_done for x in y]
            squares = []

            def diff_finish(h, t):
                def finish(u, bank, token):
                    dst = TOK[:, t, h * P:(h + 1) * P]
                    copy = dve.run(lambda e: e.tensor_copy(dst, bank), token, *tok_free)
                    squares.append(act.run(lambda e: e.activation(JUNK[:, 0:P], dst, ACT.Square,
                                                                  accum_out=SS[:, 4 * t + h:4 * t + h + 1]), copy, act.last()))
                    return [copy]
                return finish

            fox_done = []

            def fox_finish(h, t):
                def finish(u, bank, token):
                    fox_done.append(dve.run(lambda e: e.tensor_scalar(TOK[:, t, 512 + h * HD:512 + (h + 1) * HD], bank,
                                                                      u.scalar, None, ALU.mult), token, u.norm, *tok_free))
                    return [fox_done[-1]]
                return finish

            units = []
            for h in range(N_DIFF):
                for t in range(NT):
                    w = (t + 1) * P
                    units.append(Unit(
                        w=w, nv=P, maps=[(QA[m * HD:(m + 1) * HD, h, t * P:w], KA[m * HD:(m + 1) * HD, h, 0:w]) for m in range(2)],
                        ready=[qk_ready["qa", h], qk_ready["ka", h]], neg_lambda=NLAM[:, 4 + layer:5 + layer],
                        v=lambda j, h=h: V[:, j, h * P:(h + 1) * P], v_ready=all_v, finish=diff_finish(h, t)))
            dve.wait(lam_ready)
            for h in range(N_FOX):
                m, r = h // 2, slice(HD * (h % 2), HD * (h % 2) + HD)
                start, row, row_ready, row_done = bias_rows(decay_dram[layer, h].partition_broadcast(P), decay_written)
                for t in range(NT):
                    w = (t + 1) * P
                    units.append(Unit(
                        w=w, nv=HD, maps=[(QB[r, m, t * P:w], KB[r, m, 0:w])], ready=[qk_ready["qb", m], qk_ready["kb", m]],
                        bias=lambda row=row, w=w: row()[:, 0:w], bias_ready=row_ready, start=start if t == 0 else None,
                        last_of_head=row_done if t == NT - 1 else None, at=HD * (h % 2),
                        v=lambda j, m=m: V[:, j, 512 + m * P:512 + (m + 1) * P], v_ready=all_v, finish=fox_finish(h, t)))
            attend(units, e_slots, p_slots)

            r = rstd(SS, SS, P, *squares)
            heads = TOK[:, :, 0:512].rearrange("p t (h e) -> p t h e", h=N_DIFF)
            by = SS.rearrange("p (t h) -> p t h", t=NT).unsqueeze(3).to_broadcast([P, NT, N_DIFF, P])
            normed = dve.run(lambda e: e.tensor_tensor(heads, heads, by, ALU.mult), r)
            c = VEC["diff_sub"] + layer
            g_row = gain_row(a["attn_post_g"][layer])
            m_ready = turn_tokens(TOK, NT, ND, HT, [normed, fox_done[-1]],
                                  lambda k0: VC[:, c:c + 1].unsqueeze(2).to_broadcast([P, 4, P]) if k0 < 4 else None)
            out_product("out", HT, ND, m_ready, post_norm(g_row, x_tokens))
            h_ready = pre_norm(diags, VEC["ffn_pre"] + ND * layer)
            g_row = gain_row(a["ffn_post_g"][layer])
            kept = {}
            feed_forward(h_ready, keep_first(kept), post_norm(g_row, x_tokens, kept))

        h_ready = pre_norm(diags, VEC["mix_pre"])
        quiet = [pe.last(), act.last(), dve.last(), pool.last()]
        act.wait(*quiet)
        dve.wait(*quiet)

        QK = arena(0, 8, T)
        VA = arena(4096, NT, MH, P + 1)
        SO = arena(6160, MH, T)
        KTOK = arena(8208, NT, MH, P)
        RM = arena(10256, NT, T)
        HH = TOK[:, :, :].rearrange("p a b -> p (a b)")[:, 0:NT * MH * (P + 1)].rearrange(
            "p (c h e) -> p c h e", c=NT, h=MH)
        DG = TOK[:, :, :].rearrange("p a b -> p (a b)")[:, 2048:4096].rearrange("p (c h e) -> p c h e", c=NT, h=MH)
        conv_in = Slots([arena(12304 + 516 * i, 516) for i in range(2)])
        conv_acc = Slots([arena(13336 + 512 * i, T) for i in range(2)])
        VW = Slots([arena(12304 + 129 * i, P + 1) for i in range(2)])
        CST8 = arena(12562, MH, P + 1)
        PM = Slots([arena(13078 + 128 * i, P) for i in range(3)])
        PTM = Slots([arena(13462 + 128 * i, P) for i in range(3)])
        O1 = Slots([arena(13846 + 129 * i, P + 1) for i in range(2)])

        GT32 = SM[:, 0:128].rearrange("p (t c) -> p t c", t=NT)
        IFG, NGT = GT32[:, :, 0:8], GT32[:, :, 8:32]
        b, bank, token = feature_tile(("gates", "pieces", C_IF), HT, h_ready)
        copied = dve.run(lambda e: e.tensor_copy(JUNK[0:32, :], bank[0:32, :]), token, act.last())
        banks.release(b, copied)

        qk_ready = [None] * 8

        def conv_sink(m, bank, token):
            ci, cin, cfree = conv_in.take()
            ai, acc, afree = conv_acc.take()
            pad = dve.run(lambda e: e.memset(cin[:, 0:CONV - 1], 0.0), *cfree)
            copied = act.run(lambda e: e.activation(cin[:, CONV - 1:CONV - 1 + T], bank[:, :], ACT.Identity,
                                                    bias=VC[:, VEC["b_qk"] + m:VEC["b_qk"] + m + 1]), token, *cfree)
            col = lambda j: VC[:, VEC["conv"] + 8 * j + m:VEC["conv"] + 8 * j + m + 1]
            s = dve.run(lambda e: e.tensor_scalar(acc, cin[:, 0:T], col(0), None, ALU.mult), copied, pad, *afree)
            for j in range(1, CONV):
                s = dve.run(lambda e: e.scalar_tensor_tensor(acc, cin[:, j:j + T], col(j), acc, ALU.mult, ALU.add), s)
            conv_in.release(ci, s)
            done = act.run(lambda e: e.activation(QK[:, m, :], acc, ACT.Silu), s)
            if m >= 4:
                done = dve.run(lambda e: e.tensor_scalar(QK[:, m, :], QK[:, m, :], P ** -0.5, None, ALU.mult), done)
            conv_acc.release(ai, done)
            qk_ready[m] = done
            return [copied]
        project_features("qk", C_MQ, 1024, h_ready, conv_sink)

        b, bank, free = banks.take()
        pe.wait(copied, *free)
        for t in range(NT):
            f = lambda e: e.transpose(bank[:, 32 * t:32 * t + 32], JUNK[0:32, t * P:(t + 1) * P], CST[0:32, 0:32])
            token = pe.run(f) if t == NT - 1 else pe.more(f)
        gates_tok = dve.run(lambda e: e.tensor_tensor(GT32, bank[:, 0:128].rearrange("p (t c) -> p t c", t=NT),
                                                      BVR[:, 768:800].unsqueeze(1).to_broadcast([P, NT, 32]), ALU.add), token)
        banks.release(b, gates_tok)
        LF, LS = SM[:, 128:144], SM[:, 144:160]
        fb = dve.run(lambda e: e.tensor_tensor(LF.rearrange("p (c h) -> p c h", c=NT), IFG[:, :, 4:8],
                                               BFG.unsqueeze(1).to_broadcast([P, NT, MH]), ALU.add), gates_tok)
        log_exp_table()
        lf_ready = log_sigmoid(LS, LF, SM[:, 160:176], fb)

        va_ones = dve.run(lambda e: e.memset(VA[:, :, :, P:P + 1], 1.0))
        va_ready = [[va_ones] for _ in range(NT)]

        def va_sink(t, b, bank, token):
            done = dve.run(lambda e: e.tensor_tensor(VA[:, t, :, 0:P], bank[:, :].rearrange("p (h e) -> p h e", h=MH),
                                                     BVR[:, 0:512].rearrange("p (h e) -> p h e", h=MH), ALU.add), token)
            va_ready[t].append(done)
            return [done]
        project_tokens("values", C_MV, 512, HT, ND, h_ready, va_sink)

        so_ready = [None] * MH

        def so_sink(m, bank, token):
            so_ready[m] = act.run(lambda e: e.activation(SO[:, m, :], bank[:, :], ACT.Sigmoid,
                                                         bias=VC[:, VEC["b_mo"] + m:VEC["b_mo"] + m + 1]), token)
            return [so_ready[m]]
        project_features("output gate", C_MO, 512, h_ready, so_sink)
        ng_ready = [act.run(lambda e: e.activation(NGT, NGT, ACT.Sigmoid), gates_tok)]
        log_exp_table()

        ktok_ready = []
        for c in range(NT):
            b, bank, free = banks.take()
            pe.wait(*free, *qk_ready[4:8])
            for h in range(MH):
                f = lambda e, c=c, h=h, bank=bank: e.transpose(bank[:, h * P:(h + 1) * P], QK[:, 4 + h, c * P:(c + 1) * P], IDENT)
                turned = pe.run(f) if h == MH - 1 else pe.more(f)
            ktok_ready.append(evacuate(KTOK[:, c, :, :].rearrange("p h e -> p (h e)"), bank[:, :], turned))
            banks.release(b, ktok_ready[-1])

        dve.wait(act.last())
        act.wait(dve.last())

        b, bank, free = banks.take()
        pe.more(lambda e, bank=bank: e.matmul(bank[:, 0:16], TRI[:, 0:P], LS, start=True, stop=True), lf_ready, *free)
        sums = pe.run(lambda e, bank=bank: e.matmul(bank[:, 16:32], ONES[:, :], LS, start=True, stop=True), ones_ready)
        BCBL = SM[:, 176:208]
        bc = dve.run(lambda e, bank=bank: e.tensor_copy(BCBL, bank[:, 0:32]), sums)
        banks.release(b, bc)
        BC, BL = BCBL[:, 0:16], BCBL[:, 16:32]
        R = SM[:, 208:224]
        r_ready = dve.run(lambda e: e.tensor_tensor(R.rearrange("p (c h) -> p c h", c=NT), IFG[:, :, 0:4],
                                                    BC.rearrange("p (c h) -> p c h", c=NT), ALU.subtract), bc)
        MR, RX = SM[:, 224:240], SM[:, 240:256]
        rm_ready, diags = [], []
        for c in range(NT):
            for h in range(MH):
                d = dve.run(lambda e, c=c, h=h: e.tensor_scalar(DG[:, c, h, :], IDENT, R[:, 4 * c + h:4 * c + h + 1],
                                                                None, ALU.mult), r_ready)
            diags.append(d)
        for c in range(NT):
            b, bank, free = banks.take()
            spread = matmuls(bank[:, :], [(ONES[:, :], DG[:, c, :, :].rearrange("p h e -> p (h e)"))], diags[c], *free)
            b3 = bank[:, :].rearrange("p (h e) -> p h e", h=MH)
            r3 = RM[:, c, :].rearrange("p (h e) -> p h e", h=MH)
            whole = dve.run(lambda e, c=c, b3=b3: e.tensor_reduce(RX[:, 4 * c:4 * c + 4], b3, AX, ALU.max), spread)
            masked = dve.run(lambda e, b3=b3, r3=r3: e.tensor_tensor(r3, b3, MASK.unsqueeze(1).to_broadcast([P, MH, P]), ALU.add), spread)
            banks.release(b, masked)
            rm_ready.append(dve.run(lambda e, c=c, r3=r3: e.tensor_reduce(MR[:, 4 * c:4 * c + 4], r3, AX, ALU.max), masked))
        MP, MX = SM[:, 256:276], SM[:, 276:292]
        step = dve.run(lambda e: e.memset(MP[:, 0:4], 0.0))
        for c in range(NT):
            s = slice(4 * c, 4 * c + 4)
            mx = dve.run(lambda e, s=s: e.tensor_tensor(MX[:, s], MP[:, s], RX[:, s], ALU.max), step, rm_ready[c])
            step = dve.run(lambda e, s=s, c=c: e.tensor_tensor(MP[:, 4 * c + 4:4 * c + 8], BL[:, s], MX[:, s], ALU.add), mx)
        NM2, SI, EM, WK, DC = (SM[:, 292 + 16 * i:308 + 16 * i] for i in range(5))
        q = dve.run(lambda e: e.tensor_tensor(NM2, MR, MP[:, 0:16], ALU.max), step)
        q = dve.run(lambda e: e.tensor_scalar(NM2, NM2, -1.0, None, ALU.mult), q)
        q1 = dve.run(lambda e: e.tensor_tensor(SI, MP[:, 0:16], NM2, ALU.add), q)
        q2 = dve.run(lambda e: e.tensor_tensor(EM, NM2, BC, ALU.subtract), q)
        q3 = dve.run(lambda e: e.tensor_tensor(WK, R, MX, ALU.subtract), step)
        q4 = dve.run(lambda e: e.tensor_tensor(DC, MP[:, 0:16], MX, ALU.subtract), step)
        gates_ready = act.run(lambda e: e.activation(SM[:, 308:372], SM[:, 308:372], ACT.Exp), q1, q2, q3, q4)
        dve.wait(gates_ready)

        hh_ready = []
        c_ready = [None] * MH
        for c in range(NT):
            for h in range(MH):
                col = 4 * c + h
                q_ = QK[:, h, c * P:(c + 1) * P]
                b, bank, free = banks.take()
                s_tok = matmuls(bank[:, 0:P], [(q_, QK[:, 4 + h, c * P:(c + 1) * P])], *qk_ready, *free)
                pi, pm, pfree = PM.take()
                ex = act.run(lambda e, pm=pm, c=c, h=h, col=col: e.activation(
                    pm, RM[:, c, h * P:(h + 1) * P], ACT.Exp, bias=NM2[:, col:col + 1]), gates_ready, rm_ready[c], *pfree)
                pr = dve.run(lambda e, pm=pm, bank=bank: e.tensor_tensor(pm, bank[:, 0:P], pm, ALU.mult), ex, s_tok)
                banks.release(b, pr)
                b, bank, free = banks.take()
                tt = pe.run(lambda e, pm=pm, bank=bank: e.transpose(bank[:, 0:P], pm, IDENT), pr, *free)
                PM.release(pi, tt)
                ti, pt, tfree = PTM.take()
                pt_ready = evacuate(pt, bank[:, 0:P], tt, *tfree, engine=act)
                banks.release(b, pt_ready)
                b, bank, free = banks.take()
                o1 = matmuls(bank[:, 0:P + 1], [(pt, VA[:, c, h, :])], pt_ready, *va_ready[c], *free)
                PTM.release(ti, o1)
                if c == 0:
                    done = dve.run(lambda e, bank=bank, c=c, h=h: e.tensor_copy(HH[:, c, h, :], bank[:, 0:P + 1]), o1)
                    banks.release(b, done)
                else:
                    oi, o, ofree = O1.take()
                    cp = evacuate(o, bank[:, 0:P + 1], o1, *ofree, engine=act)
                    banks.release(b, cp)
                    b, bank, free = banks.take()
                    o2 = matmuls(bank[:, 0:P + 1], [(q_, CST8[:, h, :])], c_ready[h], *free)
                    done = dve.run(lambda e, bank=bank, o=o, c=c, h=h, col=col: e.scalar_tensor_tensor(
                        HH[:, c, h, :], bank[:, 0:P + 1], SI[:, col:col + 1], o, ALU.mult, ALU.add), o2, cp)
                    banks.release(b, done)
                    O1.release(oi, done)
                hh_ready.append(done)
                if c < NT - 1:
                    wi, vw, wfree = VW.take()
                    vwr = dve.run(lambda e, vw=vw, c=c, h=h, col=col: e.tensor_scalar(vw, VA[:, c, h, :], WK[:, col:col + 1],
                                                                                      None, ALU.mult), *va_ready[c], *wfree)
                    b, bank, free = banks.take()
                    up = matmuls(bank[:, 0:P + 1], [(KTOK[:, c, h, :], vw)], vwr, ktok_ready[c], *free)
                    VW.release(wi, up)
                    if c == 0:
                        c_ready[h] = dve.run(lambda e, bank=bank, h=h: e.tensor_copy(CST8[:, h, :], bank[:, 0:P + 1]), up)
                    else:
                        c_ready[h] = dve.run(lambda e, bank=bank, h=h, col=col: e.scalar_tensor_tensor(
                            CST8[:, h, :], CST8[:, h, :], DC[:, col:col + 1], bank[:, 0:P + 1], ALU.mult, ALU.add), up, o2)
                    banks.release(b, c_ready[h])

        DEN, SSM, FAC = SM[:, 372:388], SM[:, 388:404], SM[:, 404:420]
        per_head = lambda v: v.rearrange("p (c h) -> p c h", c=NT)
        q = dve.run(lambda e: e.scalar_tensor_tensor(per_head(DEN), HH[:, :, :, P], -1.0, HH[:, :, :, P],
                                                     ALU.mult, ALU.max), *hh_ready)
        q = dve.run(lambda e: e.tensor_tensor(DEN, DEN, EM, ALU.max), q)
        den = dve.run(lambda e: e.reciprocal(DEN, DEN), q)
        for c in range(NT):
            for h in range(MH):
                col = 4 * c + h
                sc = dve.run(lambda e, c=c, h=h, col=col: e.tensor_scalar(HH[:, c, h, 0:P], HH[:, c, h, 0:P], DEN[:, col:col + 1],
                                                                          None, ALU.mult), den)
                ssq = act.run(lambda e, c=c, h=h, col=col: e.activation(JUNK[:, 0:P], HH[:, c, h, 0:P], ACT.Square,
                                                                        accum_out=SSM[:, col:col + 1]), sc, act.last())
        r = rstd(FAC, SSM, P, ssq)
        by = FAC.rearrange("p (c h) -> p c h", c=NT).unsqueeze(3).to_broadcast([P, NT, MH, P])
        normed = dve.run(lambda e: e.tensor_tensor(HH[:, :, :, 0:P], HH[:, :, :, 0:P], by, ALU.mult), r)
        gated = Slots([arena(4096 + 512 * i, T) for i in range(2)])
        ym_ready = []
        for h in range(MH):
            b, bank, free = banks.take()
            pe.wait(normed, *free)
            for c in range(NT):
                f = lambda e, c=c, h=h, bank=bank: e.transpose(bank[:, c * P:(c + 1) * P], HH[:, c, h, 0:P], IDENT)
                turned = pe.run(f) if c == NT - 1 else pe.more(f)
            g = VC[:, VEC["g_head"] + h:VEC["g_head"] + h + 1]
            gi, gm, gfree = gated.take()
            prod = dve.run(lambda e: e.scalar_tensor_tensor(gm, bank[:, :], g, SO[:, h, :], ALU.mult, ALU.mult),
                           turned, so_ready[h], *gfree)
            banks.release(b, prod)
            ym_ready.append(split_pair(YM[:, 0, h, :], YM[:, 1, h, :], gm, prod))
            gated.release(gi, ym_ready[-1])

        quiet = [pe.last(), act.last(), dve.last(), pool.last()]
        act.wait(*quiet)
        dve.wait(*quiet)
        NQ = arena(0, 4, T)
        KC, VCM = arena(2048, T), arena(2560, T)
        KS, KW = arena(3072, T), arena(3584, T)
        VSW = arena(4096, NT, 256)
        XC = [arena(8192 + 2048 * j, CMP_BLOCK, 64) for j in range(2)]
        HID = arena(7168, 2, P)
        HIDT = arena(7424, 2, 64)
        KCC = arena(7552, P)
        VCC = arena(7680, P)
        e_slots = Slots([arena(8192 + 512 * i, T) for i in range(6)])
        p_slots = Slots([arena(11264 + 512 * i, T) for i in range(3)])
        YN = TOK[:, 0:2, :].rearrange("p a (b c) -> p (a b) c", b=2)

        kv_ready = {}

        def kv_sink(dsts, col):
            def sink(m, bank, token):
                c = VEC["b_kv"] + col + m
                kv_ready[col + m] = evacuate(dsts[m], bank[:, :], token, bias=VC[:, c:c + 1])
                return [kv_ready[col + m]]
            return sink
        project_features("nsa", C_NKV, 256, h_ready, kv_sink([KC, VCM], 0))
        blocks_ready = []
        for j, src in enumerate((KC, VCM)):
            zero = dve.run(lambda e: e.memset(XC[j][:, :, :], 0.0))
            for g in range(NG_):
                r = slice(HD * g, HD * (g + 1))
                s = src[r]
                windows = bass.AP(s.tensor, s.offset, [list(s.ap[0]), [1, CMP_BLOCK], [CMP_STRIDE, NCMP]])
                pos = PEC[r, CMP_BLOCK * j:CMP_BLOCK * (j + 1)].unsqueeze(2).to_broadcast([HD, CMP_BLOCK, NCMP])
                blocks_ready.append(dve.run(lambda e: e.tensor_tensor(XC[j][r, :, 32 * g:32 * g + NCMP], windows, pos, ALU.add),
                                            kv_ready[j], zero))

        nq_ready = [None] * 4

        def nq_sink(m, bank, token):
            c = VEC["b_nq"] + m
            add = evacuate(NQ[:, m, :], bank[:, :], token, bias=VC[:, c:c + 1], engine=dve)
            nq_ready[m] = dve.run(lambda e: e.tensor_scalar(NQ[:, m, :], NQ[:, m, :], SCALE, None, ALU.mult), add)
            return [add]

        for m in range(4):
            b, bank, token = feature_tile(("nsa q", "pieces", C_NQ + HD * m), HT, h_ready)
            banks.release(b, *nq_sink(m, bank, token))
        project_features("nsa", C_NKV + 256, P, h_ready, kv_sink([KS], 2))
        project_features("nsa", C_NKV + 512, P, h_ready, kv_sink([KW], 4))
        vs_ready = []

        def vs_sink(t, b, bank, token):
            vs_ready.append(dve.run(lambda e: e.tensor_tensor(VSW[:, t, :], bank[:, 0:256], BVR[:, 512:768], ALU.add), token))
            return [vs_ready[-1]]
        project_tokens("nsa values", C_NKV + 384, 256, HT, ND, h_ready, vs_sink)

        cmp_ready = []
        hid_ready = []
        for j in range(2):
            b, bank, free = banks.take()
            pe.wait(*blocks_ready, *free)
            for l in range(0, CMP_BLOCK, 8):
                slab("compress", j, l)
                i, r, arrived = arrivals[used[0] - 1][0:3]
                w1 = RAW[r][:, :].rearrange("p (l h) -> p l h", l=8)
                pe.wait(arrived)
                for ll in range(8):
                    f = lambda e: e.matmul(bank[0:64, 0:P], XC[j][:, l + ll, :], w1[:, ll, :],
                                           start=(l + ll == 0), stop=(l + ll == CMP_BLOCK - 1))
                    token = pe.run(f) if ll == 7 else pe.more(f)
                raw_slots.release(i, token)
            silu = act.run(lambda e: e.activation(HID[0:64, j, :], bank[0:64, 0:P], ACT.Silu), token)
            banks.release(b, silu)
            b, bank, free = banks.take()
            token = pe.run(lambda e: e.transpose(bank[:, 0:64], HID[0:64, j, :], CST[0:64, 0:64]), silu, *free)
            hid_ready.append(dve.run(lambda e: e.tensor_copy(HIDT[:, j, :], bank[:, 0:64]), token))
            banks.release(b, hid_ready[-1])
        log_exp_table()
        cmp_ready.append(dve.run(lambda e: e.memset(KCC[:, :], 0.0)))
        b, bank, free = banks.take()
        w2 = W2C[:, 0:2, :].rearrange("p a d -> p (a d)")
        token = pe.run(lambda e: e.matmul(bank[:, 0:64], w2, HIDT[:, 0, :], start=True, stop=True), hid_ready[0], *free)
        for g in range(NG_):
            r = slice(HD * g, HD * (g + 1))
            cmp_ready.append(dve.run(lambda e: e.tensor_copy(KCC[r, 0:NCMP], bank[r, 32 * g:32 * g + NCMP]), token, *cmp_ready))
        banks.release(b, cmp_ready[-1])
        for g in range(NG_):
            b, bank, free = banks.take()
            token = pe.run(lambda e: e.matmul(bank[0:NCMP, 0:HD], HIDT[:, 1, 32 * g:32 * g + NCMP], W2C[:, 2, :],
                                              start=True, stop=True), hid_ready[1], *free)
            cmp_ready.append(dve.run(lambda e: e.tensor_copy(VCC[0:NCMP, HD * g:HD * (g + 1)], bank[0:NCMP, 0:HD]), token))
            banks.release(b, cmp_ready[-1])
        dve.wait(pe.last())
        act.wait(pe.last())

        yn_ready = {}
        units = []

        def branch_finish(h, t, first):
            def finish(u, bank, token):
                dst = YN[:, t, h * HD:(h + 1) * HD]
                if first:
                    f = lambda e: e.tensor_scalar(dst, bank, u.scalar, None, ALU.mult)
                else:
                    f = lambda e: e.scalar_tensor_tensor(dst, bank, u.scalar, dst, ALU.mult, ALU.add)
                yn_ready[h, t] = dve.run(f, token, u.norm, yn_ready.get((h, t)))
                return [yn_ready[h, t]]
            return finish

        for h in range(NH):
            g, rr = h // NR, h % NR
            r = slice(HD * g, HD * (g + 1))
            start, row, row_ready, row_done = bias_rows(strip_dram[h], rev_written)
            for t in range(NT):
                qt = NQ[r, rr, t * P:(t + 1) * P]
                w = (t + 1) * P
                nw = (w - CMP_BLOCK) // CMP_STRIDE + 1
                first = T - P + CMP_BLOCK - 1 - P * t
                windows = lambda row=row, first=first, nw=nw: row()[:, first:first + CMP_STRIDE * (nw - 1) + 1:CMP_STRIDE]
                tokens_ = lambda row=row, t=t: row()[:, T - P - P * t:T]
                gate = lambda br: NGT[:, t, 3 * h + br:3 * h + br + 1]
                common = dict(coef_ready=ng_ready, bias_ready=row_ready, mask=False, nv=HD, at=HD * g)
                units.append(Unit(w=nw, maps=[(qt, KCC[r, :])], ready=[*nq_ready, *cmp_ready], bias=windows, floor=1e29,
                                  coef=gate(0), v=lambda j, nw=nw: VCC[0:nw, :], v_ready=cmp_ready,
                                  start=start if t == 0 else None, finish=branch_finish(h, t, True), **common))
                for br, keys, base in ((1, KS, 0), (2, KW, P)):
                    units.append(Unit(w=w, maps=[(qt, keys[r, 0:w])], ready=[*nq_ready, kv_ready[2 * br]],
                                      bias=tokens_, coef=gate(br), v=lambda j, base=base: VSW[:, j, base:base + P],
                                      last_of_head=row_done if (t, br) == (NT - 1, 2) else None,
                                      v_ready=vs_ready, finish=branch_finish(h, t, False), **common))
        attend(units, e_slots, p_slots)
        dve.wait(pe.last())
        act.wait(pe.last())
        yn_t = turn_tokens(YN, NT, 4, YNT, [dve.last()])

        gate_buf = Slots([TOK[:, 2 + i // 2, (i % 2) * 512:(i % 2) * 512 + 512] for i in range(4)])
        mix_ready = []
        for d in range(ND):
            parts = []
            for n, (y, y_tok) in enumerate(((YM, ym_ready), (YNT, yn_t))):
                b, bank, tok = feature_tile(("merge", C_MERGE + D * n + d * P), HT, h_ready)
                si, sg, sfree = gate_buf.take()
                c = VEC["b_merge"] + ND * n + d
                sig = act.run(lambda e: e.activation(sg, bank[:, :], ACT.Sigmoid, bias=VC[:, c:c + 1]), tok, *sfree)
                banks.release(b, sig)
                b, bank, tok = feature_tile((f"branch{n}", d * P), y, y_tok, 4)
                pr = dve.run(lambda e: e.tensor_tensor(sg, bank[:, :], sg, ALU.mult), tok, sig)
                banks.release(b, pr)
                parts.append((si, sg, pr))
            (i0, g0, p0), (i1, g1, p1) = parts
            both = dve.run(lambda e: e.tensor_tensor(g0, g0, g1, ALU.add), p0, p1)
            gate_buf.release(i1, both)
            mix_ready.append(split_pair(MIX[:, 0, d, :], MIX[:, 1, d, :], g0, both))
            gate_buf.release(i0, mix_ready[-1])
        log_exp_table()

        out_product("out", MIX, ND, lambda k: [mix_ready[k]], residual(x_tokens, diag_of))
        h_ready = pre_norm(diags, VEC["ffn2_pre"])
        g_row = gain_row(a["g_final_2"])
        out_done = [sem("out_stored"), 0]
        stored = []

        def finish_tokens(t):
            sq = act.run(lambda e: e.activation(TOK[:, t, :], X[:, t, :], ACT.Square, accum_out=NST[:, t:t + 1]), x_tokens[t])
            r = rstd(NST[:, 4 + t:5 + t], NST[:, t:t + 1], D, sq)
            f = dve.run(lambda e: e.scalar_tensor_tensor(TOK[:, t, :], X[:, t, :], NST[:, 4 + t:5 + t], GROW[:, :],
                                                         ALU.mult, ALU.mult), r, g_row)
            stored.append(sync.dma(out[0, t * P:(t + 1) * P, :], TOK[:, t, :], out_done, f))

        feed_forward(h_ready, residual(x_tokens), residual(x_tokens, finish_tokens))

        sync.wait(stored[-1], decay_written, rev_written)


_INS = ['x', 'positions', 'attn_pre_g', 'w_in', 'forget_bias', 'lam_q1', 'lam_k1', 'lam_q2', 'lam_k2', 'diff_sub_g',
        'w_out', 'attn_post_g', 'ffn_pre_g', 'w_gate', 'w_up', 'w_down', 'ffn_post_g', 'g_norm_mix_2', 'w_in_2',
        'b_in_2', 'b_fgate_2', 'conv_qk_2', 'g_mlstm_head_2', 'pe_cmp_2', 'w_cmp1_2', 'w_cmp2_2', 'rel_bias_2',
        'w_branch_2', 'w_out_2', 'g_norm_ffn_2', 'w_gate_2', 'w_up_2', 'w_down_2', 'g_final_2']


def kernel(**inputs):
    import numpy as _np
    import concourse.bacc as _bacc
    from concourse import mybir as _mybir
    from concourse.bass_utils import run_bass_kernel_spmd as _run

    nc = _bacc.Bacc("TRN2", target_bir_lowering=False, num_devices=1)
    arrays, args = {}, {}
    given = {name: inputs[name] for name in _INS}
    given["shape_constants"] = shape_constants()
    for name, value in given.items():
        v = _np.ascontiguousarray(value)
        if name.startswith("g_final"):
            v = v.reshape(-1)
        arrays[f"in_{name}_dram"] = v
        args[name] = nc.dram_tensor(f"in_{name}_dram", v.shape, _mybir.dt.from_np(v.dtype), kind="ExternalInput").ap()
    result = nc.dram_tensor("out_0_dram", (1, T, D), F32, kind="ExternalOutput").ap()
    program(nc, args, result)
    r = _run(nc, [arrays], core_ids=[0])
    return r.results[0]["out_0_dram"]
```

```python
from contextlib import ExitStack
import math

import numpy as np
import concourse.bass as bass
from concourse import mybir

F32 = mybir.dt.float32
F32R = mybir.dt.float32r
BF16 = mybir.dt.bfloat16
I32 = mybir.dt.int32
ALU = mybir.AluOpType
ACT = mybir.ActivationFunctionType
AX = mybir.AxisListType.X

P = 128
D = 1024
T = 512
NT = T // P
ND = D // P
DFF = 2816
NF = DFF // P
LAYERS = 2
HD = 64
NEG = -1e30
EPS = 1e-6
BIG = 3e38
SCALE = HD ** -0.5

C_QA, C_KA, C_VA, C_QB, C_KB, C_VB, C_F = [512 * i for i in range(7)]
N_DIFF, N_FOX = 4, 8
C_MQ, C_MK, C_MV, C_MO, C_IF, C_NQ, C_NKV, C_NG, C_MERGE = 0, 512, 1024, 1536, 2048, 2056, 2568, 3336, 3360
MH = 4
NH, NG_, NR = 8, 2, 4
CMP_BLOCK, CMP_STRIDE = 32, 16
NCMP = (T - CMP_BLOCK) // CMP_STRIDE + 1
BUCKETS = 32
CONV = 4
REV = 640
RAW_SLOTS = 4
TAIL = 2
PAIR_SLOTS = 3
SLAB = 1024
NCHUNK = 2
NFC = NF // NCHUNK
ARENA_WORDS = 16896

VEC = {}
_at = 0
for _name, _n in (("attn_pre", 16), ("ffn_pre", 16), ("mix_pre", 8), ("ffn2_pre", 8), ("diff_sub", 2),
                  ("b_qk", 8), ("b_mo", 4), ("b_nq", 4), ("b_kv", 6), ("b_merge", 16), ("g_head", 4),
                  ("conv", 32)):
    VEC[_name] = _at
    _at += _n
NVEC = _at

K_ID, K_ROT, K_TRI, K_MASK, K_FREQ, K_HOT = 0, 128, 256, 768, 896, 897
NCONST = 897
NTABLE = K_HOT + T


def shape_constants():
    c = np.zeros((P, NTABLE), np.float32)
    c[:, K_ID:K_ID + P] = np.eye(P)
    for m in range(P):
        if m % HD < 8:
            c[m + 8, K_ROT + m] = -1.0
        elif m % HD < 16:
            c[m - 8, K_ROT + m] = 1.0
    k = np.arange(P)[:, None]
    c[:, K_TRI:K_TRI + T] = np.arange(T)[None, :] >= k
    c[:, K_MASK:K_MASK + P] = np.where(np.arange(P)[None, :] > k, NEG, 0.0)
    dist = (T - 1 - np.arange(T)).astype(np.int64)
    nf = np.maximum(dist, 1).astype(np.float32)
    large = 16 + (np.log(nf / np.float32(16)) / np.float32(math.log(64)) * np.float32(16)).astype(np.int32)
    bucket = np.where(dist < 16, dist, np.minimum(large, BUCKETS - 1))
    c[:BUCKETS, K_HOT:K_HOT + T] = bucket[None, :] == np.arange(BUCKETS)[:, None]
    freq = (1.0 / np.power(np.float32(500000.0), np.arange(0, 16, 2, dtype=np.float32) / 16)).astype(np.float32)
    for m in range(P):
        if m % HD < 16:
            c[m, K_FREQ] = freq[m % 8]
    return c


FILL_1 = [(1, C_QA, 1), (2, C_KA, 1), (5, C_QA, 2), (6, C_KA, 2), (8, C_QA, 3), (9, C_KA, 3), (12, C_QB, 0),
          (13, C_KB, 0), (17, C_QB, 1), (20, C_KB, 1), (24, C_QB, 2), (27, C_KB, 2), (31, C_QB, 3), (34, C_KB, 3)]


class Queue:

    def __init__(self, engine, semaphore):
        self.engine, self.semaphore, self.count, self.passed = engine, semaphore, 0, {}

    def wait(self, *tokens):
        for token in tokens:
            if token is None:
                continue
            if isinstance(token, list):
                self.wait(*token)
                continue
            semaphore, value = token
            if self.passed.get(semaphore.name, 0) < value:
                self.passed[semaphore.name] = value
                self.engine.wait_ge(semaphore, value)

    def run(self, make, *after):
        self.wait(*after)
        self.count += 1
        make(self.engine).then_inc(self.semaphore, 1)
        return (self.semaphore, self.count)

    def more(self, make, *after):
        self.wait(*after)
        make(self.engine)

    def dma(self, out, in_, arrival, *after):
        self.wait(*after)
        arrival[1] += 16
        self.engine.dma_start(out, in_).then_inc(arrival[0], 16)
        return (arrival[0], arrival[1])

    def last(self):
        return (self.semaphore, self.count) if self.count else None


class Slots:

    def __init__(self, buffers):
        self.buffers, self.turn, self.free = buffers, 0, [[] for _ in buffers]

    def take(self):
        i = self.turn
        self.turn = (i + 1) % len(self.buffers)
        assert self.free[i] is not None, "buffer taken again before its readers were named"
        readers, self.free[i] = self.free[i], None
        return i, self.buffers[i], readers

    def release(self, i, *readers):
        self.free[i] = list(readers)


def program(nc, a, out):
    ctx = ExitStack()
    with ctx:
        def sb(name, shape, dt=F32):
            return ctx.enter_context(nc.sbuf_tensor(name, shape, dt))

        def sem(name):
            return ctx.enter_context(nc.semaphore(name))

        X = sb("x_residual", [P, NT, D])
        HT = sb("h_features", [P, 2, ND, T], F32R)
        TOK = sb("token_scratch", [P, NT, D])
        arena_at = -(-nc.sbuf_base // 32) * 32
        ARENA = sb("arena", [P, ARENA_WORDS])
        HIDDEN = nc.alloc_sbuf_tensor_at("hidden", [P, 2, NFC, T], F32R, offset=arena_at)
        YM = nc.alloc_sbuf_tensor_at("mlstm_features", [P, 2, 4, T], F32R, offset=arena_at + 4 * 12800)
        YNT = nc.alloc_sbuf_tensor_at("nsa_features", [P, 2, 4, T], F32R, offset=arena_at)
        MIX = nc.alloc_sbuf_tensor_at("mixed_features", [P, 2, ND, T], F32R, offset=arena_at + 4 * 4096)
        BIAS = [sb(f"bias_rows{i}", [P, T]) for i in range(3)]
        RAW = [sb(f"weights{i}", [P, SLAB]) for i in range(RAW_SLOTS)]
        PAIRS = [sb(f"weights_hi_lo{i}", [P, 2, SLAB], F32R) for i in range(PAIR_SLOTS)]
        GROW = sb("gain_row", [P, D])
        COS = sb("cos_table", [P, T])
        SIN = sb("sin_table", [P, T])
        CST = sb("shape_consts", [P, NCONST])
        VC = sb("vector_columns", [P, NVEC])
        PEC = sb("position_columns", [P, 2 * CMP_BLOCK])
        IDB = sb("identity_bf16", [P, P], BF16)
        MKB = sb("mask_bf16", [P, P], BF16)
        ONES = sb("ones", [P, P])
        EPSC = sb("eps_column", [P, 1])
        DIAG = sb("diag_rstd", [P, NT, P])
        RTMP = sb("rotary_scratch", [P, T])
        STAT = sb("row_stats", [P, 16, 8])
        NST = sb("norm_stats", [P, 64])
        NLAM = sb("neg_lambda", [P, 16])
        FBI = sb("forget_bias_columns", [N_FOX, LAYERS])
        JUNK = sb("junk", [P, T])
        NEGC = sb("neg_decay", [8, T])
        BVR = sb("value_bias_rows", [P, 800])
        SM = sb("small_tok", [P, 600])
        PSUM = [ctx.enter_context(nc.psum_tensor(f"bank{i}", [P, T], F32)) for i in range(8)]
        tok_done = [[] for _ in range(NT)]
        diag_read = [None] * NT
        decay_dram = nc.dram_tensor("decay_scratch", [LAYERS, N_FOX, T], F32).ap()
        strip_dram = nc.dram_tensor("bias_scratch", [NH, P, T], F32).ap()

        pe = Queue(nc.tensor, sem("pe_done"))
        act = Queue(nc.scalar, sem("act_done"))
        dve = Queue(nc.vector, sem("dve_done"))
        pool = Queue(nc.gpsimd, sem("pool_done"))
        sync = Queue(nc.sync, sem("sync_done"))
        raw_arrival = [[sem(f"weights{i}_arrival"), 0] for i in range(RAW_SLOTS)]
        raw_slots = Slots(list(range(RAW_SLOTS)))
        pair_slots = Slots(PAIRS)
        bias_slots = Slots(BIAS)
        bias_in = [[sem(f"bias_rows{i}_arrival"), 0] for i in range(3)]
        banks = Slots(PSUM)
        IDENT = CST[:, K_ID:K_ID + P]
        TRI = CST[:, K_TRI:K_TRI + T]
        MASK = CST[:, K_MASK:K_MASK + P]
        stat = Slots([STAT[:, i, :] for i in range(16)])

        def arena(at, *shape):
            n = int(np.prod(shape))
            assert at + n <= ARENA_WORDS
            v = ARENA[:, at:at + n]
            if len(shape) == 2:
                return v.rearrange("p (a b) -> p a b", a=shape[0])
            if len(shape) == 3:
                return v.rearrange("p (a b c) -> p a b c", a=shape[0], b=shape[1])
            return v

        const_in = [sem("consts_arrival"), 0]
        x_in = [[sem(f"x{t}_arrival"), 0] for t in range(NT)]
        vec_in = [sem("vectors_arrival"), 0]
        row_in = [sem("rows_arrival"), 0]
        late_in = [sem("second_block_rows_arrival"), 0]
        pos_in = [sem("positions_arrival"), 0]
        gain_in = [sem("gain_row_arrival"), 0]

        x_ready = [sync.dma(X[:, t, :], a["x"][0, t * P:(t + 1) * P, :], x_in[t]) for t in range(NT)]
        pool.dma(CST[:, :], a["shape_constants"][:, 0:NCONST], const_in)
        HOT = arena(12288, T)[0:BUCKETS]
        consts = pool.dma(HOT, a["shape_constants"][0:BUCKETS, K_HOT:NTABLE], const_in)

        POSI = arena(8192, T).bitcast(I32)
        positions = pool.dma(POSI, a["positions"][0].partition_broadcast(P), pos_in)

        LAM = arena(10240, 4 * LAYERS * HD).rearrange("p (a l d) -> p a l d", a=4, l=LAYERS)
        ROWS = arena(0, P)
        PER = arena(128, P)

        vec_in_act = [sem("vectors_by_scalar_arrival"), 0]
        queues = [(pool, vec_in), (act, vec_in_act)]

        def rows(name, src, at=0, cols=None):
            r = VEC[name] + at
            n = src.shape[0]
            dst = ARENA[r:r + n, 0:P] if cols is None else ARENA[r:r + n, cols[0]:cols[1]]
            queues.append(queues.pop(0))
            queue, arrival = queues[0]
            return queue.dma(dst, src, arrival)

        def tiles_of(v):
            return v.rearrange("l (k p) -> (l k) p", p=P)

        def row_tiles(v):
            return v.rearrange("(k p) -> k p", p=P)

        b_in = a["b_in_2"][0]
        rows("attn_pre", tiles_of(a["attn_pre_g"]))
        rows("ffn_pre", tiles_of(a["ffn_pre_g"]))
        rows("mix_pre", tiles_of(a["g_norm_mix_2"]))
        rows("ffn2_pre", tiles_of(a["g_norm_ffn_2"]))
        rows("diff_sub", a["diff_sub_g"])
        rows("b_qk", row_tiles(b_in[C_MQ:C_MV]))
        rows("b_mo", row_tiles(b_in[C_MO:C_IF]))
        for g in range(NG_):
            rows("b_nq", b_in[C_NQ + 256 * g:C_NQ + 256 * (g + 1)].rearrange("(r d) -> r d", d=HD),
                 cols=(HD * g, HD * (g + 1)))
        rows("b_kv", row_tiles(b_in[C_NKV:C_NG]))
        rows("b_merge", row_tiles(b_in[C_MERGE:C_MERGE + 2 * D]))
        rows("g_head", tiles_of(a["g_mlstm_head_2"]))
        rows("conv", a["conv_qk_2"][0].rearrange("j (k p) -> (j k) p", p=P))
        for g in range(2):
            vectors = pool.dma(ARENA[0:2 * CMP_BLOCK, P + HD * g:P + HD * (g + 1)],
                               a["pe_cmp_2"][0].rearrange("j l d -> (j l) d"), vec_in)
        for i, name in enumerate(("lam_q1", "lam_q2", "lam_k1", "lam_k2")):
            pool.dma(LAM[:, i, :, :], a[name].partition_broadcast(P), row_in)
        for l in range(LAYERS):
            pool.dma(FBI[:, l:l + 1], a["forget_bias"][l].unsqueeze(1), row_in)
        RELB = sb("rel_bias_sb", [BUCKETS, NH])
        row_vectors = pool.dma(RELB[:, :], a["rel_bias_2"], row_in)

        ones_ready = dve.run(lambda e: e.memset(ONES[:, :], 1.0))
        eps_ready = dve.run(lambda e: e.memset(EPSC[:, :], EPS))
        dve.run(lambda e: e.tensor_copy(IDB[:, :], IDENT), consts)
        bf_ready = dve.run(lambda e: e.tensor_copy(MKB[:, :], MASK))

        def plan_features(name, w, c0, width, kt=ND):
            return [((name, c0 + s), kt, P, True,
                     [(slice(0, P), slice(0, P), w[0:kt * P, c0 + s:c0 + s + P].rearrange("(k p) c -> p k c", p=P))])
                    for s in range(0, width, P)]

        def plan_tokens(name, w, columns, kt, k_start=0):
            width = sum(c1 - c0 for c0, c1 in columns)
            step, entries = SLAB // width, []
            for k in range(k_start, k_start + kt, step):
                n, pieces, at = min(step, k_start + kt - k), [], 0
                for c0, c1 in columns:
                    pieces.append((slice(0, P), slice(at, at + c1 - c0),
                                   w[k * P:(k + n) * P, c0:c1].rearrange("(k p) c -> p k c", p=P)))
                    at += c1 - c0
                entries.append(((name, columns[0][0], k), n, width, True, pieces))
            return entries

        def plan_pieces(name, w, columns):
            pieces, at = [], 0
            for c0, c1 in columns:
                pieces.append((slice(0, P), slice(at, at + c1 - c0), w[:, c0:c1].rearrange("(k p) c -> p k c", p=P)))
                at += c1 - c0
            return [((name, "pieces", columns[0][0]), ND, P, True, pieces)]

        def plan_ffn(name, wg, wu, wd):
            entries = []
            for c in range(NCHUNK):
                for f in range(NFC * c, NFC * (c + 1)):
                    entries += plan_features(name + " gate", wg, f * P, P) + plan_features(name + " up", wu, f * P, P)
                for half in range(2):
                    entries += plan_tokens(name + " down", wd, [(512 * half, 512 * half + 512)], NFC, NFC * c)
            return entries

        plan = []
        for layer in range(LAYERS):
            w = a["w_in"][layer]
            plan += plan_pieces("forget", w, [(C_F, C_F + N_FOX), (C_QB, C_QB + P - N_FOX)])
            plan += plan_features("qkv", w, C_QA, P)
            plan += plan_features("qkv", w, C_KA, P)
            plan += plan_tokens("values", w, [(C_VA, C_VA + 512)], ND)
            plan += plan_tokens("values", w, [(C_VB, C_VB + 512)], ND)
            for _, c, m in FILL_1:
                plan += plan_features("qkv", w, c + m * P, P)
            for half in range(2):
                plan += plan_tokens("out", a["w_out"][layer], [(512 * half, 512 * half + 512)], ND)
            plan += plan_ffn("ffn", a["w_gate"][layer], a["w_up"][layer], a["w_down"][layer])
        w = a["w_in_2"][0]
        plan += plan_pieces("gates", w, [(C_IF, C_IF + 8), (C_NG, C_NG + P - 8)])
        plan += plan_features("qk", w, C_MQ, 1024)
        plan += plan_tokens("values", w, [(C_MV, C_MV + 512)], ND)
        plan += plan_features("output gate", w, C_MO, 512)
        plan += plan_features("nsa", w, C_NKV, 384)
        for m in range(4):
            plan += plan_pieces("nsa q", w, [(C_NQ + HD * m, C_NQ + HD * (m + 1)),
                                             (C_NQ + 256 + HD * m, C_NQ + 256 + HD * (m + 1))])
        plan += plan_features("nsa", w, C_NKV + 512, P)
        plan += plan_tokens("nsa values", w, [(C_NKV + 384, C_NKV + 512), (C_NKV + 640, C_NKV + 768)], ND)
        for j in range(2):
            w1 = a["w_cmp1_2"][0, j].rearrange("(l d) h -> d l h", d=HD)
            for l in range(0, CMP_BLOCK, 8):
                plan.append((("compress", j, l), 8, P, False, [(slice(0, HD), slice(0, P), w1[:, l:l + 8, :]),
                                                               (slice(HD, P), slice(0, P), w1[:, l:l + 8, :])]))
        for d in range(ND):
            for n in range(2):
                plan += plan_features("merge", w, C_MERGE + D * n + d * P, P)
                plan += plan_features(f"branch{n}", a["w_branch_2"][0, n], d * P, P, 4)
        for half in range(2):
            plan += plan_tokens("out", a["w_out_2"][0], [(512 * half, 512 * half + 512)], ND)
        plan += plan_ffn("ffn", a["w_gate_2"][0], a["w_up_2"][0], a["w_down_2"][0])

        arrivals, splits = [], []

        def advance(using):
            while len(splits) < min(len(plan), using + PAIR_SLOTS):
                transfers()
                i, r, token, kt, width, split = arrivals[len(splits)]
                if split and pair_slots.free[pair_slots.turn] is None:
                    break
                if not split:
                    splits.append(None)
                    continue
                raw = RAW[r][:, 0:kt * width]
                j, pair, readers = pair_slots.take()
                hi, lo = pair[:, 0, 0:kt * width], pair[:, 1, 0:kt * width]
                h = act.run(lambda e: e.activation(hi, raw, ACT.Copy), token, *readers)
                l = dve.run(lambda e: e.tensor_tensor(lo, raw, hi.bitcast(F32), ALU.subtract), h)
                raw_slots.release(i, l)
                splits.append((j, hi.rearrange("p (k c) -> p k c", k=kt), lo.rearrange("p (k c) -> p k c", k=kt), l))
            transfers()

        def transfers():
            while len(arrivals) < len(plan) and raw_slots.free[raw_slots.turn] is not None:
                _, kt, width, split, pieces = plan[len(arrivals)]
                i, r, readers = raw_slots.take()
                view = RAW[r][:, 0:kt * width].rearrange("p (k c) -> p k c", k=kt)
                for parts, cols, src in pieces:
                    token = sync.dma(view[parts, :, cols], src, raw_arrival[r], *readers)
                arrivals.append((i, r, token, kt, width, split))

        used = [0]

        def slab(*key):
            i = used[0]
            assert plan[i][0] == key, (plan[i][0], key)
            used[0] += 1
            advance(i)
            return splits[i]

        def matmuls(out_ap, pairs, *after):
            pe.wait(*after)
            n = len(pairs)
            for j, (l, r) in enumerate(pairs):
                f = lambda e, l=l, r=r, j=j: e.matmul(out_ap, l, r, start=(j == 0), stop=(j == n - 1))
                token = pe.run(f) if j == n - 1 else pe.more(f)
            return token

        def matmuls3(out_ap, pairs, *after):
            return matmuls(out_ap, [x for (lh, ll), (rh, rl) in pairs for x in ((lh, rl), (ll, rh), (lh, rh))], *after)

        flip = [0]

        def evacuate(dst, src, *after, scale=None, bias=None, engine=None):
            flip[0] ^= 1
            q = engine or (dve if flip[0] else act)
            if q is dve:
                if scale is None and bias is None:
                    f = lambda e: e.tensor_copy(dst, src)
                elif bias is None:
                    f = lambda e: e.tensor_scalar(dst, src, scale, None, ALU.mult)
                elif scale is None:
                    f = lambda e: e.tensor_scalar(dst, src, bias, None, ALU.add)
                else:
                    f = lambda e: e.tensor_scalar(dst, src, scale, bias, ALU.mult, ALU.add)
            elif bias is None:
                f = lambda e: e.activation(dst, src, ACT.Copy, scale=1.0 if scale is None else scale)
            else:
                f = lambda e: e.activation(dst, src, ACT.Identity, bias=bias, scale=1.0 if scale is None else scale)
            return q.run(f, *after)

        def rstd(dst, ss, n, *after):
            ln = act.run(lambda e: e.activation(dst, ss, ACT.Ln, bias=EPSC[:, 0:1], scale=1.0 / n), eps_ready, *after)
            return act.run(lambda e: e.activation(dst, dst, ACT.Exp, scale=-0.5), ln)

        def log_exp_table():
            act.engine.preload_act_table_set("natural_log_exp_and_others")

        def split_pair(hi, lo, src, *after, engine=None):
            h = act.run(lambda e: e.activation(hi, src, ACT.Copy), *after)
            return (engine or dve).run(lambda e: e.tensor_tensor(lo, src, hi.bitcast(F32), ALU.subtract), h, *after)

        def evacuate_pair(hi, lo, bank, *after):
            h = act.run(lambda e: e.activation(hi, bank, ACT.Copy), *after)
            return dve.run(lambda e: e.tensor_tensor(lo, bank, hi.bitcast(F32), ALU.subtract), h)

        turn_slots = Slots([arena(15360 + 512 * i, T) for i in range(3)])

        def to_features(dest, t, k0, bank, token, gains=None):
            hi = dest[:, 0, k0:k0 + 4, t * P:(t + 1) * P]
            lo = dest[:, 1, k0:k0 + 4, t * P:(t + 1) * P]
            b4 = bank[:, :].rearrange("p (k n) -> p k n", k=4)
            if gains is None:
                h = act.run(lambda e: e.activation(hi, b4, ACT.Copy), token)
                return None, lambda: dve.run(lambda e: e.tensor_tensor(lo, b4, hi.bitcast(F32), ALU.subtract), h)
            i, tmp, free = turn_slots.take()
            tmp4 = tmp.rearrange("p (k n) -> p k n", k=4)
            scaled = dve.run(lambda e: e.tensor_tensor(tmp4, b4, gains, ALU.mult), token, *free)
            h = act.run(lambda e: e.activation(hi, tmp4, ACT.Copy), scaled)

            def rest():
                q = pool if k0 else dve
                done = q.run(lambda e: e.tensor_tensor(lo, tmp4, hi.bitcast(F32), ALU.subtract), h)
                turn_slots.release(i, done)
                return done
            return scaled, rest

        diags = [None] * NT

        def row_norm(x_token, t):
            squares = act.run(lambda e: e.activation(TOK[:, t, :], X[:, t, :], ACT.Square,
                                                     accum_out=NST[:, t:t + 1]), x_token, *tok_done[t])
            r = rstd(NST[:, 4 + t:5 + t], NST[:, t:t + 1], D, squares)

            def put():
                diags[t] = dve.run(lambda e: e.tensor_scalar(DIAG[:, t, :], IDENT, NST[:, 4 + t:5 + t], None, ALU.mult),
                                   r, consts, diag_read[t])
            return put

        def diag_of(t):
            row_norm(x_tokens[t], t)()

        def turner(halves, operands, dest, gains, ready):
            done, rest = [], []

            def settle():
                b, left, f = rest.pop(0)
                token = f()
                if left is None:
                    banks.release(b, token)
                done.append(token)

            def step(t):
                for k0 in halves:
                    b, bank, free = banks.take()
                    pe.wait(*ready(t), *free)
                    for k in range(4):
                        f = lambda e: operands(e, bank[:, k * P:(k + 1) * P], t, k0 + k)
                        token = pe.run(f) if k == 3 else pe.more(f)
                    left, later = to_features(dest, t, k0, bank, token, gains(k0))
                    if left is not None:
                        banks.release(b, left)
                    rest.append((b, left, later))
                    if len(rest) > 1:
                        settle()
                return token

            def flush():
                while rest:
                    settle()
            return step, flush, done

        def turn_tokens(source, tiles, kt, dest, ready, gains=lambda k0: None):
            step, flush, done = turner(range(0, kt, 4),
                                       lambda e, out_ap, t, k: e.transpose(out_ap, source[:, t, k * P:(k + 1) * P], IDENT),
                                       dest, gains, lambda t: [consts, *ready])
            for t in range(tiles):
                step(t)
                if t == 1:
                    advance(used[0])
            flush()
            return done

        class PreNorm:

            def __init__(self, gain_col, next_keys):
                self.keys = next_keys
                self.turn, self.flush, self.done = turner(
                    (0, 4), lambda e, out_ap, t, k: e.matmul(out_ap, X[:, t, k * P:(k + 1) * P], DIAG[:, t, :],
                                                             start=True, stop=True),
                    HT, lambda k0: VC[:, gain_col + k0:gain_col + k0 + 4].unsqueeze(2).to_broadcast([P, 4, P]),
                    lambda t: [diags[t]])

            def step(self, t):
                diag_read[t] = self.turn(t)
                if t == 1:
                    advance(used[0] - 1)
                if t == NT - 1:
                    for key in self.keys:
                        begin_tile(key, HT, self.done[0:4])

            def last_tile(self):
                put = row_norm(x_tokens[NT - 1], NT - 1)
                self.step(0)
                put()
                for t in range(1, NT):
                    self.step(t)

            def finish(self):
                self.flush()
                return self.done

        def hi_lo(v, *index):
            return v[(slice(None), 0) + index], v[(slice(None), 1) + index]

        begun = {}

        def begin_tile(key, source, ready):
            i, hi, lo, arrived = slab(*key)
            b, bank, free = banks.take()
            half = slice(0, T // 2)
            matmuls3(bank[:, half], [((hi[:, k, :], lo[:, k, :]), hi_lo(source, k, half)) for k in range(ND)],
                     arrived, *ready, *free)
            begun[key] = (i, hi, lo, b, bank)

        def feature_tile(key, source, ready, kt=ND):
            tokens = slice(0, T)
            if key in begun:
                i, hi, lo, b, bank = begun.pop(key)
                tokens, free, arrived = slice(T // 2, T), [], None
            else:
                i, hi, lo, arrived = slab(*key)
                b, bank, free = banks.take()
            token = matmuls3(bank[:, tokens], [((hi[:, k, :], lo[:, k, :]), hi_lo(source, k, tokens)) for k in range(kt)],
                             arrived, *ready, *free)
            pair_slots.release(i, token)
            return b, bank, token

        def project_features(name, c0, width, h_ready, sink):
            for s in range(0, width, P):
                b, bank, token = feature_tile((name, c0 + s), HT, h_ready)
                banks.release(b, *sink(s // P, bank, token))

        def project_tokens(name, c0, width, source, kt, ready, sink, k_start=0, tail=False):
            taken = [banks.take() for _ in range(NT)]
            step = SLAB // width
            starts = list(range(0, kt, step))
            together = min(len(starts), TAIL if tail else 1)
            groups = [[k0] for k0 in starts[:-together]] + [starts[-together:]]
            for group in groups:
                slabs = [slab(name, c0, k_start + k0) for k0 in group]
                for t in range(NT):
                    b, bank, free = taken[t]
                    toks = slice(t * P, (t + 1) * P)
                    for (i, hi, lo, arrived), k0 in zip(slabs, group):
                        for k in range(k0, min(k0 + step, kt)):
                            sh, sl = hi_lo(source, k, toks)
                            wh, wl = hi[:, k - k0, :], lo[:, k - k0, :]
                            pe.wait(arrived, *(ready if isinstance(ready, list) else ready(k, t)), *(free if k == 0 else []))
                            for j, (l, r) in enumerate(((sh, wl), (sl, wh), (sh, wh))):
                                first, last = k == 0 and j == 0, k == kt - 1 and j == 2
                                f = lambda e: e.matmul(bank[:, 0:width], l, r, start=first, stop=last)
                                ends = last or (t == NT - 1 and k == min(k0 + step, kt) - 1 and j == 2)
                                token = pe.run(f) if ends else pe.more(f)
                        if t == NT - 1:
                            pair_slots.release(i, token)
                    if group is groups[-1]:
                        readers = sink(t, b, bank, token)
                        if readers is not None:
                            banks.release(b, *readers)

        def gain_row(src):
            return pool.dma(GROW[:, :], src.partition_broadcast(P), gain_in, dve.last())

        def post_norm(g_row, x_tokens, norm, added=None):
            rstd_ready, scaled = {}, {}

            def weigh(half, t, b, bank, token):
                cols = slice(half * 512, half * 512 + 512)
                dst, y = TOK[:, t, cols], bank[:, :]
                if added is not None:
                    y = dst
                    token = dve.run(lambda e: e.tensor_tensor(y, bank[:, :], y, ALU.add), token, added[half, t])
                    banks.release(b, token)
                ss = NST[:, 16 + 4 * half + t:17 + 4 * half + t]
                sq = act.run(lambda e: e.activation(JUNK[:, :], y, ACT.Square, accum_out=ss), token, act.last())
                if half == 0:
                    rstd_ready[t] = dve.run(lambda e: e.tensor_scalar(NST[:, 24 + t:25 + t], ss, 1.0 / D, EPS, ALU.mult, ALU.add), sq)
                else:
                    r = NST[:, 28 + t:29 + t]
                    ln = act.run(lambda e: e.activation(r, ss, ACT.Ln, bias=NST[:, 24 + t:25 + t], scale=1.0 / D),
                                 sq, rstd_ready[t])
                    rstd_ready[t] = act.run(lambda e: e.activation(r, r, ACT.Exp, scale=-0.5), ln)
                scaled[half, t] = dve.run(lambda e: e.tensor_tensor(dst, y, GROW[:, cols], ALU.mult), sq, g_row, *tok_done[t])
                if added is None:
                    banks.release(b, scaled[half, t])

            def update(t):
                x_tokens[t] = dve.run(lambda e: e.scalar_tensor_tensor(X[:, t, :], TOK[:, t, :], NST[:, 28 + t:29 + t], X[:, t, :],
                                                                       ALU.mult, ALU.add), rstd_ready[t], scaled[1, t])
                tok_done[t] = [x_tokens[t]]

            def sink(half, t, b, bank, token):
                weigh(half, t, b, bank, token)
                if half == 1:
                    update(t)
                    if t >= 1:
                        diag_of(t - 1)
                    if t == NT - 1:
                        norm.last_tile()
                return None
            return sink

        def residual(x_tokens, then=None):
            def sink(half, t, b, bank, token):
                dst = X[:, t, half * 512:half * 512 + 512]
                x_tokens[t] = dve.run(lambda e: e.tensor_tensor(dst, bank[:, :], dst, ALU.add), token)
                banks.release(b, x_tokens[t])
                if half == 1 and then is not None:
                    then(t)
                return None
            return sink

        def out_product(name, source, kt, ready, sink, k_start=0):
            for half in range(2):
                project_tokens(name, 512 * half, 512, source, kt, ready, lambda t, b, bank, token: sink(half, t, b, bank, token),
                               k_start, tail=half == 1)

        def feed_forward(h_ready, first_sink, last_sink):
            silu = Slots([arena(11264 + 512 * i, T) for i in range(2)])
            full = Slots([arena(12288 + 512 * i, T) for i in range(2)])
            quiet = [pe.last(), act.last(), dve.last(), pool.last()]
            act.wait(*quiet)
            dve.wait(*quiet)
            for c in range(NCHUNK):
                ready = []
                for f in range(NFC):
                    col = (c * NFC + f) * P
                    gb, gate, g_done = feature_tile(("ffn gate", col), HT, h_ready)
                    si, sg, sfree = silu.take()
                    gated = act.run(lambda e: e.activation(sg, gate[:, :], ACT.Silu), g_done, *sfree)
                    banks.release(gb, gated)
                    ub, up, u_done = feature_tile(("ffn up", col), HT, h_ready)
                    fi, fl, ffree = full.take()
                    prod = dve.run(lambda e: e.tensor_tensor(fl, up[:, :], sg, ALU.mult), u_done, gated, *ffree)
                    silu.release(si, prod)
                    banks.release(ub, prod)
                    hi, lo = hi_lo(HIDDEN, f, slice(None))
                    ready.append(split_pair(hi, lo, fl, prod))
                    full.release(fi, ready[-1])
                if c == NCHUNK - 1:
                    log_exp_table()
                out_product("ffn down", HIDDEN, NFC, lambda k, t: [ready[k]], last_sink if c == NCHUNK - 1 else first_sink,
                            NFC * c)

        def keep_first(kept):
            def sink(half, t, b, bank, token):
                kept[half, t] = evacuate(TOK[:, t, half * 512:half * 512 + 512], bank[:, :], token, *tok_done[t])
                banks.release(b, kept[half, t])
                return None
            return sink

        def attend(units, e_slots, p_slots, fill):

            def scores(u):
                u.banks = []
                for l, r in u.maps:
                    b, bank, free = banks.take()
                    pe.wait(*u.ready(), *free)
                    n = r.shape[1]
                    f = lambda e: e.matmul(bank[:, 0:n], l, r, start=True, stop=not u.mask)
                    if u.mask:
                        pe.more(f)
                        token = pe.run(lambda e, bank=bank: e.matmul(bank[:, u.w - P:u.w], IDB[:, :], MKB[:, :],
                                                                     start=False, stop=True), bf_ready)
                    else:
                        token = pe.run(f)
                    u.banks.append((b, bank, token))

            def soften(u):
                si, u.stat, sfree = stat.take()
                u.si, u.e = si, []
                for j, (b, bank, token) in enumerate(u.banks):
                    ei, e_, efree = e_slots.take()
                    nm, sm = u.stat[:, j:j + 1], u.stat[:, 2 + j:3 + j]
                    dst = e_[:, 0:u.w]
                    if u.bias is None:
                        mx = dve.run(lambda e, bank=bank, nm=nm: e.tensor_reduce(nm, bank[:, 0:u.w], AX, ALU.max, negate=True),
                                     token, *sfree)
                        ex = act.run(lambda e, bank=bank, nm=nm, sm=sm, dst=dst: e.activation(
                            dst, bank[:, 0:u.w], ACT.Exp, bias=nm, accum_out=sm), mx, *efree, *sfree)
                        banks.release(b, ex)
                    else:
                        mx = dve.run(lambda e, bank=bank, nm=nm, dst=dst: e.tensor_tensor_reduce(
                            dst, bank[:, 0:u.w], u.bias(), -1.0, u.floor, ALU.add, ALU.min, nm),
                            token, *sfree, *efree, *u.bias_ready())
                        if u.last_of_head is not None:
                            u.last_of_head(mx)
                        ex = act.run(lambda e, nm=nm, sm=sm, dst=dst: e.activation(
                            dst, dst, ACT.Exp, bias=nm, scale=-1.0, accum_out=sm), mx)
                        banks.release(b, mx)
                    u.e.append((ei, e_, ex))

            def mix(u):
                n = len(u.maps)
                rc = u.stat[:, 4:4 + n]
                u.rc = rc
                if u.coef is not None:
                    cf = u.stat[:, 6:7]
                    s1 = dve.run(lambda e: e.tensor_scalar(cf, u.stat[:, 2:3], 1e-30, None, ALU.max), u.e[0][2])
                    s2 = dve.run(lambda e: e.reciprocal(rc, cf), s1)
                    u.norm = dve.run(lambda e: e.tensor_tensor(cf, rc, u.coef, ALU.mult), s2, *u.coef_ready)
                    u.scalar = cf
                else:
                    u.norm = dve.run(lambda e: e.reciprocal(rc, u.stat[:, 2:2 + n]), *[x[2] for x in u.e])
                    u.scalar = rc
                u.p_ready = u.e[0][2]
                if n == 2:
                    (i0, e0, _), (i1, e1, _) = u.e
                    nl = u.stat[:, 6:7]
                    l = dve.run(lambda e: e.tensor_tensor(nl, u.stat[:, 5:6], u.neg_lambda, ALU.mult), u.norm)
                    s = act.run(lambda e: e.activation(e0[:, 0:u.w], e0[:, 0:u.w], ACT.Copy, scale=u.stat[:, 4:5]), u.norm)
                    u.p_ready = dve.run(lambda e: e.scalar_tensor_tensor(e0[:, 0:u.w], e1[:, 0:u.w], nl, e0[:, 0:u.w],
                                                                         ALU.mult, ALU.add), l, s)
                    e_slots.release(i1, u.p_ready)

            def turn(u):
                b, bank, free = banks.take()
                pe.wait(u.p_ready, *free)
                e0 = u.e[0][1]
                chunks = [(c, min(P, u.w - c)) for c in range(0, u.w, P)]
                for c, n in chunks:
                    f = lambda e, c=c, n=n: e.transpose(bank[0:n, c:c + P], e0[:, c:c + n], IDENT)
                    token = pe.run(f) if c + n == u.w else pe.more(f)
                e_slots.release(u.e[0][0], token)
                u.pi, u.pt, pfree = p_slots.take()
                n = chunks[0][1]
                w = len(chunks) * P
                u.pt_ready = evacuate(u.pt[0:n, 0:w], bank[0:n, 0:w], token, *pfree)
                banks.release(b, u.pt_ready)

            def values(u):
                b, bank, free = banks.take()
                pairs = []
                for j, c in enumerate(range(0, u.w, P)):
                    n = min(P, u.w - c)
                    pairs.append((u.pt[0:n, c:c + P], u.v(j)))
                token = matmuls(bank[:, 0:P], pairs, u.pt_ready, *u.v_ready, *free)
                p_slots.release(u.pi, token)
                tokens = u.finish(u, bank[:, u.at:u.at + u.nv], token)
                banks.release(b, *tokens)
                stat.release(u.si, *tokens)

            n = len(units)
            for i in range(n + 3):
                if i < n:
                    if units[i].start is not None:
                        units[i].start()
                    scores(units[i])
                    soften(units[i])
                for at, f in fill:
                    if at == i + 1:
                        f()
                if 1 <= i <= n:
                    mix(units[i - 1])
                if 2 <= i <= n + 1:
                    turn(units[i - 2])
                if i >= 3:
                    values(units[i - 3])

        class Unit:

            def __init__(self, w, nv, maps, ready, v, v_ready, finish, neg_lambda=None, bias=None, bias_ready=(),
                         floor=BIG, coef=None, coef_ready=(), mask=True, at=0, start=None, last_of_head=None):
                self.w, self.nv, self.maps, self.ready, self.v, self.v_ready = w, nv, maps, ready, v, v_ready
                self.finish, self.neg_lambda, self.bias, self.bias_ready = finish, neg_lambda, bias, bias_ready
                self.floor, self.coef, self.coef_ready, self.mask = floor, coef, coef_ready, mask
                self.at, self.start, self.last_of_head = at, start, last_of_head

        def log_sigmoid(dst, src, tmp, ready):
            m = dve.run(lambda e: e.tensor_scalar(dst, src, 0.0, None, ALU.min), ready)
            ab = dve.run(lambda e: e.scalar_tensor_tensor(tmp, src, -1.0, src, ALU.mult, ALU.max), ready)
            ex = act.run(lambda e: e.activation(tmp, tmp, ACT.Exp, scale=-1.0), ab)
            ln = act.run(lambda e: e.activation(tmp, tmp, ACT.Ln, bias=ONES[0:tmp.shape[0], 0:1]), ex, ones_ready)
            return dve.run(lambda e: e.tensor_tensor(dst, dst, tmp, ALU.subtract), ln, m)

        log_exp_table()
        puts = [row_norm(x_ready[t], t) for t in range(NT)]

        ang, turns_ = arena(8704, T), arena(9216, T)
        c2pi = [6.28125, 0.0019350051879882812, 3.019916050561733e-07]
        posf = dve.run(lambda e: e.tensor_copy(ang, POSI), positions)
        angle = dve.run(lambda e: e.tensor_scalar(ang, ang, CST[:, K_FREQ:K_FREQ + 1], None, ALU.mult), posf, consts)
        for table, quarter, arg in ((SIN, 0.0, arena(9728, T)), (COS, 0.25, arena(11264, T))):
            q = dve.run(lambda e, quarter=quarter: e.tensor_scalar(turns_, ang, 1.0 / (2 * math.pi), quarter, ALU.mult, ALU.add),
                        angle)
            q = dve.run(lambda e: e.tensor_scalar(turns_, turns_, 12582912.0, None, ALU.add), q)
            q = dve.run(lambda e: e.tensor_scalar(turns_, turns_, -12582912.0, None, ALU.add), q)
            src = ang
            for c in c2pi:
                q = dve.run(lambda e, c=c, src=src, arg=arg: e.scalar_tensor_tensor(arg, turns_, -c, src, ALU.mult, ALU.add), q)
                src = arg
            q = dve.run(lambda e, quarter=quarter: e.tensor_scalar(arg, arg, quarter * 2 * math.pi, 3.1415925, ALU.add, ALU.min), q)
            q = dve.run(lambda e: e.tensor_scalar(arg, arg, -3.1415925, None, ALU.max), q)
            rope_ready = act.run(lambda e, table=table, arg=arg: e.activation(table[:, :], arg, ACT.Sin), q)

        log_exp_table()
        for put in puts:
            put()
        b, bank, free = banks.take()
        turned = pe.run(lambda e, bank=bank: e.transpose(bank[:, 0:NVEC], ROWS[0:NVEC, :], CST[0:NVEC, 0:NVEC]), consts, vectors, (vec_in_act[0], vec_in_act[1]))
        vc_ready = evacuate(VC[:, :], bank[:, 0:NVEC], turned, engine=dve)
        banks.release(b, vc_ready)
        b, bank, free = banks.take()
        turned = pe.run(lambda e, bank=bank: e.transpose(bank[:, 0:64], PER[0:64, :], CST[0:64, 0:64]))
        pec_ready = evacuate(PEC[:, :], bank[:, 0:64], turned, engine=dve)
        banks.release(b, pec_ready)
        lam_init = [0.8 - 0.6 * math.exp(-0.3 * l) for l in range(LAYERS)]
        for l in range(LAYERS):
            c = VEC["diff_sub"] + l
            vc_ready = dve.run(lambda e, c=c, l=l: e.tensor_scalar(VC[:, c:c + 1], VC[:, c:c + 1], 1.0 - lam_init[l],
                                                                   None, ALU.mult), vc_ready)
        act.wait(vc_ready)
        norm = PreNorm(VEC["attn_pre"], [("forget", "pieces", C_F), ("qkv", C_QA)])
        for t in range(NT):
            norm.step(t)
        h_ready = norm.finish()
        pool.dma(BVR[:, 0:512], b_in[C_MV:C_MO].partition_broadcast(P), late_in)
        pool.dma(BVR[:, 512:640], b_in[C_NKV + 384:C_NKV + 512].partition_broadcast(P), late_in)
        pool.dma(BVR[:, 640:768], b_in[C_NKV + 640:C_NKV + 768].partition_broadcast(P), late_in)
        pool.dma(BVR[:, 768:776], b_in[C_IF:C_NQ].partition_broadcast(P), late_in)
        pool.dma(BVR[:, 776:800], b_in[C_NG:C_MERGE].partition_broadcast(P), late_in)
        BFG = NLAM[:, 8:12]
        pool.dma(BFG, a["b_fgate_2"][0].partition_broadcast(P), late_in)
        W2C = sb("w_cmp2_sb", [P, 3, HD])
        for slot, j in ((0, 0), (1, 0), (2, 1)):
            late_rows = pool.dma(W2C[:, slot, :], a["w_cmp2_2"][0, j], late_in)

        prod = dve.run(lambda e: e.tensor_tensor(LAM[:, 0:2, :, :], LAM[:, 0:2, :, :], LAM[:, 2:4, :, :], ALU.mult), row_vectors)
        dots = dve.run(lambda e: e.tensor_reduce(NLAM[:, 0:4], LAM[:, 0:2, :, :].rearrange("p a l d -> p (a l) d"),
                                                 AX, ALU.add), prod)
        exps = act.run(lambda e: e.activation(NLAM[:, 0:4], NLAM[:, 0:4], ACT.Exp), dots)
        diff = dve.run(lambda e: e.tensor_tensor(NLAM[:, 4:6], NLAM[:, 2:4], NLAM[:, 0:2], ALU.subtract), exps)
        for l in range(LAYERS):
            lam_ready = dve.run(lambda e, l=l: e.tensor_scalar(NLAM[:, 4 + l:5 + l], NLAM[:, 4 + l:5 + l], -lam_init[l],
                                                               None, ALU.add), diff)

        rev_io = [sem("bias_scratch_io"), 0]
        strip_in = [sem("bias_strips_arrival"), 0]
        b, bank, free = banks.take()
        hot = matmuls(bank[0:NH, :], [(RELB[:, :], HOT)], row_vectors, consts, *free)
        REVB = ARENA[0:NH, 13440:13440 + REV]
        rv = dve.run(lambda e: e.tensor_copy(REVB[:, 0:T], bank[0:NH, :]), hot)
        banks.release(b, rv)
        rv2 = dve.run(lambda e: e.memset(REVB[:, T:REV], NEG))
        rows_of = REVB[:, P - 1:P - 1 + T]
        shifted = bass.AP(rows_of.tensor, rows_of.offset, [list(rows_of.ap[0]), [-1, P], [1, T]])
        rev_written = pool.dma(strip_dram, shifted, rev_io, rv, rv2)

        decay_io = [sem("decay_scratch_io"), 0]
        x_tokens = list(x_ready)

        def bias_rows(src, written):
            state = [None, None]

            def start():
                i, buf, readers = bias_slots.take()
                state[0] = buf
                state[1] = [pool.dma(buf[:, :], src, bias_in[i], written, *readers)]
                state.append(i)
            return start, lambda: state[0], lambda: state[1], lambda token: bias_slots.release(state[2], token)

        for layer in range(LAYERS):
            QA, KA, QB, KB = (arena(2048 * i, 4, T) for i in range(4))
            V = arena(8192, NT, D)
            e_slots = Slots([arena(12288 + 512 * i, T) for i in range(6)])
            p_slots = Slots([arena(15360 + 512 * i, T) for i in range(3)])
            rope = Slots([DIAG[:, :, :].rearrange("p t n -> p (t n)"), RTMP[:, :]])
            FG, FGT = arena(12288, 2, T)[0:N_FOX], arena(13312, NT * N_FOX)
            quiet = [pe.last(), act.last(), dve.last(), pool.last()]
            act.wait(*quiet)
            dve.wait(*quiet)

            b, bank, token = feature_tile(("forget", "pieces", C_F), HT, h_ready)
            biased = dve.run(lambda e: e.tensor_scalar(FG[:, 0, :], bank[0:N_FOX, :], FBI[:, layer:layer + 1], None, ALU.add),
                             token, row_vectors)
            banks.release(b, biased)
            lf = log_sigmoid(NEGC[:, :], FG[:, 0, :], FG[:, 1, :], biased)
            v_ready = {}

            def value_sink(base):
                def sink(t, b, bank, token):
                    v_ready[t, base] = evacuate(V[:, t, base:base + 512], bank[:, :], token)
                    return [v_ready[t, base]]
                return sink
            qk_ready = {}

            def turned_tile(c, dst, m, scale):
                b, bank, token = feature_tile(("qkv", c + m * P), HT, h_ready)
                ri, tmp, rfree = rope.take()
                copied = evacuate(tmp, bank[:, :], token, *rfree, scale=scale, engine=act)
                banks.release(b, copied)
                straight = dve.run(lambda e: e.tensor_tensor(dst[:, m, :], tmp, COS[:, :], ALU.mult), copied, rope_ready)

                def finish():
                    b, bank, free = banks.take()
                    rot = matmuls(bank[:, :], [(CST[:, K_ROT:K_ROT + P], tmp)], copied, consts, *free)
                    crossed = dve.run(lambda e: e.tensor_tensor(tmp, bank[:, :], SIN[:, :], ALU.mult), rot, straight)
                    banks.release(b, crossed)
                    qk_ready[c, m] = dve.run(lambda e: e.tensor_tensor(dst[:, m, :], dst[:, m, :], tmp, ALU.add), crossed)
                    rope.release(ri, qk_ready[c, m])
                return finish

            def plain_tile(c, dst, m, scale):
                b, bank, token = feature_tile(("qkv", c + m * P), HT, h_ready)
                qk_ready[c, m] = evacuate(dst[:, m, :], bank[:, :], token, scale=scale, engine=act)
                banks.release(b, qk_ready[c, m])

            tile_of = {C_QA: (turned_tile, QA, SCALE), C_KA: (turned_tile, KA, None),
                       C_QB: (plain_tile, QB, SCALE), C_KB: (plain_tile, KB, None)}

            def tile(c, m):
                make, dst, scale = tile_of[c]
                return make(c, dst, m, scale)

            finish_q = tile(C_QA, 0)
            finish_k = tile(C_KA, 0)
            finish_q()
            finish_k()
            project_tokens("values", C_VA, 512, HT, ND, h_ready, value_sink(0))
            b, bank, free = banks.take()
            pe.wait(lf, *free)
            for t in range(NT):
                f = lambda e: e.transpose(bank[:, N_FOX * t:N_FOX * (t + 1)], NEGC[:, t * P:(t + 1) * P],
                                          CST[0:N_FOX, 0:N_FOX])
                token = pe.run(f) if t == NT - 1 else pe.more(f)
            fgt = dve.run(lambda e: e.tensor_copy(FGT, bank[:, 0:NT * N_FOX]), token)
            banks.release(b, fgt)
            project_tokens("values", C_VB, 512, HT, ND, h_ready, value_sink(512))
            b, bank, free = banks.take()
            pe.wait(fgt, *free)
            for s in range(NT):
                f = lambda e: e.matmul(bank[0:N_FOX, s * P:T], FGT[:, N_FOX * s:N_FOX * (s + 1)], TRI[:, 0:T - s * P],
                                       start=(s == 0), stop=(s == NT - 1))
                summed = pe.run(f) if s == NT - 1 else pe.more(f)
            nc_ready = dve.run(lambda e: e.tensor_scalar(NEGC[:, :], bank[0:N_FOX, :], -1.0, None, ALU.mult), summed)
            banks.release(b, nc_ready)
            decay_written = pool.dma(decay_dram[layer], NEGC[:, :], decay_io, nc_ready)
            all_v = list(v_ready.values())
            dve.wait(act.last())

            waiting = []

            def filler(c, m):
                def fill():
                    if waiting:
                        waiting.pop()()
                    finish = tile(c, m)
                    if finish is not None:
                        waiting.append(finish)
                return fill
            fill = []
            for at, c, m in FILL_1:
                fill.append((at, filler(c, m)))
                if c in (C_QA, C_KA):
                    fill.append((at + 1, lambda: waiting.pop()() if waiting else None))
            fill.sort(key=lambda x: x[0])

            SS = NST[:, 32:48]
            tok_free = [x for y in tok_done for x in y]
            squares = []

            def diff_finish(h, t):
                def finish(u, bank, token):
                    dst = TOK[:, t, h * P:(h + 1) * P]
                    copy = dve.run(lambda e: e.tensor_copy(dst, bank), token, *tok_free)
                    squares.append(act.run(lambda e: e.activation(JUNK[:, 0:P], dst, ACT.Square,
                                                                  accum_out=SS[:, 4 * t + h:4 * t + h + 1]), copy, act.last()))
                    return [copy]
                return finish

            fox_done = []

            def fox_finish(h, t):
                def finish(u, bank, token):
                    fox_done.append(dve.run(lambda e: e.tensor_scalar(TOK[:, t, 512 + h * HD:512 + (h + 1) * HD], bank,
                                                                      u.scalar, None, ALU.mult), token, u.norm, *tok_free))
                    return [fox_done[-1]]
                return finish

            if layer == 0:
                act.wait(rev_written)
                dve.wait(rev_written)
            units = []
            for h in range(N_DIFF):
                for t in range(NT):
                    w = (t + 1) * P
                    units.append(Unit(
                        w=w, nv=P, maps=[(QA[m * HD:(m + 1) * HD, h, t * P:w], KA[m * HD:(m + 1) * HD, h, 0:w]) for m in range(2)],
                        ready=lambda h=h: [qk_ready[C_QA, h], qk_ready[C_KA, h]], neg_lambda=NLAM[:, 4 + layer:5 + layer],
                        v=lambda j, h=h: V[:, j, h * P:(h + 1) * P], v_ready=all_v, finish=diff_finish(h, t)))
            dve.wait(lam_ready)
            for h in range(N_FOX):
                m, r = h // 2, slice(HD * (h % 2), HD * (h % 2) + HD)
                start, row, row_ready, row_done = bias_rows(decay_dram[layer, h].partition_broadcast(P), decay_written)
                for t in range(NT):
                    w = (t + 1) * P
                    units.append(Unit(
                        w=w, nv=HD, maps=[(QB[r, m, t * P:w], KB[r, m, 0:w])], ready=lambda m=m: [qk_ready[C_QB, m], qk_ready[C_KB, m]],
                        bias=lambda row=row, w=w: row()[:, 0:w], bias_ready=row_ready, start=start if t == 0 else None,
                        last_of_head=row_done if t == NT - 1 else None, at=HD * (h % 2),
                        v=lambda j, m=m: V[:, j, 512 + m * P:512 + (m + 1) * P], v_ready=all_v, finish=fox_finish(h, t)))
            attend(units, e_slots, p_slots, fill)

            r = rstd(SS, SS, P, *squares)
            heads = TOK[:, :, 0:512].rearrange("p t (h e) -> p t h e", h=N_DIFF)
            by = SS.rearrange("p (t h) -> p t h", t=NT).unsqueeze(3).to_broadcast([P, NT, N_DIFF, P])
            normed = dve.run(lambda e: e.tensor_tensor(heads, heads, by, ALU.mult), r)
            c = VEC["diff_sub"] + layer
            g_row = gain_row(a["attn_post_g"][layer])
            m_ready = turn_tokens(TOK, NT, ND, HT, [normed, fox_done[-1]],
                                  lambda k0: VC[:, c:c + 1].unsqueeze(2).to_broadcast([P, 4, P]) if k0 < 4 else None)
            norm = PreNorm(VEC["ffn_pre"] + ND * layer, [("ffn gate", 0), ("ffn up", 0)])
            out_product("out", HT, ND, lambda k, t: [m_ready[2 * t + k // 4]], post_norm(g_row, x_tokens, norm))
            h_ready = norm.finish()
            g_row = gain_row(a["ffn_post_g"][layer])
            kept = {}
            if layer < LAYERS - 1:
                norm = PreNorm(VEC["attn_pre"] + ND * (layer + 1), [("forget", "pieces", C_F), ("qkv", C_QA)])
            else:
                norm = PreNorm(VEC["mix_pre"], [("gates", "pieces", C_IF), ("qk", C_MQ)])
            feed_forward(h_ready, keep_first(kept), post_norm(g_row, x_tokens, norm, kept))
            h_ready = norm.finish()

        quiet = [pe.last(), act.last(), dve.last(), pool.last()]
        act.wait(*quiet)
        dve.wait(*quiet)

        pe.wait(late_rows)
        dve.wait(late_rows)
        QK = arena(0, 8, T)
        VA = arena(4096, NT, MH, P + 1)
        SO = arena(6160, MH, T)
        KTOK = arena(8208, NT, MH, P)
        RM = arena(10256, NT, T)
        TOK_WORDS = TOK[:, :, :].rearrange("p a b -> p (a b)")
        HH = TOK_WORDS[:, 0:NT * MH * (P + 1)].rearrange(
            "p (c h e) -> p c h e", c=NT, h=MH)
        DG = TOK_WORDS[:, 2048:4096].rearrange("p (c h e) -> p c h e", c=NT, h=MH)
        conv_in = Slots([arena(12304 + 516 * i, 516) for i in range(2)])
        conv_acc = Slots([arena(13336 + 512 * i, T) for i in range(2)])
        VW = Slots([arena(12304 + 129 * i, P + 1) for i in range(2)])
        CST8 = arena(12562, MH, P + 1)
        PM = Slots([arena(13078 + 128 * i, P) for i in range(3)])
        PTM = Slots([arena(13462 + 128 * i, P) for i in range(3)])
        O1 = Slots([arena(13846 + 129 * i, P + 1) for i in range(2)])

        GT32 = SM[:, 0:128].rearrange("p (t c) -> p t c", t=NT)
        IFG, NGT = GT32[:, :, 0:8], GT32[:, :, 8:32]
        b, bank, token = feature_tile(("gates", "pieces", C_IF), HT, h_ready)
        copied = dve.run(lambda e: e.tensor_copy(JUNK[0:32, :], bank[0:32, :]), token, act.last())
        banks.release(b, copied)

        qk_ready = [None] * 8

        def conv_sink(m, bank, token):
            ci, cin, cfree = conv_in.take()
            ai, acc, afree = conv_acc.take()
            pad = dve.run(lambda e: e.memset(cin[:, 0:CONV - 1], 0.0), *cfree)
            copied = act.run(lambda e: e.activation(cin[:, CONV - 1:CONV - 1 + T], bank[:, :], ACT.Identity,
                                                    bias=VC[:, VEC["b_qk"] + m:VEC["b_qk"] + m + 1]), token, *cfree)
            col = lambda j: VC[:, VEC["conv"] + 8 * j + m:VEC["conv"] + 8 * j + m + 1]
            s = dve.run(lambda e: e.tensor_scalar(acc, cin[:, 0:T], col(0), None, ALU.mult), copied, pad, *afree)
            for j in range(1, CONV):
                s = dve.run(lambda e: e.scalar_tensor_tensor(acc, cin[:, j:j + T], col(j), acc, ALU.mult, ALU.add), s)
            conv_in.release(ci, s)
            done = act.run(lambda e: e.activation(QK[:, m, :], acc, ACT.Silu), s)
            if m >= 4:
                done = dve.run(lambda e: e.tensor_scalar(QK[:, m, :], QK[:, m, :], P ** -0.5, None, ALU.mult), done)
            conv_acc.release(ai, done)
            qk_ready[m] = done
            return [copied]
        project_features("qk", C_MQ, 1024, h_ready, conv_sink)

        b, bank, free = banks.take()
        pe.wait(copied, *free)
        for t in range(NT):
            f = lambda e: e.transpose(bank[:, 32 * t:32 * t + 32], JUNK[0:32, t * P:(t + 1) * P], CST[0:32, 0:32])
            token = pe.run(f) if t == NT - 1 else pe.more(f)
        gates_tok = dve.run(lambda e: e.tensor_tensor(GT32, bank[:, 0:128].rearrange("p (t c) -> p t c", t=NT),
                                                      BVR[:, 768:800].unsqueeze(1).to_broadcast([P, NT, 32]), ALU.add), token)
        banks.release(b, gates_tok)
        LF, LS = SM[:, 128:144], SM[:, 144:160]
        fb = dve.run(lambda e: e.tensor_tensor(LF.rearrange("p (c h) -> p c h", c=NT), IFG[:, :, 4:8],
                                               BFG.unsqueeze(1).to_broadcast([P, NT, MH]), ALU.add), gates_tok)
        log_exp_table()
        lf_ready = log_sigmoid(LS, LF, SM[:, 160:176], fb)

        va_ones = dve.run(lambda e: e.memset(VA[:, :, :, P:P + 1], 1.0))
        va_ready = [[va_ones] for _ in range(NT)]

        def va_sink(t, b, bank, token):
            done = dve.run(lambda e: e.tensor_tensor(VA[:, t, :, 0:P], bank[:, :].rearrange("p (h e) -> p h e", h=MH),
                                                     BVR[:, 0:512].rearrange("p (h e) -> p h e", h=MH), ALU.add), token)
            va_ready[t].append(done)
            return [done]
        project_tokens("values", C_MV, 512, HT, ND, h_ready, va_sink)

        b, bank, free = banks.take()
        pe.more(lambda e, bank=bank: e.matmul(bank[:, 0:16], TRI[:, 0:P], LS, start=True, stop=True), lf_ready, *free)
        sums = pe.run(lambda e, bank=bank: e.matmul(bank[:, 16:32], ONES[:, :], LS, start=True, stop=True), ones_ready)
        BCBL = SM[:, 176:208]
        bc = dve.run(lambda e, bank=bank: e.tensor_copy(BCBL, bank[:, 0:32]), sums)
        banks.release(b, bc)
        BC, BL = BCBL[:, 0:16], BCBL[:, 16:32]
        R = SM[:, 208:224]
        r_ready = dve.run(lambda e: e.tensor_tensor(R.rearrange("p (c h) -> p c h", c=NT), IFG[:, :, 0:4],
                                                    BC.rearrange("p (c h) -> p c h", c=NT), ALU.subtract), bc)
        MR, RX = SM[:, 224:240], SM[:, 240:256]
        rm_ready, r_diags = [], []
        for c in range(NT):
            for h in range(MH):
                d = dve.run(lambda e, c=c, h=h: e.tensor_scalar(DG[:, c, h, :], IDENT, R[:, 4 * c + h:4 * c + h + 1],
                                                                None, ALU.mult), r_ready)
            r_diags.append(d)

        def spread_chunk(c):
            b, bank, free = banks.take()
            spread = matmuls(bank[:, :], [(ONES[:, :], DG[:, c, :, :].rearrange("p h e -> p (h e)"))], r_diags[c], *free)
            b3 = bank[:, :].rearrange("p (h e) -> p h e", h=MH)
            r3 = RM[:, c, :].rearrange("p (h e) -> p h e", h=MH)
            whole = dve.run(lambda e, c=c, b3=b3: e.tensor_reduce(RX[:, 4 * c:4 * c + 4], b3, AX, ALU.max), spread)
            masked = dve.run(lambda e, b3=b3, r3=r3: e.tensor_tensor(r3, b3, MASK.unsqueeze(1).to_broadcast([P, MH, P]), ALU.add), spread)
            banks.release(b, masked)
            rm_ready.append(dve.run(lambda e, c=c, r3=r3: e.tensor_reduce(MR[:, 4 * c:4 * c + 4], r3, AX, ALU.max), masked))

        so_ready = [None] * MH

        def so_sink(m, bank, token):
            so_ready[m] = act.run(lambda e: e.activation(SO[:, m, :], bank[:, :], ACT.Sigmoid,
                                                         bias=VC[:, VEC["b_mo"] + m:VEC["b_mo"] + m + 1]), token)
            spread_chunk(m)
            return [so_ready[m]]
        project_features("output gate", C_MO, 512, h_ready, so_sink)
        ng_ready = [act.run(lambda e: e.activation(NGT, NGT, ACT.Sigmoid), gates_tok)]
        log_exp_table()

        MP, MX = SM[:, 256:276], SM[:, 276:292]
        step = dve.run(lambda e: e.memset(MP[:, 0:4], 0.0))
        for c in range(NT):
            s = slice(4 * c, 4 * c + 4)
            mx = dve.run(lambda e, s=s: e.tensor_tensor(MX[:, s], MP[:, s], RX[:, s], ALU.max), step, rm_ready[c])
            step = dve.run(lambda e, s=s, c=c: e.tensor_tensor(MP[:, 4 * c + 4:4 * c + 8], BL[:, s], MX[:, s], ALU.add), mx)
        NM2, SI, EM, WK, DC = (SM[:, 292 + 16 * i:308 + 16 * i] for i in range(5))
        q = dve.run(lambda e: e.tensor_tensor(NM2, MR, MP[:, 0:16], ALU.max), step)
        q = dve.run(lambda e: e.tensor_scalar(NM2, NM2, -1.0, None, ALU.mult), q)
        q1 = dve.run(lambda e: e.tensor_tensor(SI, MP[:, 0:16], NM2, ALU.add), q)
        q2 = dve.run(lambda e: e.tensor_tensor(EM, NM2, BC, ALU.subtract), q)
        q3 = dve.run(lambda e: e.tensor_tensor(WK, R, MX, ALU.subtract), step)
        q4 = dve.run(lambda e: e.tensor_tensor(DC, MP[:, 0:16], MX, ALU.subtract), step)
        gates_ready = act.run(lambda e: e.activation(SM[:, 308:372], SM[:, 308:372], ACT.Exp), q1, q2, q3, q4)


        ktok_ready = []
        for c in range(NT):
            b, bank, free = banks.take()
            pe.wait(*free, *qk_ready[4:8])
            for h in range(MH):
                f = lambda e, c=c, h=h, bank=bank: e.transpose(bank[:, h * P:(h + 1) * P], QK[:, 4 + h, c * P:(c + 1) * P], IDENT)
                turned = pe.run(f) if h == MH - 1 else pe.more(f)
            ktok_ready.append(evacuate(KTOK[:, c, :, :].rearrange("p h e -> p (h e)"), bank[:, :], turned))
            banks.release(b, ktok_ready[-1])

        dve.wait(act.last())
        act.wait(dve.last())

        KC, VCM, KS = (TOK_WORDS[:, at:at + T] for at in (2064, 2576, 3088))
        kv_ready = {}

        def kv_tile(dst, col):
            b, bank, token = feature_tile(("nsa", C_NKV + P * col), HT, h_ready)
            c = VEC["b_kv"] + col
            kv_ready[col] = evacuate(dst, bank[:, :], token, bias=VC[:, c:c + 1])
            banks.release(b, kv_ready[col])

        DEN, SSM, FAC = SM[:, 372:388], SM[:, 388:404], SM[:, 404:420]
        c_ready = [None] * MH
        state, normed = {}, []

        def weights(c, h):
            col = 4 * c + h
            q_ = QK[:, h, c * P:(c + 1) * P]
            u = state[c, h] = {}
            b, bank, free = banks.take()
            s_tok = matmuls(bank[:, 0:P], [(q_, QK[:, 4 + h, c * P:(c + 1) * P])], *qk_ready, *free)
            pi, pm, pfree = PM.take()
            ex = act.run(lambda e: e.activation(pm, RM[:, c, h * P:(h + 1) * P], ACT.Exp, bias=NM2[:, col:col + 1]),
                         gates_ready, rm_ready[c], *pfree)
            if c < NT - 1:
                wi, vw, wfree = VW.take()
                vwr = dve.run(lambda e: e.tensor_scalar(vw, VA[:, c, h, :], WK[:, col:col + 1], None, ALU.mult),
                              gates_ready, *va_ready[c], *wfree)
            pr = dve.run(lambda e: e.tensor_tensor(pm, bank[:, 0:P], pm, ALU.mult), ex, s_tok)
            banks.release(b, pr)
            u["pm"] = (pi, pm, pr)
            yield
            if c > 0:
                b, bank2, free = banks.take()
                u["o2"] = (b, bank2, matmuls(bank2[:, 0:P + 1], [(q_, CST8[:, h, :])], c_ready[h], *free))
            if c < NT - 1:
                b, bank3, free = banks.take()
                u["up"] = (b, bank3, matmuls(bank3[:, 0:P + 1], [(KTOK[:, c, h, :], vw)], vwr, ktok_ready[c], *free))
                VW.release(wi, u["up"][2])
            yield

        def turn_weights(c, h):
            col, u = 4 * c + h, state[c, h]
            pi, pm, pr = u["pm"]
            b, bank, free = banks.take()
            tt = pe.run(lambda e: e.transpose(bank[:, 0:P], pm, IDENT), pr, *free)
            PM.release(pi, tt)
            ti, pt, tfree = PTM.take()
            pt_ready = evacuate(pt, bank[:, 0:P], tt, *tfree, engine=act)
            banks.release(b, pt_ready)
            u["pt"] = (ti, pt, pt_ready)
            if c > 0:
                b, bank2, o2 = u["o2"]
                oi, o, ofree = O1.take()
                cp = evacuate(o, bank2[:, 0:P + 1], o2, gates_ready, *ofree, scale=SI[:, col:col + 1], engine=act)
                banks.release(b, cp)
                u["o"] = (oi, o, cp)
            if c < NT - 1:
                b, bank3, up = u["up"]
                if c == 0:
                    c_ready[h] = dve.run(lambda e: e.tensor_copy(CST8[:, h, :], bank3[:, 0:P + 1]), up)
                else:
                    c_ready[h] = dve.run(lambda e: e.scalar_tensor_tensor(
                        CST8[:, h, :], CST8[:, h, :], DC[:, col:col + 1], bank3[:, 0:P + 1], ALU.mult, ALU.add), up, o2)
                banks.release(b, c_ready[h])

        def weigh_values(c, h):
            u = state[c, h]
            ti, pt, pt_ready = u["pt"]
            b, bank, free = banks.take()
            o1 = matmuls(bank[:, 0:P + 1], [(pt, VA[:, c, h, :])], pt_ready, *va_ready[c], *free)
            PTM.release(ti, o1)
            if c == 0:
                u["done"] = dve.run(lambda e: e.tensor_copy(HH[:, c, h, :], bank[:, 0:P + 1]), o1)
            else:
                oi, o, cp = u["o"]
                u["done"] = dve.run(lambda e: e.tensor_tensor(HH[:, c, h, :], bank[:, 0:P + 1], o, ALU.add), o1, cp)
                O1.release(oi, u["done"])
            banks.release(b, u["done"])

        def normalise(c):
            s = slice(4 * c, 4 * c + 4)
            q = dve.run(lambda e: e.scalar_tensor_tensor(DEN[:, s], HH[:, c, :, P], -1.0, HH[:, c, :, P], ALU.mult, ALU.max),
                        *[state[c, h]["done"] for h in range(MH)])
            q = dve.run(lambda e: e.tensor_tensor(DEN[:, s], DEN[:, s], EM[:, s], ALU.max), q)
            den = dve.run(lambda e: e.reciprocal(DEN[:, s], DEN[:, s]), q)
            for h in range(MH):
                col = 4 * c + h
                ssq = act.run(lambda e: e.activation(JUNK[:, 0:P], HH[:, c, h, 0:P], ACT.Square, scale=DEN[:, col:col + 1],
                                                     accum_out=SSM[:, col:col + 1]), den, act.last())
            r = rstd(FAC[:, s], SSM[:, s], P, ssq)

            def finish():
                f = dve.run(lambda e: e.tensor_tensor(FAC[:, s], FAC[:, s], DEN[:, s], ALU.mult), r)
                by = FAC[:, s].unsqueeze(2).to_broadcast([P, MH, P])
                normed.append(dve.run(lambda e: e.tensor_tensor(HH[:, c, :, 0:P], HH[:, c, :, 0:P], by, ALU.mult), f))
            return finish

        order = [(c, h) for c in range(NT) for h in range(MH)]
        between = {3: lambda: kv_tile(KC, 0), 7: lambda: kv_tile(VCM, 1), 11: lambda: kv_tile(KS, 2)}
        finish = None
        for i in range(len(order) + 2):
            rest = None
            if i < len(order):
                rest = weights(*order[i])
                next(rest)
            if 1 <= i <= len(order):
                turn_weights(*order[i - 1])
            if i >= 2:
                weigh_values(*order[i - 2])
            if rest is not None:
                next(rest)
            if finish is not None:
                finish()
                finish = None
            if i >= 2 and order[i - 2][1] == MH - 1:
                finish = normalise(order[i - 2][0])
            if i in between:
                between[i]()
        NQ = arena(0, 4, T)
        nq_ready = [None] * 4

        def nq_sink(m, bank, token):
            c = VEC["b_nq"] + m
            add = evacuate(NQ[:, m, :], bank[:, :], token, bias=VC[:, c:c + 1], engine=dve)
            nq_ready[m] = dve.run(lambda e: e.tensor_scalar(NQ[:, m, :], NQ[:, m, :], SCALE, None, ALU.mult), add)
            return [add]

        finish()
        for m in range(4):
            b, bank, token = feature_tile(("nsa q", "pieces", C_NQ + HD * m), HT, h_ready)
            banks.release(b, *nq_sink(m, bank, token))

        gated = Slots([arena(4096 + 512 * i, T) for i in range(2)])
        ym_ready = []
        for h in range(MH):
            b, bank, free = banks.take()
            pe.wait(*normed, *free)
            for c in range(NT):
                f = lambda e, c=c, h=h, bank=bank: e.transpose(bank[:, c * P:(c + 1) * P], HH[:, c, h, 0:P], IDENT)
                turned = pe.run(f) if c == NT - 1 else pe.more(f)
            g = VC[:, VEC["g_head"] + h:VEC["g_head"] + h + 1]
            gi, gm, gfree = gated.take()
            prod = dve.run(lambda e: e.scalar_tensor_tensor(gm, bank[:, :], g, SO[:, h, :], ALU.mult, ALU.mult),
                           turned, so_ready[h], *gfree)
            banks.release(b, prod)
            ym_ready.append(split_pair(YM[:, 0, h, :], YM[:, 1, h, :], gm, prod))
            gated.release(gi, ym_ready[-1])

        KW = arena(3584, T)
        VSW = arena(4096, NT, 256)
        XC = [arena(8192 + 2048 * j, CMP_BLOCK, 64) for j in range(2)]
        HID = arena(7168, 2, P)
        HIDT = arena(7424, 2, 64)
        KCC = arena(7552, P)
        VCC = arena(7680, P)
        e_slots = Slots([arena(8192 + 512 * i, T) for i in range(6)])
        p_slots = Slots([arena(11264 + 512 * i, T) for i in range(3)])
        YN = TOK[:, 0:2, :].rearrange("p a (b c) -> p (a b) c", b=2)

        kv_tile(KW, 4)
        quiet = [pe.last(), act.last(), dve.last(), pool.last()]
        dve.wait(*quiet)
        blocks_ready = []
        for j, src in enumerate((KC, VCM)):
            zero = dve.run(lambda e: e.memset(XC[j][:, :, :], 0.0))
            for g in range(NG_):
                r = slice(HD * g, HD * (g + 1))
                s = src[r]
                windows = bass.AP(s.tensor, s.offset, [list(s.ap[0]), [1, CMP_BLOCK], [CMP_STRIDE, NCMP]])
                pos = PEC[r, CMP_BLOCK * j:CMP_BLOCK * (j + 1)].unsqueeze(2).to_broadcast([HD, CMP_BLOCK, NCMP])
                blocks_ready.append(dve.run(lambda e: e.tensor_tensor(XC[j][r, :, 32 * g:32 * g + NCMP], windows, pos, ALU.add),
                                            kv_ready[j], zero))

        vs_ready = []

        def vs_sink(t, b, bank, token):
            vs_ready.append(dve.run(lambda e: e.tensor_tensor(VSW[:, t, :], bank[:, 0:256], BVR[:, 512:768], ALU.add), token))
            return [vs_ready[-1]]
        project_tokens("nsa values", C_NKV + 384, 256, HT, ND, h_ready, vs_sink)

        cmp_ready = []
        hid_ready = []
        for j in range(2):
            b, bank, free = banks.take()
            pe.wait(*blocks_ready, *free)
            for l in range(0, CMP_BLOCK, 8):
                slab("compress", j, l)
                i, r, arrived = arrivals[used[0] - 1][0:3]
                w1 = RAW[r][:, :].rearrange("p (l h) -> p l h", l=8)
                pe.wait(arrived)
                for ll in range(8):
                    f = lambda e: e.matmul(bank[0:64, 0:P], XC[j][:, l + ll, :], w1[:, ll, :],
                                           start=(l + ll == 0), stop=(l + ll == CMP_BLOCK - 1))
                    token = pe.run(f) if ll == 7 else pe.more(f)
                raw_slots.release(i, token)
            silu = act.run(lambda e: e.activation(HID[0:64, j, :], bank[0:64, 0:P], ACT.Silu), token)
            banks.release(b, silu)
            b, bank, free = banks.take()
            token = pe.run(lambda e: e.transpose(bank[:, 0:64], HID[0:64, j, :], CST[0:64, 0:64]), silu, *free)
            hid_ready.append(dve.run(lambda e: e.tensor_copy(HIDT[:, j, :], bank[:, 0:64]), token))
            banks.release(b, hid_ready[-1])
        log_exp_table()
        cmp_ready.append(dve.run(lambda e: e.memset(KCC[:, :], 0.0)))
        b, bank, free = banks.take()
        w2 = W2C[:, 0:2, :].rearrange("p a d -> p (a d)")
        token = pe.run(lambda e: e.matmul(bank[:, 0:64], w2, HIDT[:, 0, :], start=True, stop=True), hid_ready[0], *free)
        for g in range(NG_):
            r = slice(HD * g, HD * (g + 1))
            cmp_ready.append(dve.run(lambda e: e.tensor_copy(KCC[r, 0:NCMP], bank[r, 32 * g:32 * g + NCMP]), token, *cmp_ready))
        banks.release(b, cmp_ready[-1])
        for g in range(NG_):
            b, bank, free = banks.take()
            token = pe.run(lambda e: e.matmul(bank[0:NCMP, 0:HD], HIDT[:, 1, 32 * g:32 * g + NCMP], W2C[:, 2, :],
                                              start=True, stop=True), hid_ready[1], *free)
            cmp_ready.append(dve.run(lambda e: e.tensor_copy(VCC[0:NCMP, HD * g:HD * (g + 1)], bank[0:NCMP, 0:HD]), token))
            banks.release(b, cmp_ready[-1])
        dve.wait(pe.last())
        act.wait(pe.last())

        yn_ready = {}
        units = []

        def branch_finish(h, t, first):
            def finish(u, bank, token):
                dst = YN[:, t, h * HD:(h + 1) * HD]
                if first:
                    f = lambda e: e.tensor_scalar(dst, bank, u.scalar, None, ALU.mult)
                else:
                    f = lambda e: e.scalar_tensor_tensor(dst, bank, u.scalar, dst, ALU.mult, ALU.add)
                yn_ready[h, t] = dve.run(f, token, u.norm, yn_ready.get((h, t)))
                return [yn_ready[h, t]]
            return finish

        for h in range(NH):
            g, rr = h // NR, h % NR
            r = slice(HD * g, HD * (g + 1))
            start, row, row_ready, row_done = bias_rows(strip_dram[h], rev_written)
            for t in range(NT):
                qt = NQ[r, rr, t * P:(t + 1) * P]
                w = (t + 1) * P
                nw = (w - CMP_BLOCK) // CMP_STRIDE + 1
                first = T - P + CMP_BLOCK - 1 - P * t
                windows = lambda row=row, first=first, nw=nw: row()[:, first:first + CMP_STRIDE * (nw - 1) + 1:CMP_STRIDE]
                tokens_ = lambda row=row, t=t: row()[:, T - P - P * t:T]
                gate = lambda br: NGT[:, t, 3 * h + br:3 * h + br + 1]
                common = dict(coef_ready=ng_ready, bias_ready=row_ready, mask=False, nv=HD, at=HD * g)
                units.append(Unit(w=nw, maps=[(qt, KCC[r, :])], ready=lambda: [*nq_ready, *cmp_ready], bias=windows, floor=1e29,
                                  coef=gate(0), v=lambda j, nw=nw: VCC[0:nw, :], v_ready=cmp_ready,
                                  start=start if t == 0 else None, finish=branch_finish(h, t, True), **common))
                for br, keys, base in ((1, KS, 0), (2, KW, P)):
                    units.append(Unit(w=w, maps=[(qt, keys[r, 0:w])], ready=lambda br=br: [*nq_ready, kv_ready[2 * br]],
                                      bias=tokens_, coef=gate(br), v=lambda j, base=base: VSW[:, j, base:base + P],
                                      last_of_head=row_done if (t, br) == (NT - 1, 2) else None,
                                      v_ready=vs_ready, finish=branch_finish(h, t, False), **common))
        attend(units, e_slots, p_slots, [])
        dve.wait(pe.last())
        act.wait(pe.last())
        yn_t = turn_tokens(YN, NT, 4, YNT, [dve.last()])

        gate_buf = Slots([TOK[:, 2 + i // 2, (i % 2) * 512:(i % 2) * 512 + 512] for i in range(4)])
        mix_ready = []
        for d in range(ND):
            parts = []
            for n, (y, y_tok) in enumerate(((YM, ym_ready), (YNT, yn_t))):
                b, bank, tok = feature_tile(("merge", C_MERGE + D * n + d * P), HT, h_ready)
                si, sg, sfree = gate_buf.take()
                c = VEC["b_merge"] + ND * n + d
                sig = act.run(lambda e: e.activation(sg, bank[:, :], ACT.Sigmoid, bias=VC[:, c:c + 1]), tok, *sfree)
                banks.release(b, sig)
                b, bank, tok = feature_tile((f"branch{n}", d * P), y, y_tok, 4)
                pr = dve.run(lambda e: e.tensor_tensor(sg, bank[:, :], sg, ALU.mult), tok, sig)
                banks.release(b, pr)
                parts.append((si, sg, pr))
            (i0, g0, p0), (i1, g1, p1) = parts
            both = dve.run(lambda e: e.tensor_tensor(g0, g0, g1, ALU.add), p0, p1)
            gate_buf.release(i1, both)
            mix_ready.append(split_pair(MIX[:, 0, d, :], MIX[:, 1, d, :], g0, both))
            gate_buf.release(i0, mix_ready[-1])
        log_exp_table()

        norm = PreNorm(VEC["ffn2_pre"], [("ffn gate", 0), ("ffn up", 0)])

        def update_rows(t):
            if t < NT - 1:
                diag_of(t)
            else:
                norm.last_tile()
        out_product("out", MIX, ND, lambda k, t: [mix_ready[k]], residual(x_tokens, update_rows))
        h_ready = norm.finish()
        g_row = gain_row(a["g_final_2"])
        out_done = [sem("out_stored"), 0]
        stored = []

        def finish_tokens(t):
            sq = act.run(lambda e: e.activation(TOK[:, t, :], X[:, t, :], ACT.Square, accum_out=NST[:, t:t + 1]), x_tokens[t])
            r = rstd(NST[:, 4 + t:5 + t], NST[:, t:t + 1], D, sq)
            f = dve.run(lambda e: e.scalar_tensor_tensor(TOK[:, t, :], X[:, t, :], NST[:, 4 + t:5 + t], GROW[:, :],
                                                         ALU.mult, ALU.mult), r, g_row)
            stored.append(sync.dma(out[0, t * P:(t + 1) * P, :], TOK[:, t, :], out_done, f))

        feed_forward(h_ready, residual(x_tokens), residual(x_tokens, finish_tokens))

        sync.wait(stored[-1], decay_written, rev_written)


_INS = ['x', 'positions', 'attn_pre_g', 'w_in', 'forget_bias', 'lam_q1', 'lam_k1', 'lam_q2', 'lam_k2', 'diff_sub_g',
        'w_out', 'attn_post_g', 'ffn_pre_g', 'w_gate', 'w_up', 'w_down', 'ffn_post_g', 'g_norm_mix_2', 'w_in_2',
        'b_in_2', 'b_fgate_2', 'conv_qk_2', 'g_mlstm_head_2', 'pe_cmp_2', 'w_cmp1_2', 'w_cmp2_2', 'rel_bias_2',
        'w_branch_2', 'w_out_2', 'g_norm_ffn_2', 'w_gate_2', 'w_up_2', 'w_down_2', 'g_final_2']


def kernel(**inputs):
    import numpy as _np
    import concourse.bacc as _bacc
    from concourse import mybir as _mybir
    from concourse.bass_utils import run_bass_kernel_spmd as _run

    nc = _bacc.Bacc("TRN2", target_bir_lowering=False, num_devices=1)
    arrays, args = {}, {}
    given = {name: inputs[name] for name in _INS}
    given["shape_constants"] = shape_constants()
    for name, value in given.items():
        v = _np.ascontiguousarray(value)
        if name.startswith("g_final"):
            v = v.reshape(-1)
        arrays[f"in_{name}_dram"] = v
        args[name] = nc.dram_tensor(f"in_{name}_dram", v.shape, _mybir.dt.from_np(v.dtype), kind="ExternalInput").ap()
    result = nc.dram_tensor("out_0_dram", (1, T, D), F32, kind="ExternalOutput").ap()
    program(nc, args, result)
    r = _run(nc, [arrays], core_ids=[0])
    return r.results[0]["out_0_dram"]
```
